# Optimizing a Trainium2 kernel written in Bass

```python
import functools
import jax, jax.numpy as jnp
from jax import lax
import numpy as np

D_MODEL = 1024
BATCH = 1
SEQ = 512
DEPTH = 1
DEC_BATCH = 8
DEC_SEQ = 1
PAST_LEN = 4096
PAGE_SIZE = 128

F32 = jnp.float32
NORM_EPS = 1e-6
A_HEADS = 6
A_HEAD_DIM = 64
A_WIDTH = A_HEADS * A_HEAD_DIM
DILATED_GROUPS = ((128, 1), (512, 4), (2048, 16))
DIL_KEYS = 128
SWA_SPAN = 2048
B_HEADS = 4
B_HEAD_DIM = 64
B_WIDTH = B_HEADS * B_HEAD_DIM
SB_BLOCK = 128
SB_BIAS_INIT = -6.0
C_HEADS = 4
C_KEY_DIM = 64
C_VAL_DIM = 64
C_KEY_WIDTH = C_HEADS * C_KEY_DIM
C_VAL_WIDTH = C_HEADS * C_VAL_DIM
HGRN_CHUNK = 64
D_GROUPS = 4
D_GROUP_DIM = 64
D_WIDTH = D_GROUPS * D_GROUP_DIM
SGU_CHUNK = 128
N_BRANCH = 4
PROJ_SPLITS = (A_WIDTH, A_WIDTH, A_WIDTH, B_WIDTH, B_WIDTH, B_WIDTH, C_KEY_WIDTH, C_KEY_WIDTH, C_VAL_WIDTH, C_VAL_WIDTH, D_WIDTH, D_WIDTH)
IN_WIDTH = sum(PROJ_SPLITS)
N_EXPERTS = 64
TOP_K = 8
N_EXPERT_GROUPS = 8
TOPK_GROUPS = 4
EXPERT_DIM = 256
SHARED_DIM = 256
ROUTE_SCALE = 2.5
MOE_BLOCK = 128

kernel_name = 'hybrid_gated_dilswa_stickbreak_hgrn2_sgu_moe_step'

def rms_norm(x, g):
    xf = x.astype(F32)
    y = xf * lax.rsqrt(jnp.mean(xf * xf, axis=-1, keepdims=True) + NORM_EPS)
    return (y * g.astype(F32)).astype(x.dtype)

def dilated_attention_prompt(q, k, v):
    bsz, t, h, dh = q.shape
    blk = DIL_KEYS
    qi = jnp.arange(blk)[:, None]
    kj = jnp.arange(2 * blk)[None, :]
    dist = qi + blk - kj
    maxs, dens, nums = [], [], []
    for _, dil in DILATED_GROUPS:
        span = dil * blk
        tp = -(-t // span) * span
        nb = tp // span

        def to_blocks(a):
            a = jnp.pad(a, ((0, 0), (0, tp - t), (0, 0), (0, 0)))
            return a.reshape(bsz, nb, blk, dil, h, dh)

        def with_prev(a):
            prev = jnp.pad(a[:, :-1], ((0, 0), (1, 0), (0, 0), (0, 0), (0, 0), (0, 0)))
            return jnp.concatenate([prev, a], axis=2)

        qb = to_blocks(q)
        kb = with_prev(to_blocks(k))
        vb = with_prev(to_blocks(v))
        s = jnp.einsum('bnirhd,bnjrhd->bnrhij', qb, kb).astype(F32) * dh ** -0.5
        first = jnp.arange(nb)[:, None, None] * blk - blk + kj[None]
        valid = (dist >= 0)[None] & (dist <= blk)[None] & (first >= 0)
        s = jnp.where(valid[None, :, None, None], s, -jnp.inf)
        m = jnp.max(s, axis=-1)
        p = jnp.exp(s - m[..., None])
        den = jnp.sum(p, axis=-1)
        num = jnp.einsum('bnrhij,bnjrhd->bnrhid', p, vb.astype(F32))
        back = lambda a: jnp.moveaxis(a, 4, 2).reshape((bsz, tp, h) + a.shape[5:])[:, :t]
        maxs.append(back(m))
        dens.append(back(den))
        nums.append(back(num))
    mx = functools.reduce(jnp.maximum, maxs)
    wts = [jnp.exp(m - mx) for m in maxs]
    num = sum(n * w[..., None] for n, w in zip(nums, wts))
    den = sum(d * w for d, w in zip(dens, wts))
    return num / den[..., None]

def dilated_attention_sample(q, k_all, v_all):
    bsz, s_new, h, dh = q.shape
    buf = k_all.shape[1] - s_new
    offs = np.concatenate([np.arange(w // d + 1) * d for w, d in DILATED_GROUPS])
    idx = buf + jnp.arange(s_new)[:, None] - offs[None, :]
    valid = idx >= 0
    idx = jnp.maximum(idx, 0)
    kg = k_all[:, idx]
    vg = v_all[:, idx]
    sc = jnp.einsum('bshd,bsnhd->bhsn', q, kg).astype(F32) * dh ** -0.5
    sc = jnp.where(valid[None, None], sc, -jnp.inf)
    p = jax.nn.softmax(sc, axis=-1)
    return jnp.einsum('bhsn,bsnhd->bshd', p, vg.astype(F32))

def stick_breaking_weights(z, mask):
    log_beta = jax.nn.log_sigmoid(z)
    log_keep = jnp.where(mask, jax.nn.log_sigmoid(-z), 0.0)
    log_after = lax.cumsum(log_keep, axis=z.ndim - 1, reverse=True) - log_keep
    return jnp.where(mask, jnp.exp(log_beta + log_after), 0.0)

def stick_breaking_prompt(q, k, v, bias):
    bsz, t, h, dh = q.shape
    nb = t // SB_BLOCK
    qb = jnp.moveaxis(q.reshape(bsz, nb, SB_BLOCK, h, dh), 1, 0)
    vf = v.astype(F32)
    kpos = jnp.arange(t)
    bias_f = bias.astype(F32)[None, :, None, None]

    def one_block(args):
        qblk, n = args
        z = jnp.einsum('bqhd,bkhd->bhqk', qblk, k).astype(F32) * dh ** -0.5 + bias_f
        qpos = n * SB_BLOCK + jnp.arange(SB_BLOCK)
        a = stick_breaking_weights(z, kpos[None, :] < qpos[:, None])
        return jnp.einsum('bhqk,bkhd->bqhd', a, vf)

    o = lax.map(one_block, (qb, jnp.arange(nb)))
    return jnp.moveaxis(o, 0, 1).reshape(bsz, t, h, dh)

def stick_breaking_sample(q, k_all, v_all, bias):
    bsz, s_new, h, dh = q.shape
    past = k_all.shape[1] - s_new
    z = jnp.einsum('bqhd,bkhd->bhqk', q, k_all).astype(F32) * dh ** -0.5 + bias.astype(F32)[None, :, None, None]
    qpos = past + jnp.arange(s_new)
    kpos = jnp.arange(past + s_new)
    a = stick_breaking_weights(z, kpos[None, :] < qpos[:, None])
    return jnp.einsum('bhqk,bkhd->bqhd', a, v_all.astype(F32))

def hgrn2_chunked(q, k, v, log_f, s0):
    bsz, t = q.shape[:2]
    c = min(HGRN_CHUNK, t)
    tp = -(-t // c) * c
    pad = lambda a: jnp.pad(a.astype(F32), ((0, 0), (0, tp - t), (0, 0), (0, 0)))
    nc = tp // c
    chunks = lambda a: jnp.swapaxes(a.reshape((bsz, nc, c) + a.shape[2:]), 0, 1)
    causal = jnp.tril(jnp.ones((c, c), bool))[None, :, :, None, None]

    def step(state, xs):
        qc, kc, vc, gc = xs
        b = jnp.cumsum(gc, axis=1)
        o_inter = jnp.einsum('bthk,bhkv->bthv', qc * jnp.exp(b), state)
        decay = jnp.exp(jnp.where(causal, b[:, :, None] - b[:, None, :], -jnp.inf))
        att = jnp.einsum('bthk,bshk,btshk->bhts', qc, kc, decay)
        o = o_inter + jnp.einsum('bhts,bshv->bthv', att, vc)
        b_last = b[:, -1]
        state = jnp.exp(b_last)[..., None] * state + jnp.einsum('bshk,bshv->bhkv', kc * jnp.exp(b_last[:, None] - b), vc)
        return state, o

    xs = tuple(chunks(pad(a)) for a in (q, k, v, log_f))
    state, o = lax.scan(step, s0.astype(F32), xs)
    o = jnp.swapaxes(o, 0, 1).reshape(bsz, tp, q.shape[2], v.shape[-1])[:, :t]
    return o, state

def spatial_gate(u, v, w_s, b_s):
    bsz, t, g, dc = v.shape
    c = min(SGU_CHUNK, t)
    w = jnp.tril(w_s[:, :c, :c])
    vb = v.reshape(bsz, t // c, c, g, dc)
    mixed = jnp.einsum('gpq,bnqgc->bnpgc', w, vb) + jnp.swapaxes(b_s[:, :c], 0, 1)[:, :, None]
    return u * mixed.reshape(bsz, t, g, dc)

def project_mixers(h, lp, layer, lbs):
    bsz, t, _ = h.shape
    cuts, acc = [], 0
    for w in PROJ_SPLITS[:-1]:
        acc += w
        cuts.append(acc)
    qa, ka, va, qb, kb, vb, qc, fc, ic, gc, ud, vd = jnp.split(h @ lp['w_in'], cuts, axis=-1)
    heads = lambda a, n: a.reshape(bsz, t, n, a.shape[-1] // n)
    fz = heads(fc, C_HEADS).astype(F32)
    if layer == 0:
        log_f = jax.nn.log_sigmoid(fz)
        k_c = jax.nn.sigmoid(-fz)
    else:
        lb = lbs[layer].reshape(C_HEADS, C_KEY_DIM)
        log_f = jnp.logaddexp(jnp.log(lb), jnp.log1p(-lb) + jax.nn.log_sigmoid(fz))
        k_c = (1.0 - lb) * jax.nn.sigmoid(-fz)
    return {
        'qa': rms_norm(heads(qa, A_HEADS), lp['a_q_norm_g']),
        'ka': rms_norm(heads(ka, A_HEADS), lp['a_k_norm_g']),
        'va': heads(va, A_HEADS),
        'qb': heads(qb, B_HEADS), 'kb': heads(kb, B_HEADS), 'vb': heads(vb, B_HEADS),
        'qc': jax.nn.silu(heads(qc, C_HEADS)), 'kc': k_c, 'log_f': log_f,
        'vc': heads(ic, C_HEADS), 'gc': heads(gc, C_HEADS),
        'ud': jax.nn.gelu(heads(ud, D_GROUPS), approximate=False),
        'vd': jax.nn.gelu(heads(vd, D_GROUPS), approximate=False),
    }

def merge_branches(h, oa, ob, oc, od, lp):
    bsz, t, _ = h.shape
    flat = lambda a: a.reshape(bsz, t, -1).astype(h.dtype)
    gates = jax.nn.sigmoid((h @ lp['w_merge_gate'] + lp['b_merge_gate']).astype(F32)).astype(h.dtype)
    ga, gb, gc, gd = jnp.split(gates, N_BRANCH, axis=-1)
    merged = (ga * (flat(oa) @ lp['w_branch_a']) + gb * (flat(ob) @ lp['w_branch_b'])
              + gc * (flat(oc) @ lp['w_branch_c']) + gd * (flat(od) @ lp['w_branch_d']))
    return merged @ lp['w_out']

def mixers_prompt(h, lp, layer, lbs):
    p = project_mixers(h, lp, layer, lbs)
    bsz, t, _ = h.shape
    oa = dilated_attention_prompt(p['qa'], p['ka'], p['va'])
    ob = stick_breaking_prompt(p['qb'], p['kb'], p['vb'], lp['sb_bias'])
    s0 = jnp.zeros((bsz, C_HEADS, C_KEY_DIM, C_VAL_DIM), F32)
    oc_raw, s_c = hgrn2_chunked(p['qc'], p['kc'], p['vc'], p['log_f'], s0)
    oc = rms_norm(oc_raw, lp['c_out_norm_g']) * jax.nn.silu(p['gc'])
    od = spatial_gate(p['ud'], p['vd'], lp['sgu_w'], lp['sgu_b'])
    keep = min(SWA_SPAN, t)
    state = (p['ka'][:, t - keep:], p['va'][:, t - keep:], p['kb'], p['vb'], s_c)
    return merge_branches(h, oa, ob, oc, od, lp), state

def mixers_sample(h, lp, layer, lbs, swa_k, swa_v, sb_k, sb_v, page_table, s_hgrn):
    p = project_mixers(h, lp, layer, lbs)
    bsz = h.shape[0]
    oa = dilated_attention_sample(p['qa'], jnp.concatenate([swa_k, p['ka']], axis=1),
                                  jnp.concatenate([swa_v, p['va']], axis=1))
    past_k = sb_k[layer][page_table].reshape(bsz, -1, B_HEADS, B_HEAD_DIM)
    past_v = sb_v[layer][page_table].reshape(bsz, -1, B_HEADS, B_HEAD_DIM)
    ob = stick_breaking_sample(p['qb'], jnp.concatenate([past_k, p['kb']], axis=1),
                               jnp.concatenate([past_v, p['vb']], axis=1), lp['sb_bias'])
    oc_raw, s_c = hgrn2_chunked(p['qc'], p['kc'], p['vc'], p['log_f'], s_hgrn)
    oc = rms_norm(oc_raw, lp['c_out_norm_g']) * jax.nn.silu(p['gc'])
    od = spatial_gate(p['ud'], p['vd'], lp['sgu_w'], lp['sgu_b'])
    state = (p['ka'], p['va'], p['kb'], p['vb'], s_c.astype(s_hgrn.dtype), p['vd'])
    return merge_branches(h, oa, ob, oc, od, lp), state

def swiglu(x, wg, wu, wd):
    return (jax.nn.silu(x @ wg) * (x @ wu)) @ wd

def routed_experts(x2, idx, wts, w_gate, w_up, w_down):
    n, d = x2.shape
    n_assign = n * TOP_K
    e_flat = idx.reshape(-1)
    tok_flat = jnp.arange(n_assign, dtype=jnp.int32) // TOP_K
    w_flat = wts.reshape(-1)
    order = jnp.argsort(e_flat)
    e_sorted = e_flat[order]
    counts = jnp.bincount(e_flat, length=N_EXPERTS)
    starts = jnp.cumsum(counts) - counts
    padded = (counts + MOE_BLOCK - 1) // MOE_BLOCK * MOE_BLOCK
    pends = jnp.cumsum(padded)
    dest = pends[e_sorted] - padded[e_sorted] + jnp.arange(n_assign) - starts[e_sorted]
    n_blocks = -(-n_assign // MOE_BLOCK) + N_EXPERTS
    rows = n_blocks * MOE_BLOCK
    row_tok = jnp.full((rows,), n, jnp.int32).at[dest].set(tok_flat[order])
    row_w = jnp.zeros((rows,), x2.dtype).at[dest].set(w_flat[order])
    blk_exp = jnp.minimum(jnp.searchsorted(pends, jnp.arange(n_blocks) * MOE_BLOCK, side='right'), N_EXPERTS - 1)
    x_pad = jnp.concatenate([x2, jnp.zeros((1, d), x2.dtype)], axis=0)

    def step(out, blk):
        toks, wb, e = blk
        y = swiglu(x_pad[toks], w_gate[e], w_up[e], w_down[e]) * wb[:, None]
        return out.at[toks].add(y.astype(out.dtype)), None

    out, _ = lax.scan(step, jnp.zeros((n + 1, d), x2.dtype),
                      (row_tok.reshape(n_blocks, MOE_BLOCK), row_w.reshape(n_blocks, MOE_BLOCK), blk_exp))
    return out[:n]

def moe_ffn(h, lp):
    bsz, t, d = h.shape
    x2 = h.reshape(bsz * t, d)
    scores = jax.nn.sigmoid((x2 @ lp['w_router']).astype(F32))
    choice = scores + lp['b_router'].astype(F32)
    grouped = choice.reshape(-1, N_EXPERT_GROUPS, N_EXPERTS // N_EXPERT_GROUPS)
    group_score = jnp.sum(lax.top_k(grouped, 2)[0], axis=-1)
    _, top_groups = lax.top_k(group_score, TOPK_GROUPS)
    group_mask = jnp.any(top_groups[..., None] == jnp.arange(N_EXPERT_GROUPS), axis=1)
    expert_mask = jnp.repeat(group_mask, N_EXPERTS // N_EXPERT_GROUPS, axis=1)
    _, idx = lax.top_k(jnp.where(expert_mask, choice, -jnp.inf), TOP_K)
    gate = jnp.take_along_axis(scores, idx, axis=1)
    gate = gate / jnp.sum(gate, axis=-1, keepdims=True) * ROUTE_SCALE
    routed = routed_experts(x2, idx, gate.astype(x2.dtype), lp['w_exp_gate'], lp['w_exp_up'], lp['w_exp_down'])
    shared = swiglu(x2, lp['w_sh_gate'], lp['w_sh_up'], lp['w_sh_down'])
    return (routed + shared).reshape(bsz, t, d)

def decoder_layer(x, c, lp, mix_fn):
    mod = jax.nn.silu(c) @ lp['w_ada'] + lp['b_ada']
    sh1, sc1, g1, sh2, sc2, g2 = [m[:, None, :] for m in jnp.split(mod, 6, axis=-1)]
    h = rms_norm(x, lp['norm1_g']) * (1.0 + sc1) + sh1
    mix, state = mix_fn(h)
    x = x + g1 * mix
    h = rms_norm(x, lp['norm2_g']) * (1.0 + sc2) + sh2
    x = x + g2 * moe_ffn(h, lp)
    return x, state

def setup_inputs(seed: int = 0) -> dict:
    key = jax.random.key(seed)
    ks = jax.random.split(key, 37)
    nrm = lambda i, shape, s: s * jax.random.normal(ks[i], shape, F32)
    D = D_MODEL
    n_pages = PAST_LEN // PAGE_SIZE
    n_used = DEC_BATCH * n_pages
    n_phys = n_used + max(n_used // 4, 1)
    swa_buf = min(SWA_SPAN, PAST_LEN)
    perm = jax.random.permutation(ks[9], n_phys)
    page_table = perm[:n_used].reshape(DEC_BATCH, n_pages).astype(jnp.int32)
    return {
        'x_prompt': nrm(0, (BATCH, SEQ, D), 1.0),
        'x_sample': nrm(1, (DEC_BATCH, DEC_SEQ, D), 1.0),
        'c_prompt': nrm(2, (BATCH, D), 1.0),
        'c_sample': nrm(3, (DEC_BATCH, D), 1.0),
        'cache_swa_k': nrm(4, (DEPTH, DEC_BATCH, swa_buf, A_HEADS, A_HEAD_DIM), 1.0),
        'cache_swa_v': nrm(5, (DEPTH, DEC_BATCH, swa_buf, A_HEADS, A_HEAD_DIM), 1.0),
        'cache_sb_k': nrm(6, (DEPTH, n_phys, PAGE_SIZE, B_HEADS, B_HEAD_DIM), 1.0),
        'cache_sb_v': nrm(7, (DEPTH, n_phys, PAGE_SIZE, B_HEADS, B_HEAD_DIM), 1.0),
        'state_hgrn': nrm(8, (DEPTH, DEC_BATCH, C_HEADS, C_KEY_DIM, C_VAL_DIM), 0.5),
        'page_table': page_table,
        'norm1_g': 1.0 + nrm(10, (DEPTH, D), 0.05),
        'norm2_g': 1.0 + nrm(11, (DEPTH, D), 0.05),
        'w_ada': nrm(12, (DEPTH, D, 6 * D), 0.5 * D ** -0.5),
        'b_ada': nrm(13, (DEPTH, 6 * D), 0.02),
        'w_in': nrm(14, (DEPTH, D, IN_WIDTH), D ** -0.5),
        'a_q_norm_g': 1.0 + nrm(15, (DEPTH, A_HEAD_DIM), 0.05),
        'a_k_norm_g': 1.0 + nrm(16, (DEPTH, A_HEAD_DIM), 0.05),
        'sb_bias': SB_BIAS_INIT + nrm(36, (DEPTH, B_HEADS), 0.1),
        'c_lower_bounds': nrm(17, (DEPTH, C_KEY_WIDTH), 0.5),
        'c_out_norm_g': 1.0 + nrm(18, (DEPTH, C_VAL_DIM), 0.05),
        'sgu_w': nrm(19, (DEPTH, D_GROUPS, SGU_CHUNK, SGU_CHUNK), SGU_CHUNK ** -0.5),
        'sgu_b': 1.0 + nrm(20, (DEPTH, D_GROUPS, SGU_CHUNK), 0.1),
        'w_branch_a': nrm(21, (DEPTH, A_WIDTH, D), A_WIDTH ** -0.5),
        'w_branch_b': nrm(22, (DEPTH, B_WIDTH, D), B_WIDTH ** -0.5),
        'w_branch_c': nrm(23, (DEPTH, C_VAL_WIDTH, D), C_VAL_WIDTH ** -0.5),
        'w_branch_d': nrm(24, (DEPTH, D_WIDTH, D), D_WIDTH ** -0.5),
        'w_merge_gate': nrm(25, (DEPTH, D, N_BRANCH * D), D ** -0.5),
        'b_merge_gate': nrm(26, (DEPTH, N_BRANCH * D), 0.02),
        'w_out': nrm(27, (DEPTH, D, D), D ** -0.5),
        'w_router': nrm(28, (DEPTH, D, N_EXPERTS), D ** -0.5),
        'b_router': nrm(29, (DEPTH, N_EXPERTS), 0.01),
        'w_exp_gate': nrm(30, (DEPTH, N_EXPERTS, D, EXPERT_DIM), D ** -0.5),
        'w_exp_up': nrm(31, (DEPTH, N_EXPERTS, D, EXPERT_DIM), D ** -0.5),
        'w_exp_down': nrm(32, (DEPTH, N_EXPERTS, EXPERT_DIM, D), EXPERT_DIM ** -0.5),
        'w_sh_gate': nrm(33, (DEPTH, D, SHARED_DIM), D ** -0.5),
        'w_sh_up': nrm(34, (DEPTH, D, SHARED_DIM), D ** -0.5),
        'w_sh_down': nrm(35, (DEPTH, SHARED_DIM, D), SHARED_DIM ** -0.5),
    }

def reference(x_prompt, x_sample, c_prompt, c_sample, cache_swa_k, cache_swa_v, cache_sb_k, cache_sb_v,
              state_hgrn, page_table, norm1_g, norm2_g, w_ada, b_ada, w_in, a_q_norm_g, a_k_norm_g, sb_bias,
              c_lower_bounds, c_out_norm_g, sgu_w, sgu_b, w_branch_a, w_branch_b, w_branch_c, w_branch_d,
              w_merge_gate, b_merge_gate, w_out, w_router, b_router, w_exp_gate, w_exp_up, w_exp_down,
              w_sh_gate, w_sh_up, w_sh_down):
    lbs = jax.nn.softmax(c_lower_bounds.astype(F32), axis=0)
    lbs = jnp.cumsum(lbs, axis=0) - lbs[0]
    xp, xs = x_prompt, x_sample
    st_p, st_s = [], []
    for layer in range(DEPTH):
        lp = {
            'norm1_g': norm1_g[layer], 'norm2_g': norm2_g[layer], 'w_ada': w_ada[layer], 'b_ada': b_ada[layer],
            'w_in': w_in[layer], 'a_q_norm_g': a_q_norm_g[layer], 'a_k_norm_g': a_k_norm_g[layer],
            'sb_bias': sb_bias[layer],
            'c_out_norm_g': c_out_norm_g[layer], 'sgu_w': sgu_w[layer], 'sgu_b': sgu_b[layer],
            'w_branch_a': w_branch_a[layer], 'w_branch_b': w_branch_b[layer], 'w_branch_c': w_branch_c[layer],
            'w_branch_d': w_branch_d[layer], 'w_merge_gate': w_merge_gate[layer], 'b_merge_gate': b_merge_gate[layer],
            'w_out': w_out[layer], 'w_router': w_router[layer], 'b_router': b_router[layer],
            'w_exp_gate': w_exp_gate[layer], 'w_exp_up': w_exp_up[layer], 'w_exp_down': w_exp_down[layer],
            'w_sh_gate': w_sh_gate[layer], 'w_sh_up': w_sh_up[layer], 'w_sh_down': w_sh_down[layer],
        }
        xp, sp = decoder_layer(xp, c_prompt, lp, functools.partial(mixers_prompt, lp=lp, layer=layer, lbs=lbs))
        st_p.append(sp)
        xs, ss = decoder_layer(xs, c_sample, lp, functools.partial(
            mixers_sample, lp=lp, layer=layer, lbs=lbs, swa_k=cache_swa_k[layer], swa_v=cache_swa_v[layer],
            sb_k=cache_sb_k, sb_v=cache_sb_v, page_table=page_table, s_hgrn=state_hgrn[layer]))
        st_s.append(ss)
    stack = lambda states, i: jnp.stack([s[i] for s in states])
    swa_k_p, swa_v_p, sb_k_p, sb_v_p, hgrn_p = (stack(st_p, i) for i in range(5))
    swa_k_s, swa_v_s, sb_k_s, sb_v_s, hgrn_s, sgu_v_s = (stack(st_s, i) for i in range(6))
    return (xp, xs, swa_k_p, swa_v_p, sb_k_p, sb_v_p, hgrn_p, swa_k_s, swa_v_s, sb_k_s, sb_v_s, hgrn_s, sgu_v_s)


_drawn_inputs = setup_inputs


def setup_inputs(seed=0):
    import zlib

    import numpy as np

    out = dict(_drawn_inputs(seed))
    spreads = {}
    factors = {'cache_sb_k': 39.64,
     'a_q_norm_g': 7.164,
     'sb_bias': 40.016,
     'c_out_norm_g': 3.274,
     'b_merge_gate': 5.987,
     'cache_sb_v': 8.0,
     'w_branch_b': 8.0}
    for name, (base, spread) in spreads.items():
        noise = np.random.default_rng([zlib.crc32(name.encode()), seed]).standard_normal(out[name].shape)
        drawn = base * np.exp(spread * noise) if base else spread * noise
        out[name] = __import__('jax').numpy.asarray(drawn.astype(out[name].dtype))
    for name, factor in factors.items():
        out[name] = (out[name] * factor).astype(out[name].dtype)
    return out
```

```python
from contextlib import ExitStack

import concourse.bass as bass
from concourse import mybir

ALU = mybir.AluOpType
ACT = mybir.ActivationFunctionType
F32 = mybir.dt.float32
I32 = mybir.dt.int32
U32 = mybir.dt.uint32
AX = mybir.AxisListType.X

P = 128
D = 1024
KC = D // P
SEQ = 512
NT = SEQ // P
NS = 8
TILES = NT + 1
TOK = SEQ + NS
AH, BH, CH, DG, HD = 6, 4, 4, 4, 64
AW, BW = AH * HD, BH * HD
GROUPS_A = 3
PAST = 4096
PAGE = 128
PAGES = PAST // PAGE
SWA = 2048
NE, TOPK, EG, TOPG = 64, 8, 8, 4
ED = 256
MAXB = 99
EPS = 1e-6
SCALE = HD ** -0.5
BIG = 1e30
NB = 4
ROUTE_SCALE = 2.5
NPARAM = 15
PANEL = 512
IN_W = 3 * AW + 3 * BW + 6 * 256
BR_K = [AW // P, BW // P, 2, 2]
BR_AT = [0, 3, 5, 7]
LEVELS = [64, 32, 16, 8, 4, 2, 1]

SEMS = """const_ready params_in x_in c_in bada_in silu_c cT_ps cT_ready small_ps small_ready dense_out dense_evac
mod_gain bc_ps rstd_sqrt h_row h_ps hT_evac hro0 hro1
w_in0 w_in1 w_br0 w_br1 qk_sum qk_sqrt qk_norm t_ps t_evac t_act rows_saved rows_out
a_s a_nm a_exp a_p a_pt a_ptc a_pv a_o
b_z b_zs b_l b_lk b_after b_sum b_e b_a b_pv b_o
kv0 kv1 kv2 kv3 kvk_used kvv_used qd_ready qb_ps as_used sT_ps s_nm s_exp s_norm pT_ps pT_ready as_pv as_o
idx_ready bs_qd bs_z bs_l bs_tot bs_cross bs_e bs_ex bs_pv bs_o
c_lf c_x c_ab c_e c_q c_k c_lev c_cp c_kk c_kt c_ktc c_pv c_s c_raw c_sum c_sqrt hg_out
s0_in c_vd c_vb c_new c_so
d_gelu d_mix d_o oT_ps oT_evac m_sig m_acc x2_in g_ps mix_sb x1_ready
sh_gu sh_rv sh_sg sh_h sh_hT sh_hTc sh_y sh_row
r_log r_sc r_mask r_pos r_tab_in r_tab r_ready
wg0 wg1 wg2 wd0 wd1 wd2 x_col x_t x_ca x_cv gu_done m_sg m_h m_hT m_hTc dn_done y_a y_v yst0 yst1 yst2
gather0 gather1 gather2 gather3 f_used f_acc out_done act_chain dve_chain pool_chain""".split()


class Chain:

    def __init__(self, eng, sem):
        self.eng, self.sem, self.n = eng, sem, 0

    def __call__(self, ins):
        self.n += 1
        ins.then_inc(self.sem, 1)
        self.eng.wait_ge(self.sem, self.n)


def later(p):
    return not isinstance(p, int) or p > 0


def block_at(p, q, off):
    return p + (q + off) // 3, (q + off) % 3


THREES_MIN = -(-TOK * TOPK // P) // 3


def dense_plan():
    panels = [("ada", g, 1) for g in range(6)]
    panels += [("in", g, TILES) for g in range(7)]
    panels += [("gate", (half, br), 8) for half in range(2) for br in range(NB)]
    panels += [("out", g, TILES) for g in range(2)]
    panels += [("ada", g, 1) for g in range(6, 12)]
    panels += [("shgu", 0, 0), ("shd", 0, 0)]
    used, n = [], 0
    for _, _, outs in panels:
        n += outs
        used.append(n)
    return panels, used


def trunk(nc, A, O):
    panels, panel_used = dense_plan()
    at_of = {(kind, g): i for i, (kind, g, _) in enumerate(panels)}
    out_before = [0] + panel_used
    IN0_OUT, GATE_OUT = out_before[at_of[("in", 0)]], out_before[at_of[("gate", (0, 0))]]
    IN0, GATE0, OUT0, ADA2, SHGU, SHD = (at_of[k] for k in (("in", 0), ("gate", (0, 0)), ("out", 0), ("ada", 6), ("shgu", 0), ("shd", 0)))

    h2d = nc.dram_tensor("h2_rows", (TOK, D), F32, kind="Internal").ap()
    yd = nc.dram_tensor("expert_rows", (TOK * TOPK, D), F32, kind="Internal").ap()

    with ExitStack() as ctx:
        sem = {n: ctx.enter_context(nc.semaphore(n)) for n in SEMS}
        total = 53200
        arena = ctx.enter_context(nc.sbuf_tensor("arena", [P, total], F32))
        top = [0]

        def view(off, dims, parts=P, dt=F32):
            n = 1
            for d in dims:
                n *= d
            ap = arena[0:parts, off:off + n]
            if dt is not F32:
                ap = ap.bitcast(dt)
            names = "abcd"[:len(dims)]
            if len(dims) > 1:
                kw = {names[i]: dims[i] for i in range(1, len(dims))}
                ap = ap.rearrange(f"p ({' '.join(names)}) -> p {' '.join(names)}", **kw)
            return ap

        def region(n):
            at = top[0]
            top[0] += n
            assert top[0] <= total, (top[0], total)
            return at

        def new(dims, parts=P, dt=F32):
            n = 1
            for d in dims:
                n *= d
            return view(region(n), dims, parts, dt)

        bank = [ctx.enter_context(nc.psum_tensor(f"bank{i}", [P, 512], F32)) for i in range(8)]

        ident, ones, tri_gt, tri_lt = new([P]), new([P]), new([P]), new([P])
        amult, aneg = new([NT, P]), new([NT, P])
        lmask = new([8, P], dt=I32)
        iota_e, iota_s, iota_b, row_code, pcol = new([NE]), new([P]), new([MAXB]), new([TILES, TOPK]), new([1])
        d88, sel9, eps_t = new([8, 8]), new([P]), new([1])
        qk_g, co_g, sbb = new([2, HD]), new([HD]), new([BH])
        sgu_wt, sgu_bt, w00, b00 = new([DG, P]), new([DG]), new([DG]), new([DG])
        bmg_t, brt, w_router = new([32]), new([NE]), new([KC, NE])
        pt_sb, q4, idx_kv = new([NS], dt=I32), new([1], dt=I32), new([NS, 4], dt=I32)
        cT, gates = new([KC, 9]), new([TILES, TOPK])
        ssq, rstd, qk_ss = new([8]), new([8]), new([TILES, 12])
        nm, den = new([2]), new([2])
        HT = region(KC * TOK)
        hT = view(HT, [KC, TOK])
        mod_sb = new([3, D])
        ring = region(8192)
        X = region(5760)
        W = region(TILES * 1792)
        PV = region(TILES * 1664)
        T = region(14 * SEQ)
        tts = new([4, NS])
        os_T = new([5, NS])
        rows_s = new([1024])

        xr = view(X, [TILES, D])
        orow = view(X, [TILES, 1152])
        pqk = view(W, [TILES, 1792])
        pv = view(PV, [TILES, 1664])
        tt = view(T, [14, SEQ])
        panel = [view(ring + 4096 * i, [KC, PANEL]) for i in range(2)]
        panel_wide = [view(ring + 4096 * i, [4, D]) for i in range(2)]
        branch_panel = [view(PV + 1536 * i, [3, PANEL]) for i in range(2)]
        kvbuf = [ring + 2048 * i for i in range(4)]

        bada = view(T, [3, D], 9)
        hrow = [view(T + 3072 + 1024 * i, [D]) for i in range(2)]
        junk = view(T + 5120, [D])
        g9 = view(T + 6144, [D], 9)
        cs = view(W, [D], 9)
        bmg_r = view(W + 2048, [P], 32)
        sgub_r = view(W + 2176, [P], 4)
        sguw_r = view(W + 2304, [DG, P])
        m_dist, m_bits = view(W + 3072, [NT, P], dt=I32), view(W + 3584, [NT, P], dt=I32)
        m_a, m_b, m_c = (view(W + 4096 + 512 * i, [NT, P]) for i in range(3))
        l_t, l_s, l_x, l_sh = (view(W + 5632 + 128 * i, [P], dt=I32) for i in range(4))
        l_gt, l_eq, tri_le = view(W + 6144, [P]), view(W + 6272, [P]), view(W + 6400, [P])
        qk_sq = view(T, [768])
        a_sm = [view(W + 512 * i, [512]) for i in range(2)]
        a_pr = [view(W + 1024 + 512 * i, [512]) for i in range(2)]
        a_prT = [view(W + 2048 + 512 * i, [4, P]) for i in range(2)]
        JN = [SEQ - j * P for j in range(NT)]
        JO = [sum(JN[:j]) for j in range(NT)]
        JW = sum(JN)
        bz = [view(W + 3840 * i, [JW]) for i in range(2)]
        bl = [view(W + 3840 * i + 1280, [JW]) for i in range(2)]
        blb = [view(W + 3840 * i + 2560, [JW]) for i in range(2)]
        JPIECE = [(0, 0, 512, 0), (1, 512, 384, 0), (2, 896, 384, 0)]
        J_BANK = [(0, 0), (1, 0), (2, 0), (2, 256)]
        as_qd = view(T, [NS, AW], NS)
        as_prod = view(T + 3072, [3, AW])
        as_s = view(T + 4224, [3, NS * AH])
        as_self = view(T + 4368, [NS, AH], NS)
        as_p = view(T + 4416, [392], 48)
        as_pT = view(T + 4808, [4, 48])
        as_tmp = view(T + 5000, [AH], NS)
        bs_z, bs_l, bs_lb = (view(W + 1024 * i, [NS, 32, BH]) for i in range(3))
        bs_prod = view(W + 3072, [8, BW])
        bs_e = [view(W + 3072 + 1024 * i, [NS, 32, BH]) for i in range(2)]
        bs_qd = view(W + 5120, [NS, BW], NS)
        bs_tot = view(W + 7168, [NS, BH])
        ck, cb, cx = (view(W + 1024 * i, [2, SEQ]) for i in range(3))
        cq1 = [view(W + 3072, [2, SEQ]), view(T, [2, SEQ])]
        ck1 = [view(W + 4096, [2, SEQ]), view(T + 1024, [2, SEQ])]
        c_att = view(W + 5120, [CH, NT, P])
        c_krow = view(W + 7168, [8, P])
        c_S = view(W + 8192, [2, HD])
        c_tot = view(W + 8320, [2, NT])
        c_qd = view(W + 8328, [2, NS, NS])
        cs_lf, cs_k = view(W + 8456, [2, NS]), view(W + 8472, [2, NS])
        c_ss = view(W + 8488, [TILES, CH])
        c_vdiag = view(T + 2048, [2, NS, HD], NS)
        c_S0 = view(T + 3072, [NS, 2, HD])
        c_new = view(T + 4096, [NS, 2, HD])
        cs_tmp = view(W + 3072, [NS, HD])
        c_sq = view(W + 4096, [CH, HD])
        oT = view(T, [9, TOK])
        mT = view(W, [KC, TOK])
        sg_m = [view(W + 4160 + 520 * i, [TOK]) for i in range(2)]
        tmp_m = view(W + 5200, [TOK])
        mixs = [view(W + 5720 + 512 * i, [512]) for i in range(2)]
        mixt = view(W + 6744, [512])
        sh = view(PV, [TILES, D])
        xg = [view(PV + 5120, [D]), view(PV + 6144, [D]), view(T + 3072, [D])]
        sgate = [view(PV + 7168, [ED]), view(PV + 7424, [ED]), view(W + 7168, [ED])]
        hmid = [view(PV + 7680, [ED]), view(PV + 7936, [ED]), view(W + 7424, [ED])]
        xT = [view(T, [KC, P]), view(T + D, [KC, P]), view(T + 4096, [KC, P])]
        hmT = [view(T + 2048, [2, P]), view(T + 2304, [2, P]), view(W + 7680, [2, P])]
        slot_tok = view(T + 2560, [MAXB], dt=I32)
        be_row = view(T + 2660, [P], 1, dt=I32)
        gidx = [view(T + 2790 + i, [1], dt=I32) for i in range(3)]
        slot_row = view(T + 2840, [MAXB], dt=I32)
        sidx = [view(T + 2940 + i, [1], dt=I32) for i in range(3)]
        dest_i = view(T + 2800, [TILES, TOPK], dt=I32)
        ybuf = [view(T + 5120, [D]), view(T + 6144, [D]), view(W + 6144, [D])]
        onehot = view(W + 6144, [TILES, TOPK, NE])
        r_s = view(T + 5120, [TILES, NE])
        r_c = view(T + 5440, [TILES, NE])
        r_M = view(T + 5760, [TILES, NE])
        r_m8 = view(T + 6080, [EG, 8])
        r_g, r_g8, r_gi = view(T + 6144, [8]), view(T + 6152, [8]), view(T + 6160, [8], dt=U32)
        r_gf, r_gm = view(T + 6168, [8]), view(T + 6176, [8])
        r_eq = view(T + 6184, [8, 4])
        r_mc, r_t8, r_ti, r_tf = view(T + 6216, [NE]), view(T + 6280, [8]), view(T + 6288, [8], dt=U32), view(T + 6296, [8])
        r_prod = view(T + 6304, [TOPK, NE])
        r_sum = view(T + 6816, [1])
        r_cnt, r_cnti, r_nb, r_end = view(T + 6820, [NE]), view(T + 6884, [NE], dt=I32), view(T + 6948, [NE]), view(T + 7012, [NE])
        r_st, r_be = view(T + 7076, [NE]), view(T + 7140, [1])
        r_d, r_dv = view(T + 7142, [8]), view(T + 7150, [8], dt=I32)
        r_f8 = view(T + 7158, [8])
        r_hs = mod_sb[:, 0, :].rearrange("p (a b) -> p a b", b=P)
        r_hb = mod_sb[:, 1, 0:TOPK * MAXB].rearrange("p (a b) -> p a b", b=MAXB)
        wset = [W, ring, HT]
        wgu = [view(w, [2, KC, ED]) for w in wset]
        gu_bank = [2, 3, 7]
        wdn = [view(w + 4096, [2, D]) for w in wset]
        fbuf = [view(W + D * i, [D]) for i in range(4)]

        def rows(t):
            return P if t < NT else NS

        def cols(t):
            return slice(t * P, t * P + rows(t))

        blk = ctx.enter_context(nc.Block())

        @blk.sync
        def _(sp):
            def load(dst, src, s):
                sp.dma_start(dst, src).then_inc(sem[s], 16)

            def w_panel(name, c0, w):
                return A[name][0, :, c0:c0 + w].rearrange("(c p) n -> p c n", p=P)

            def panel_load(i):
                kind, g, _ = panels[i]
                s = f"w_in{i % 2}"
                if i >= 2:
                    sp.wait_ge(sem["dense_out"], panel_used[i - 2])
                dst = panel[i % 2]
                if kind == "ada":
                    load(dst, w_panel("w_ada", g * PANEL, PANEL), s)
                elif kind == "in":
                    w = min(PANEL, IN_W - g * PANEL)
                    load(dst[:, :, 0:w], w_panel("w_in", g * PANEL, w), s)
                elif kind == "gate":
                    load(dst, w_panel("w_merge_gate", g[1] * D + g[0] * PANEL, PANEL), s)
                elif kind == "out":
                    load(dst, w_panel("w_out", g * PANEL, PANEL), s)
                elif kind == "shgu":
                    load(dst[:, :, 0:ED], w_panel("w_sh_gate", 0, ED), s)
                    load(dst[:, :, ED:2 * ED], w_panel("w_sh_up", 0, ED), s)
                else:
                    load(panel_wide[i % 2][:, 0:2, :], w_panel("w_sh_down", 0, D), s)

            def branch_load(k):
                half, br = k // NB, k % NB
                if k >= 2:
                    sp.wait_ge(sem["dense_out"], panel_used[GATE0 + k - 2])
                name = "w_branch_" + "abcd"[br]
                load(branch_panel[k % 2][:, 0:BR_K[br], :], w_panel(name, half * PANEL, PANEL), f"w_br{k % 2}")

            load(cs[0:NS, :], A["c_sample"], "c_in")
            load(cs[NS:NS + 1, :], A["c_prompt"], "c_in")
            panel_load(0)
            panel_load(1)
            load(xr[:, 0:NT, :], A["x_prompt"][0].rearrange("(t p) d -> p t d", p=P), "x_in")
            load(xr[0:NS, NT, :], A["x_sample"][:, 0, :], "x_in")
            load(bada.rearrange("p a b -> p (a b)"), A["b_ada"][0, 0:3 * D].partition_broadcast(9), "bada_in")
            load(g9, A["norm1_g"][0].partition_broadcast(9), "bada_in")
            load(qk_g[:, 0, :], A["a_q_norm_g"][0].partition_broadcast(P), "params_in")
            load(qk_g[:, 1, :], A["a_k_norm_g"][0].partition_broadcast(P), "params_in")
            load(co_g, A["c_out_norm_g"][0].partition_broadcast(P), "params_in")
            load(sbb, A["sb_bias"][0].partition_broadcast(P), "params_in")
            load(brt, A["b_router"][0].partition_broadcast(P), "params_in")
            load(sguw_r, A["sgu_w"][0].rearrange("g p q -> p g q"), "params_in")
            load(sgub_r, A["sgu_b"][0], "params_in")
            load(bmg_r, A["b_merge_gate"][0].rearrange("(c p) -> c p", p=P), "params_in")
            load(w_router, A["w_router"][0].rearrange("(c p) n -> p c n", p=P), "params_in")
            with nc.allow_non_contiguous_dma("a few words of parameters and the page table"):
                load(w00[0:NS, :], A["sgu_w"][0, :, 0, 0].partition_broadcast(NS), "params_in")
                load(b00[0:NS, :], A["sgu_b"][0, :, 0].partition_broadcast(NS), "params_in")
                for q in range(4):
                    load(pt_sb[q::4, :], A["page_table"].rearrange("b a -> a b"), "params_in")
            for i in range(2, GATE0):
                panel_load(i)
            sp.wait_ge(sem["qk_norm"], TILES)
            sp.wait_ge(sem["dense_evac"], 6 + 7 * TILES)
            for n, (name, buf, c) in enumerate((("swa_k", pqk, AW), ("swa_v", pv, 0), ("sb_k", pqk, 2 * AW + BW), ("sb_v", pv, AW))):
                w = AW if n < 2 else BW
                sp.dma_start(O[name + "_p"].rearrange("(t p) n -> p t n", p=P), buf[:, 0:NT, c:c + w]).then_inc(sem["rows_out"], 16)
                sp.dma_start(O[name + "_s"], buf[0:NS, NT, c:c + w]).then_inc(sem["rows_out"], 16)
            for n in range(16):
                cache = A["cache_swa_k"] if n < NS else A["cache_swa_v"]
                src = cache[0, n % NS].rearrange("r h d -> r (h d)")
                if n < 4:
                    sp.wait_ge(sem["dense_out"], panel_used[GATE0 - 1])
                elif n < 12:
                    sp.wait_ge(sem["kvk_used"], n - 3)
                else:
                    sp.wait_ge(sem["kvv_used"], n - 11)
                dst = view(kvbuf[n % 4], [3, AW])
                for g, step in enumerate((1, 4, 16)):
                    load(dst[:, g, :], src[SWA - P * step:SWA:step, :], f"kv{n % 4}")
            sp.wait_ge(sem["kvv_used"], NS + 32)
            panel_load(GATE0)
            panel_load(GATE0 + 1)
            sp.wait_ge(sem["as_o"], 1)
            for two in range(2):
                load(c_S0[two * HD:two * HD + HD, :, :, :], A["state_hgrn"][0].rearrange("b (c two) k v -> two k b c v", two=2)[two], "s0_in")
            sp.wait_ge(sem["c_s"], NT)
            for two in range(2):
                load(O["hgrn_p"].rearrange("(c two) k v -> two k c v", two=2)[two], c_S[two * HD:two * HD + HD, :, :], "hg_out")
            sp.wait_ge(sem["c_new"], 2)
            for two in range(2):
                for c in range(2):
                    load(O["hgrn_s"].rearrange("b (c two) k v -> c two k b v", two=2)[c, two], c_new[two * HD:two * HD + HD, :, c, :], "hg_out")
            sp.wait_ge(sem["d_gelu"], 1)
            sp.dma_start(O["sgu_v_s"], pv[0:NS, NT, 1408:1664]).then_inc(sem["rows_out"], 16)
            sp.wait_ge(sem["d_o"], 1)
            sp.wait_ge(sem["rows_out"], 16 * 9)
            branch_load(0)
            branch_load(1)
            for k in range(2, 8):
                panel_load(GATE0 + k)
                branch_load(k)
            sp.wait_ge(sem["oT_ps"], 13)
            load(xr[:, 0:NT, :], A["x_prompt"][0].rearrange("(t p) d -> p t d", p=P), "x2_in")
            load(xr[0:NS, NT, :], A["x_sample"][:, 0, :], "x2_in")
            panel_load(OUT0)
            panel_load(OUT0 + 1)
            sp.wait_ge(sem["dense_out"], out_before[OUT0])
            load(bada.rearrange("p a b -> p (a b)"), A["b_ada"][0, 3 * D:6 * D].partition_broadcast(9), "bada_in")
            load(g9, A["norm2_g"][0].partition_broadcast(9), "bada_in")
            for i in range(ADA2, len(panels)):
                panel_load(i)
            for t in range(TILES):
                sp.wait_ge(sem["h_row"], TILES + t + 1)
                sp.dma_start(h2d[t * P:t * P + rows(t), :], hrow[t % 2][0:rows(t), :]).then_inc(sem[f"hro{t % 2}"], 16)

            sp.wait_ge(sem["r_ready"], 1)
            last = sp.value_load(be_row[0:1, MAXB:MAXB + 1], min_val=THREES_MIN - 2, max_val=MAXB // 3 - 2) + 1

            def block_loads(p, q, first):
                i = p * 3 + q
                e = sp.value_load(be_row[0:1, bass.ds(i, 1)], min_val=0, max_val=NE - 1)
                if not first:
                    sp.wait_ge(sem["gu_done"], i - 2)
                sp.dma_start(wgu[q][:, 0, :, :], A["w_exp_gate"][0, bass.ds(e, 1)].rearrange("e (p c) n -> p (e c) n", c=KC)).then_inc(sem[f"wg{q}"], 16)
                sp.dma_start(wgu[q][:, 1, :, :], A["w_exp_up"][0, bass.ds(e, 1)].rearrange("e (p c) n -> p (e c) n", c=KC)).then_inc(sem[f"wg{q}"], 16)
                if not first:
                    sp.wait_ge(sem["dn_done"], i - 2)
                sp.dma_start(wdn[q], A["w_exp_down"][0, bass.ds(e, 1)].rearrange("e (p c) n -> p (e c) n", c=2)).then_inc(sem[f"wd{q}"], 16)

            sp.wait_ge(sem["sh_y"], TILES)
            for q in range(3):
                block_loads(0, q, True)
            with sp.Fori(1, last + 1) as p:
                for q in range(3):
                    block_loads(p, q, False)
            for q in range(3):
                sp.wait_ge(sem[f"yst{q}"], last * 16 + 16)
            for n in range(TILES * TOPK):
                t, k = n // TOPK, n % TOPK
                if n >= 4:
                    sp.wait_ge(sem["f_used"], n - 3)
                load(fbuf[n % 4][0:rows(t), :], yd.rearrange("(n k) d -> n k d", k=TOPK)[t * P:t * P + rows(t), k, :], f"kv{n % 4}")
            for t in range(TILES):
                sp.wait_ge(sem["f_acc"], t + 1)
                dst = O["y_p"][t * P:t * P + P, :] if t < NT else O["y_s"]
                sp.dma_start(dst, xr[0:rows(t), t, :]).then_inc(sem["out_done"], 16)
            sp.wait_ge(sem["rows_out"], 16 * 9)
            sp.wait_ge(sem["hg_out"], 16 * 6)
            sp.wait_ge(sem["hro0"], 16 * 3)
            sp.wait_ge(sem["hro1"], 16 * 2)
            sp.wait_ge(sem["out_done"], 16 * TILES)

        @blk.gpsimd
        def _(pool):
            step = Chain(pool, sem["pool_chain"])

            def select(out, in_, pattern, base, mult, op, fill):
                step(pool.affine_select(out=out, in_=in_, pattern=pattern, base=base, channel_multiplier=mult,
                                        compare_op=op, fill=fill))

            step(pool.memset(ones, 1.0))
            step(pool.memset(ident, 0.0))
            select(ident, ident, [[-1, P]], 0, 1, ALU.not_equal, 1.0)
            pool.memset(eps_t, EPS)
            select(tri_gt, ones, [[-1, P]], 0, 1, ALU.is_gt, 0.0)
            select(tri_lt, ones, [[1, P]], 0, -1, ALU.is_gt, 0.0)
            step(pool.memset(sel9, 0.0))
            select(sel9, sel9, [[0, P]], -NS, 1, ALU.not_equal, 1.0)
            step(pool.memset(d88, 0.0))
            select(d88, d88, [[1, NS], [-1, NS]], 0, 0, ALU.not_equal, 1.0)
            step(pool.iota(m_dist, pattern=[[-P, NT], [-1, P]], base=(NT - 1) * P, channel_multiplier=1))
            step(pool.iota(l_t, pattern=[[1, P]], base=0, channel_multiplier=0))
            step(pool.iota(l_s, pattern=[[0, P]], base=0, channel_multiplier=1))
            for out, pat in ((iota_e, [[1, NE]]), (iota_s, [[1, P]]), (iota_b, [[1, MAXB]])):
                step(pool.iota(out, pattern=pat, base=0, channel_multiplier=0, allow_small_or_imprecise_dtypes=True))
            step(pool.iota(row_code, pattern=[[-P * TOPK, TILES], [-1, TOPK]], base=TOK * TOPK, channel_multiplier=-TOPK, allow_small_or_imprecise_dtypes=True))
            pool.iota(pcol, pattern=[[0, 1]], base=0, channel_multiplier=1, allow_small_or_imprecise_dtypes=True)
            pool.iota(q4, pattern=[[0, 1]], base=0, channel_multiplier=1).then_inc(sem["const_ready"], 1)

            pool.wait_ge(sem["idx_ready"], 1)
            for n in range(64):
                cache = A["cache_sb_k"] if n < 32 else A["cache_sb_v"]
                src = cache[0].rearrange("n (q r) h d -> (n q) (r h d)", q=16)
                b, c = (n % 32) // 4, n % 4
                if n < 4:
                    pool.wait_ge(sem["kvv_used"], 5 + n)
                elif n < 36:
                    pool.wait_ge(sem["kvk_used"], NS + n - 3)
                else:
                    pool.wait_ge(sem["kvv_used"], NS + n - 35)
                pool.indirect_dma_start(out=view(kvbuf[n % 4], [2048]), out_offset=None, in_=src,
                                        in_offset=bass.IndirectOffsetOnAxis(ap=idx_kv[:, b, c:c + 1], axis=0)).then_inc(sem[f"gather{n % 4}"], 16)

            for L in range(9):
                pool.wait_ge(sem["c_e"], L + 1)
                if L == 0:
                    pool.wait_ge(sem["c_kk"], 1)
                if L >= 2:
                    pool.wait_ge(sem["c_lev"], L - 1)
                if L != 7:
                    pool.tensor_tensor(ck1[L % 2], ck, cx, ALU.mult).then_inc(sem["c_k"], 1)

            pool.wait_ge(sem["r_ready"], 1)
            pool.wait_ge(sem["hro0"], 16 * 3)
            pool.wait_ge(sem["hro1"], 16 * 2)
            last = pool.value_load(be_row[0:1, MAXB:MAXB + 1], min_val=THREES_MIN - 2, max_val=MAXB // 3 - 2) + 1

            def column(dst, table, i, count):
                pool.tensor_copy(dst, table[:, bass.ds(i, 1)]).then_inc(sem["pool_chain"], 1)
                pool.wait_ge(sem["pool_chain"], count)
                pool.sem_inc(sem["x_col"], 1)

            def block_gather(p, q, count):
                i = p * 3 + q
                if not isinstance(p, int) or p > 0:
                    pool.wait_ge(sem["x_t"], i - 2)
                column(gidx[q], slot_tok, i, count)
                pool.indirect_dma_start(out=xg[q], out_offset=None, in_=h2d, bounds_check=TOK - 1, oob_is_err=False,
                                        in_offset=bass.IndirectOffsetOnAxis(ap=gidx[q], axis=0)).then_inc(sem[f"gather{q}"], 16)

            def block_scatter(p, q, count):
                i = p * 3 + q
                if not isinstance(p, int) or p > 0:
                    pool.wait_ge(sem[f"yst{q}"], p * 16)
                column(sidx[q], slot_row, i, count)
                pool.wait_ge(sem["y_a"], i + 1)
                pool.wait_ge(sem["y_v"], i + 1)
                pool.sem_inc(sem["x_col"], 1)
                pool.indirect_dma_start(out=yd, out_offset=bass.IndirectOffsetOnAxis(ap=sidx[q], axis=0), in_=ybuf[q],
                                        in_offset=None, bounds_check=TOK * TOPK - 1, oob_is_err=False).then_inc(sem[f"yst{q}"], 16)

            for q in range(3):
                step(pool.memset(xg[q], 0.0))
            n0 = step.n
            for q in range(3):
                block_gather(0, q, n0 + q + 1)

            def gather_and_scatter(p):
                for q in range(3):
                    block_gather(p, q, p * 6 + (n0 + 2 * q - 2))
                    block_scatter(p - 1, q, p * 6 + (n0 + 2 * q - 1))

            gather_and_scatter(1)
            with pool.Fori(2, last + 1) as p:
                gather_and_scatter(p)
            for q in range(3):
                block_scatter(last, q, last * 6 + (n0 + 4 + q))

        @blk.scalar
        def _(act):
            step = Chain(act, sem["act_chain"])
            fn = nc.scalar.activation

            def norm_stats(half):
                if half == 0:
                    act.wait_ge(sem["x_in"], 32)
                for t in range(TILES):
                    n = rows(t)
                    if half == 1:
                        act.wait_ge(sem["x1_ready"], TILES + t + 1)
                    step(fn(junk[0:n], xr[0:n, t, :], ACT.Square, accum_out=ssq[0:n, t:t + 1]))
                    fn(rstd[0:n, t:t + 1], ssq[0:n, t:t + 1], ACT.Sqrt, bias=eps_t[0:n], scale=1.0 / D).then_inc(sem["rstd_sqrt"], 1)

            def hT_copies(half):
                for t in range(TILES):
                    for j in range(2):
                        act.wait_ge(sem["h_ps"], 2 * (TILES * half + t) + j + 1)
                        n = rows(t)
                        src = bank[2 + j][:, 0:4 * n].rearrange("p (c n) -> p c n", n=n)
                        act.copy(hT[:, 4 * j:4 * j + 4, cols(t)], src).then_inc(sem["hT_evac"], 1)

            act.wait_ge(sem["c_in"], 32)
            fn(cs, cs, ACT.Silu).then_inc(sem["silu_c"], 1)
            act.wait_ge(sem["const_ready"], 1)
            norm_stats(0)
            hT_copies(0)

            places = [(0, 768, pqk, 0), (768, 1152, pv, 0), (1152, 1664, pqk, 768), (1664, 1920, pv, 384),
                      (1920, 2432, pqk, 1280), (2432, 3456, pv, 640)]
            for g in range(7):
                for t in range(TILES):
                    k = IN0_OUT + g * TILES + t
                    act.wait_ge(sem["dense_out"], k + 1)
                    for lo, hi, buf, at in places:
                        a, b = max(lo, g * PANEL), min(hi, (g + 1) * PANEL)
                        if a < b:
                            last = act.copy(buf[0:rows(t), t, at + a - lo:at + b - lo],
                                            bank[k % 2][0:rows(t), a - g * PANEL:b - g * PANEL])
                    last.then_inc(sem["dense_evac"], 1)
            for t in range(TILES):
                act.wait_ge(sem["qk_sum"], t + 1)
                n = rows(t)
                fn(qk_ss[0:n, t, :], qk_ss[0:n, t, :], ACT.Sqrt, bias=eps_t[0:n], scale=1.0 / HD).then_inc(sem["qk_sqrt"], 1)
            for t in range(NT):
                for j in range(4):
                    act.wait_ge(sem["t_ps"], 4 * t + j + 1)
                    w = 4 if j < 3 else 2
                    src = bank[2 + j][:, 0:P * w].rearrange("p (c n) -> p c n", n=P)
                    act.copy(tt[:, 4 * j:4 * j + w, cols(t)], src).then_inc(sem["t_evac"], 1)
            act.wait_ge(sem["t_ps"], 17)
            act.copy(tts, bank[2][:, 0:32].rearrange("p (c n) -> p c n", n=NS)).then_inc(sem["t_evac"], 1)
            act.wait_ge(sem["t_evac"], 17)
            fn(tt[:, 10:12, :], tt[:, 10:12, :], ACT.Silu)
            fn(tts[:, 0:2, :], tts[:, 0:2, :], ACT.Silu)
            step(fn(pv[:, 0:NT, 896:1152], pv[:, 0:NT, 896:1152], ACT.Silu))
            fn(pv[0:NS, NT, 896:1152], pv[0:NS, NT, 896:1152], ACT.Silu).then_inc(sem["t_act"], 1)
            step(fn(pv[:, 0:NT, 1152:1664], pv[:, 0:NT, 1152:1664], ACT.Gelu))
            fn(pv[0:NS, NT, 1152:1664], pv[0:NS, NT, 1152:1664], ACT.Gelu).then_inc(sem["d_gelu"], 1)

            NI = AH * NT
            act.wait_ge(sem["rows_out"], 16 * 8)

            def a_exp(i):
                t = i % NT
                w = (t + 1) * P
                act.wait_ge(sem["a_nm"], i + 1)
                if i >= 2:
                    act.wait_ge(sem["a_pt"], i - 1)
                fn(a_pr[i % 2][:, 0:w], a_sm[i % 2][:, 0:w], ACT.Exp, bias=nm[:, i % 2:i % 2 + 1], scale=SCALE).then_inc(sem["a_exp"], 1)

            a_exp(0)
            for i in range(NI):
                if i + 1 < NI:
                    a_exp(i + 1)
                act.wait_ge(sem["a_pt"], i + 1)
                if i >= 2:
                    act.wait_ge(sem["a_pv"], i - 1)
                w = i % NT + 1
                act.copy(a_prT[i % 2][:, 0:w, :], bank[6][:, 0:w * P].rearrange("p (c n) -> p c n", n=P)).then_inc(sem["a_ptc"], 1)

            act.wait_ge(sem["a_o"], NI)

            def b_logits(h):
                if h >= 2:
                    act.wait_ge(sem["b_pv"], h - 1)
                act.wait_ge(sem["b_z"], h + 1)
                for j, at, w, _ in JPIECE:
                    step(fn(bz[h % 2][:, at:at + w], bank[4 * (h % 2) + j][:, 0:w], ACT.Identity, bias=sbb[:, h:h + 1], scale=SCALE))
                act.sem_inc(sem["b_zs"], 1)
                step(fn(bl[h % 2], bz[h % 2], ACT.Abs))
                step(fn(bl[h % 2], bl[h % 2], ACT.Exp, scale=-1.0))
                fn(bl[h % 2], bl[h % 2], ACT.Ln, bias=ones[:, 0:1]).then_inc(sem["b_l"], 1)

            b_logits(0)
            for h in range(BH):
                if h + 1 < BH:
                    b_logits(h + 1)
                act.wait_ge(sem["b_sum"], h + 1)
                fn(bl[h % 2], blb[h % 2], ACT.Exp).then_inc(sem["b_e"], 1)
                act.wait_ge(sem["b_pv"], h + 1)
                c0 = AW + h * HD
                act.copy(orow[:, 0:NT, c0:c0 + HD], bank[3][:, 0:NT * HD].rearrange("p (t n) -> p t n", n=HD)).then_inc(sem["b_o"], 1)

            act.wait_ge(sem["s_nm"], 1)
            fn(as_p, bank[2][0:48, 0:392], ACT.Exp, bias=nm[0:48, 0:1], scale=SCALE).then_inc(sem["s_exp"], 1)
            act.wait_ge(sem["pT_ps"], 1)
            act.copy(as_pT[:, 0:3, :], bank[3][:, 0:144].rearrange("p (g n) -> p g n", n=48))
            act.copy(as_pT[0:NS, 3, :], bank[3][0:NS, 144:192]).then_inc(sem["pT_ready"], 1)

            act.wait_ge(sem["bs_z"], 1)
            step(fn(bs_l, bs_z, ACT.Abs))
            step(fn(bs_l, bs_l, ACT.Exp, scale=-1.0))
            fn(bs_l, bs_l, ACT.Ln, bias=ones[:, 0:1]).then_inc(sem["bs_l"], 1)
            act.wait_ge(sem["bs_e"], 1)
            fn(bs_l, bs_e[1], ACT.Exp).then_inc(sem["bs_ex"], 1)

            act.wait_ge(sem["bs_o"], 1)
            fz = tt[:, 12:14, :]
            fn(ck, fz, ACT.Sigmoid, scale=-1.0)
            fn(cs_k, tts[:, 2:4, :], ACT.Sigmoid, scale=-1.0)
            step(fn(cs_lf, tts[:, 2:4, :], ACT.Sigmoid))
            act.sem_inc(sem["c_kk"], 1)
            step(fn(cx, fz, ACT.Abs))
            step(fn(cx, cx, ACT.Exp, scale=-1.0))
            fn(cx, cx, ACT.Ln, bias=ones[:, 0:1]).then_inc(sem["c_lf"], 1)
            for L in range(9):
                act.wait_ge(sem["c_x"], L + 1)
                src = cb if L == 7 else cx
                step(fn(cx, src, ACT.Abs))
                fn(cx, cx, ACT.Exp, scale=-1.0).then_inc(sem["c_e"], 1)
            fn(c_tot, cb.rearrange("p c (t n) -> p c t n", n=P)[:, :, :, P - 1], ACT.Exp).then_inc(sem["c_ab"], 1)
            for j in range(2):
                act.wait_ge(sem["c_kt"], j + 1)
                act.copy(c_krow[:, 4 * j:4 * j + 4, :], bank[j][:, :].rearrange("p (c n) -> p c n", n=P)).then_inc(sem["c_ktc"], 1)
            for t in range(NT):
                act.wait_ge(sem["c_pv"], 2 * t + 1)
                for two in range(2):
                    o4 = orow[:, t, 640:896].rearrange("p (c two v) -> p c two v", two=2, v=HD)[:, :, two, :]
                    last = act.copy(o4, bank[2 + 4 * two + t % 2][:, 0:256].rearrange("p (c two v) -> p c two v", two=2, v=HD)[:, :, two, :])
                last.then_inc(sem["c_raw"], 1)
            act.wait_ge(sem["c_so"], 1)
            for two in range(2):
                o4 = orow[0:NS, NT, 640:896].rearrange("p (c two v) -> p c two v", two=2, v=HD)[:, :, two, :]
                last = act.copy(o4, bank[5 - two][0:NS, 0:256].rearrange("p (c two v) -> p c two v", two=2, v=HD)[:, :, two, :])
            last.then_inc(sem["c_raw"], 1)
            act.wait_ge(sem["c_sum"], 1)
            fn(c_ss[:, 0:NT, :], c_ss[:, 0:NT, :], ACT.Sqrt, bias=eps_t, scale=1.0 / HD)
            fn(c_ss[0:NS, NT, :], c_ss[0:NS, NT, :], ACT.Sqrt, bias=eps_t[0:NS], scale=1.0 / HD).then_inc(sem["c_sqrt"], 1)

            act.wait_ge(sem["hg_out"], 16 * 6)
            for t in range(NT):
                for j in range(3):
                    act.wait_ge(sem["oT_ps"], 3 * t + j + 1)
                    w = 4 if j < 2 else 1
                    act.copy(oT[:, 4 * j:4 * j + w, cols(t)], bank[j][:, 0:P * w].rearrange("p (c n) -> p c n", n=P)).then_inc(sem["oT_evac"], 1)
            act.wait_ge(sem["oT_ps"], 13)
            act.copy(oT[:, 5:9, SEQ:TOK], bank[3][:, 0:32].rearrange("p (c n) -> p c n", n=NS))
            act.copy(oT[:, 0:5, SEQ:TOK], os_T).then_inc(sem["oT_evac"], 1)

            for j in range(32):
                half, br, m = j // 16, j // 4 % 4, j % 4
                b = bmg_t[:, br * KC + half * 4 + m:br * KC + half * 4 + m + 1]
                act.wait_ge(sem["dense_out"], GATE_OUT + 2 * j + 1)
                if j >= 2:
                    act.wait_ge(sem["m_acc"], j - 1)
                fn(sg_m[j % 2][:, 0:SEQ], bank[j % 2][:, :], ACT.Sigmoid, bias=b)
                fn(sg_m[j % 2][:, SEQ:TOK], bank[4 + j % 2][:, 0:NS], ACT.Sigmoid, bias=b).then_inc(sem["m_sig"], 1)
            for k in range(2 * TILES):
                n = rows(k % TILES)
                act.wait_ge(sem["dense_out"], out_before[OUT0] + k + 1)
                if k >= 2:
                    act.wait_ge(sem["x1_ready"], k - 1)
                act.copy(mixs[k % 2][0:n, :], bank[k % 2][0:n, :]).then_inc(sem["mix_sb"], 1)
            act.wait_ge(sem["mod_gain"], 2)
            norm_stats(1)
            hT_copies(1)
            act.wait_ge(sem["r_log"], 1)
            fn(r_s[:, 0:NT, :], bank[0][:, 0:NT * NE].rearrange("p (t n) -> p t n", n=NE), ACT.Sigmoid)
            fn(r_s[0:NS, NT, :], bank[0][0:NS, NT * NE:TILES * NE], ACT.Sigmoid).then_inc(sem["r_sc"], 1)

            def sh_gate(t):
                act.wait_ge(sem["sh_gu"], t + 1)
                if t >= 2:
                    act.wait_ge(sem["sh_h"], t - 1)
                fn(sgate[t % 2][0:rows(t), :], bank[4 + t % 2][0:rows(t), 0:ED], ACT.Silu).then_inc(sem["sh_sg"], 1)

            sh_gate(0)
            for t in range(TILES):
                if t + 1 < TILES:
                    sh_gate(t + 1)
                n = rows(t)
                act.wait_ge(sem["sh_hT"], t + 1)
                act.copy(hmT[t % 2][:, :, 0:n], bank[6][:, 0:2 * n].rearrange("p (c n) -> p c n", n=n)).then_inc(sem["sh_hTc"], 1)
                act.wait_ge(sem["sh_y"], t + 1)
                act.copy(sh[0:n, t, 0:512], bank[2][0:n, :]).then_inc(sem["sh_row"], 1)

            act.wait_ge(sem["r_ready"], 1)
            act.wait_ge(sem["sh_rv"], TILES)
            last = act.value_load(be_row[0:1, MAXB:MAXB + 1], min_val=THREES_MIN - 2, max_val=MAXB // 3 - 2) + 1

            def gate(p, q):
                i = p * 3 + q
                act.wait_ge(sem["gu_done"], i + 1)
                if later(p):
                    act.wait_ge(sem["m_h"], i - 2)
                fn(sgate[q], bank[gu_bank[q]][:, 0:ED], ACT.Silu).then_inc(sem["m_sg"], 1)

            def rows_half(p, q):
                i = p * 3 + q
                act.wait_ge(sem["x_t"], i + 1)
                if later(p):
                    act.wait_ge(sem["gu_done"], i - 2)
                act.copy(xT[q][:, 0:4, :], bank[0][:, :].rearrange("p (c n) -> p c n", n=P)).then_inc(sem["x_ca"], 1)

            def result_half(p, q):
                i = p * 3 + q
                act.wait_ge(sem["dn_done"], i + 1)
                if later(p):
                    act.wait_ge(sem[f"yst{q}"], p * 16)
                act.copy(ybuf[q][:, 0:512], bank[5][:, :]).then_inc(sem["y_a"], 1)

            def middle(p, q):
                i = p * 3 + q
                act.wait_ge(sem["m_hT"], i + 1)
                if later(p):
                    act.wait_ge(sem["dn_done"], i - 2)
                act.copy(hmT[q], bank[4][:, 0:2 * P].rearrange("p (c n) -> p c n", n=P)).then_inc(sem["m_hTc"], 1)

            def block(p, q, front=True, back=True):
                gate(p, q)
                if front:
                    rows_half(*block_at(p, q, 1))
                if back:
                    result_half(*block_at(p, q, -1))
                middle(p, q)

            rows_half(0, 0)
            block(0, 0, back=False)
            for i in range(1, 6):
                block(i // 3, i % 3)
            with act.Fori(2, last) as p:
                for q in range(3):
                    block(p, q)
            for q in range(3):
                block(last, q, front=q < 2)
            result_half(last, 2)

        @blk.vector
        def _(dve):
            step = Chain(dve, sem["dve_chain"])
            tt_, ts_, stt = dve.tensor_tensor, dve.tensor_scalar, dve.scalar_tensor_tensor

            dve.wait_ge(sem["const_ready"], 1)
            dve.wait_ge(sem["c_in"], 32)
            step(ts_(m_c, m_dist, 0.0, None, ALU.is_ge))
            step(ts_(m_a, m_dist, float(P), None, ALU.is_le))
            for dil in (4, 16):
                step(ts_(m_bits, m_dist, dil - 1, None, ALU.bitwise_and))
                step(ts_(m_b, m_bits, 0.0, None, ALU.is_equal))
                step(tt_(m_a, m_a, m_b, ALU.add))
            step(tt_(amult, m_a, m_c, ALU.mult))
            step(ts_(aneg, amult, 0.0, -BIG, ALU.is_equal, ALU.mult))
            step(tt_(l_x, l_t, l_s, ALU.bitwise_xor))
            step(tt_(l_gt, l_t, l_s, ALU.is_gt))
            for L, H in enumerate(LEVELS):
                step(ts_(l_sh, l_x, H.bit_length() - 1, None, ALU.logical_shift_right))
                step(ts_(l_eq, l_sh, 1.0, None, ALU.is_equal))
                step(tt_(lmask[:, L, :], l_eq, l_gt, ALU.mult))
            step(ts_(lmask[:, 7, :], l_x, 0.0, None, ALU.is_equal))
            step(tt_(tri_le, tri_lt, ident, ALU.add))
            dve.wait_ge(sem["params_in"], 16 * NPARAM)
            step(ts_(q4, q4, 3, None, ALU.bitwise_and))
            step(ts_(q4, q4, 2, None, ALU.logical_shift_left))
            step(ts_(pt_sb, pt_sb, 4, None, ALU.logical_shift_left))
            step(tt_(pt_sb, pt_sb, q4.to_broadcast([P, NS]), ALU.add))
            for c in range(4):
                step(ts_(idx_kv[:, :, c], pt_sb, float(c), None, ALU.add))
            dve.sem_inc(sem["idx_ready"], 1)
            dve.wait_ge(sem["small_ps"], 1)
            dve.tensor_copy(bmg_t, bank[3][:, 0:32])
            dve.tensor_copy(sgu_bt, bank[3][:, 32:36])
            for g in range(DG):
                last = tt_(sgu_wt[:, g, :], bank[4][:, g * P:(g + 1) * P], tri_le, ALU.mult)
            last.then_inc(sem["small_ready"], 1)
            dve.wait_ge(sem["cT_ps"], 1)
            dve.tensor_copy(cT, bank[2][:, 0:72].rearrange("p (c n) -> p c n", n=9)).then_inc(sem["cT_ready"], 1)

            def modulation(half):
                base = out_before[0 if half == 0 else ADA2]
                for g in range(6):
                    dve.wait_ge(sem["dense_out"], base + g + 1)
                    if g == 0:
                        dve.wait_ge(sem["bada_in"], 32 * (half + 1))
                    s, c = g // 2, g % 2 * PANEL
                    tt_(mod_sb[0:9, s, c:c + PANEL], bank[(base + g) % 2][0:9, :], bada[:, s, c:c + PANEL], ALU.add).then_inc(sem["dense_evac"], 1)
                dve.wait_ge(sem["dense_evac"], 6 if half == 0 else 6 + 7 * TILES + 6)
                stt(out=mod_sb[0:9, 1, :], in0=mod_sb[0:9, 1, :], scalar=1.0, in1=g9, op0=ALU.add, op1=ALU.mult).then_inc(sem["mod_gain"], 1)

            def norm_rows(half):
                base = half * TILES
                for t in range(TILES):
                    n = rows(t)
                    dve.wait_ge(sem["rstd_sqrt"], base + t + 1)
                    step(dve.reciprocal(rstd[0:n, t:t + 1], rstd[0:n, t:t + 1]))
                    if t == 0:
                        dve.wait_ge(sem["bc_ps"], half + 1)
                        dve.wait_ge(sem["mod_gain"], half + 1)
                    if t >= 2:
                        dve.wait_ge(sem["h_ps"], 2 * (base + t - 1))
                        if half == 1:
                            dve.wait_ge(sem[f"hro{t % 2}"], 16 * (t // 2))
                    h = hrow[t % 2]
                    for c in range(2):
                        cc = slice(c * 512, c * 512 + 512)
                        gain = bank[4 + c][:, :] if t < NT else mod_sb[0:NS, 1, cc]
                        shift = bank[6 + c][:, :] if t < NT else mod_sb[0:NS, 0, cc]
                        step(stt(out=h[0:n, cc], in0=xr[0:n, t, cc], scalar=rstd[0:n, t:t + 1], in1=gain, op0=ALU.mult, op1=ALU.mult))
                        last = tt_(h[0:n, cc], h[0:n, cc], shift, ALU.add)
                        if c == 0:
                            step(last)
                    last.then_inc(sem["h_row"], 1)

            modulation(0)
            norm_rows(0)

            dve.wait_ge(sem["h_ps"], 2 * TILES)
            for t in range(TILES):
                n = rows(t)
                qk = pqk[0:n, t, 0:768]
                qk3 = qk.rearrange("p (h d) -> p h d", d=HD)
                dve.wait_ge(sem["dense_evac"], 6 + TILES + t + 1)
                if t:
                    dve.wait_ge(sem["qk_sum"], t)
                step(tt_(qk_sq[0:n], qk, qk, ALU.mult))
                dve.tensor_reduce(qk_ss[0:n, t, :], qk_sq[0:n].rearrange("p (h d) -> p h d", d=HD), AX, ALU.add).then_inc(sem["qk_sum"], 1)
            for t in range(TILES):
                n = rows(t)
                qk3 = pqk[0:n, t, 0:768].rearrange("p (h d) -> p h d", d=HD)
                dve.wait_ge(sem["qk_sqrt"], t + 1)
                step(dve.reciprocal(qk_ss[0:n, t, :], qk_ss[0:n, t, :]))
                step(tt_(qk3, qk3, qk_ss[0:n, t, :].unsqueeze(2).to_broadcast([n, 12, HD]), ALU.mult))
                for k in range(2):
                    part = qk3[:, AH * k:AH * k + AH, :]
                    last = tt_(part, part, qk_g[0:n, k:k + 1, :].to_broadcast([n, AH, HD]), ALU.mult)
                last.then_inc(sem["qk_norm"], 1)
            dve.wait_ge(sem["qk_norm"], TILES)
            dve.tensor_copy(rows_s[0:NS, :], pqk[0:NS, NT, 0:1024]).then_inc(sem["rows_saved"], 1)

            dve.wait_ge(sem["rows_out"], 16 * 8)
            dve.wait_ge(sem["t_ps"], 17)
            NI = AH * NT

            def a_front(i):
                t = i % NT
                w = (t + 1) * P
                b = i % 2
                dve.wait_ge(sem["a_s"], i + 1)
                if i >= 2:
                    dve.wait_ge(sem["a_exp"], i - 1)
                neg = aneg.rearrange("p a j -> p (a j)")[:, SEQ - w:SEQ]
                step(tt_(a_sm[b][:, 0:w], bank[4 + b][:, 0:w], neg, ALU.add))
                step(dve.tensor_reduce(nm[:, b:b + 1], a_sm[b][:, 0:w], AX, ALU.max))
                ts_(nm[:, b:b + 1], nm[:, b:b + 1], -SCALE, None, ALU.mult).then_inc(sem["a_nm"], 1)

            def a_out(i):
                b = i % 2
                c0 = i // NT * HD
                dve.wait_ge(sem["a_pv"], i + 1)
                ts_(orow[:, i % NT, c0:c0 + HD], bank[7 - 4 * b][:, 0:HD], den[:, b:b + 1], None, ALU.mult).then_inc(sem["a_o"], 1)

            a_front(0)
            for i in range(NI):
                if i + 1 < NI:
                    a_front(i + 1)
                if i >= 2:
                    dve.wait_ge(sem["a_o"], i - 1)
                b, w = i % 2, (i % NT + 1) * P
                mult = amult.rearrange("p a j -> p (a j)")[:, SEQ - w:SEQ]
                dve.wait_ge(sem["a_exp"], i + 1)
                step(stt(out=a_pr[b][:, 0:w], in0=a_pr[b][:, 0:w], scalar=1.0, in1=mult, op0=ALU.mult, op1=ALU.mult, accum_out=den[:, b:b + 1]))
                dve.reciprocal(den[:, b:b + 1], den[:, b:b + 1]).then_inc(sem["a_p"], 1)
                if i >= 1:
                    a_out(i - 1)
            a_out(NI - 1)

            def b_front(h):
                s = h % 2
                dve.wait_ge(sem["b_l"], h + 1)
                step(stt(out=blb[s], in0=bz[s], scalar=0.0, in1=bl[s], op0=ALU.min, op1=ALU.subtract))
                step(tt_(bz[s], blb[s], bz[s], ALU.subtract))
                for j in range(NT):
                    last = tt_(bz[s][:, JO[j]:JO[j] + P], bz[s][:, JO[j]:JO[j] + P], tri_lt, ALU.mult)
                last.then_inc(sem["b_lk"], 1)

            def b_back(h):
                s = h % 2
                dve.wait_ge(sem["b_after"], h + 1)
                for j, at, w, _ in JPIECE:
                    last = tt_(blb[s][:, at:at + w], blb[s][:, at:at + w], bank[4 * s + j][:, 0:w], ALU.add)
                last.then_inc(sem["b_sum"], 1)
                dve.wait_ge(sem["b_e"], h + 1)
                for j in range(NT):
                    last = tt_(bl[s][:, JO[j]:JO[j] + P], bl[s][:, JO[j]:JO[j] + P], tri_lt, ALU.mult)
                last.then_inc(sem["b_a"], 1)

            b_front(0)
            for h in range(BH):
                if h + 1 < BH:
                    b_front(h + 1)
                b_back(h)

            d8 = ident[0:NS, 0:NS]
            dve.wait_ge(sem["b_o"], BH)
            tt_(as_qd, rows_s[0:NS, 0:AW].unsqueeze(1).to_broadcast([NS, NS, AW]), d8.unsqueeze(2).to_broadcast([NS, NS, AW]), ALU.mult).then_inc(sem["qd_ready"], 1)
            step(tt_(bs_prod[0:NS, 0:AW // 256 + 1, :].rearrange("p a b -> p (a b)")[:, 0:AW], rows_s[0:NS, 0:AW], rows_s[0:NS, AW:2 * AW], ALU.mult))
            step(dve.tensor_reduce(as_tmp, bs_prod[0:NS, 0:2, :].rearrange("p a b -> p (a b)")[:, 0:AW].rearrange("p (h d) -> p h d", d=HD), AX, ALU.add))
            step(ts_(as_self, d8.unsqueeze(2).to_broadcast([NS, NS, AH]), BIG, -BIG, ALU.mult, ALU.add))
            step(tt_(as_self, as_self, as_tmp.unsqueeze(1).to_broadcast([NS, NS, AH]), ALU.add))
            for b in range(NS):
                dve.wait_ge(sem["qb_ps"], b + 1)
                dve.wait_ge(sem[f"kv{b % 4}"], 48 * (b // 4 + 1))
                tt_(as_prod, view(kvbuf[b % 4], [3, AW]), bank[b % 2][:, 0:AW].unsqueeze(1).to_broadcast([P, 3, AW]), ALU.mult).then_inc(sem["kvk_used"], 1)
                dve.wait_ge(sem["kvk_used"], b + 1)
                step(dve.tensor_reduce(as_s[:, :, b * AH:(b + 1) * AH], as_prod.rearrange("p g (h d) -> p g h d", d=HD), AX, ALU.add))
            dve.sem_inc(sem["as_used"], 1)
            dve.wait_ge(sem["sT_ps"], 1)
            step(dve.tensor_reduce(nm[0:48, 0:1], bank[2][0:48, 0:392], AX, ALU.max))
            ts_(nm[0:48, 0:1], nm[0:48, 0:1], -SCALE, None, ALU.mult).then_inc(sem["s_nm"], 1)
            dve.wait_ge(sem["s_exp"], 1)
            step(ts_(as_p[:, 384:392], as_p[:, 384:392], float(GROUPS_A), None, ALU.mult))
            step(dve.tensor_reduce(den[0:48, 0:1], as_p, AX, ALU.add))
            step(dve.reciprocal(den[0:48, 0:1], den[0:48, 0:1]))
            ts_(as_p, as_p, den[0:48, 0:1], None, ALU.mult).then_inc(sem["s_norm"], 1)

            tt_(bs_qd, rows_s[0:NS, 768:1024].unsqueeze(1).to_broadcast([NS, NS, BW]), d8.unsqueeze(2).to_broadcast([NS, NS, BW]), ALU.mult).then_inc(sem["bs_qd"], 1)
            for n in range(32):
                b, c = n // 4, n % 4
                if c == 0:
                    dve.wait_ge(sem["qb_ps"], NS + b + 1)
                dve.wait_ge(sem[f"gather{n % 4}"], 16 * (n // 4 + 1))
                q = bank[4 + b % 2][:, 0:BW].unsqueeze(1).to_broadcast([P, 8, BW])
                tt_(bs_prod, view(kvbuf[n % 4], [8, BW]), q, ALU.mult).then_inc(sem["kvk_used"], 1)
                dve.wait_ge(sem["kvk_used"], NS + n + 1)
                step(dve.tensor_reduce(bs_z[:, b, 8 * c:8 * c + 8, :], bs_prod.rearrange("p r (h d) -> p r h d", d=HD), AX, ALU.add))
            flat = lambda v: v.rearrange("p b r h -> p (b r) h")
            stt(out=flat(bs_z), in0=flat(bs_z), scalar=SCALE, in1=sbb.unsqueeze(1).to_broadcast([P, NS * 32, BH]), op0=ALU.mult, op1=ALU.add).then_inc(sem["bs_z"], 1)
            dve.wait_ge(sem["as_pv"], 1)
            for j in range(2):
                last = dve.tensor_copy(os_T[j * HD:j * HD + HD, 0:3, :].rearrange("p c b -> p b c"),
                                       bank[7][j * HD:j * HD + HD, 0:48].rearrange("p (b c two) -> p b c two", c=3, two=2)[:, :, :, j])
            last.then_inc(sem["as_o"], 1)
            dve.wait_ge(sem["bs_l"], 1)
            one = lambda v: v.rearrange("p b r h -> p (b r h)")
            step(stt(out=one(bs_lb), in0=one(bs_z), scalar=0.0, in1=one(bs_l), op0=ALU.min, op1=ALU.subtract))
            step(tt_(one(bs_z), one(bs_lb), one(bs_z), ALU.subtract))
            dve.memset(bs_e[0][:, :, 31:32, :], 0.0)
            step(dve.tensor_copy(bs_e[0][:, :, 0:31, :], bs_z[:, :, 1:32, :]))
            for k, s in enumerate((1, 2, 4, 8, 16)):
                a, b = bs_e[k % 2], bs_e[(k + 1) % 2]
                dve.tensor_copy(b[:, :, 32 - s:32, :], a[:, :, 32 - s:32, :])
                step(tt_(b[:, :, 0:32 - s, :], a[:, :, 0:32 - s, :], a[:, :, s:32, :], ALU.add))
            tt_(bs_tot, bs_e[1][:, :, 0, :], bs_z[:, :, 0, :], ALU.add).then_inc(sem["bs_tot"], 1)
            dve.wait_ge(sem["bs_tot"], 1)
            step(tt_(one(bs_e[1]), one(bs_e[1]), one(bs_lb), ALU.add))
            dve.wait_ge(sem["bs_cross"], 1)
            cross = bank[6][:, 0:32].rearrange("p (b h) -> p b h", h=BH).unsqueeze(2).to_broadcast([P, NS, 32, BH])
            tt_(bs_e[1], bs_e[1], cross, ALU.add).then_inc(sem["bs_e"], 1)
            dve.wait_ge(sem["bs_pv"], 1)
            for hp in range(2):
                for j in range(2):
                    last = dve.tensor_copy(os_T[j * HD:j * HD + HD, 3 + hp, :],
                                           bank[hp][j * HD:j * HD + HD, 0:2 * NS].rearrange("p (b two) -> p b two", two=2)[:, :, j])
            last.then_inc(sem["bs_o"], 1)

            fz = tt[:, 12:14, :]
            dve.wait_ge(sem["c_lf"], 1)
            step(stt(out=fz, in0=fz, scalar=0.0, in1=cx, op0=ALU.min, op1=ALU.subtract))
            for c in range(2):
                for t in range(NT):
                    step(dve.tensor_tensor_scan(out=cb[:, c, cols(t)], data0=ones, data1=fz[:, c, cols(t)], initial=0.0, op0=ALU.mult, op1=ALU.add))
            flatc = lambda v: v.rearrange("p c n -> p (c n)")
            qz = tt[:, 10:12, :]
            step(dve.memset(c_att, 0.0))

            def c_decay(L):
                if L == 7:
                    dve.sem_inc(sem["c_x"], 1)
                    return
                H = LEVELS[L] if L < 7 else P
                b2 = 2 * H if L < 7 else P
                blocks = flatc(cb).rearrange("p (m w) -> p m w", w=b2)
                ref = blocks[:, :, H - 1:H].to_broadcast([P, 2 * SEQ // b2, b2])
                tt_(flatc(cx).rearrange("p (m w) -> p m w", w=b2), blocks, ref, ALU.subtract).then_inc(sem["c_x"], 1)

            def c_copies(L):
                dve.wait_ge(sem["c_lev"], L + 1)
                if L:
                    dve.wait_ge(sem["c_cp"], 4 * L)
                for h in range(CH):
                    dve.copy_predicated(c_att[:, h, :, :], lmask[:, L:L + 1, :].to_broadcast([P, NT, P]),
                                        bank[4 * (L % 2) + h][:, :].rearrange("p (t n) -> p t n", n=P)).then_inc(sem["c_cp"], 1)

            for L in range(9):
                if L >= 1:
                    dve.wait_ge(sem["c_q"], min(L, 8))
                    dve.wait_ge(sem["c_k"], min(L, 7))
                c_decay(L)
                if L < 8:
                    dve.wait_ge(sem["c_e"], L + 1)
                    if L >= 2:
                        dve.wait_ge(sem["c_lev"], L - 1)
                    tt_(cq1[L % 2], qz, cx, ALU.mult).then_inc(sem["c_q"], 1)
                if 1 <= L:
                    c_copies(L - 1)
            dve.wait_ge(sem["c_ab"], 1)
            for t in range(NT):
                dve.wait_ge(sem["c_pv"], 2 * t + 2)
                for hp in range(2):
                    u = bank[4 + t % 2][:, hp * HD:(hp + 1) * HD]
                    if t == 0:
                        last = dve.tensor_copy(c_S[:, hp, :], u)
                    else:
                        last = stt(out=c_S[:, hp, :], in0=c_S[:, hp, :], scalar=c_tot[:, hp, t:t + 1], in1=u, op0=ALU.mult, op1=ALU.add)
                last.then_inc(sem["c_s"], 1)
                dve.wait_ge(sem["c_s"], t + 1)
            dve.wait_ge(sem["s0_in"], 32)
            vc = pv[0:NS, NT, 640:896].rearrange("p (h v) -> p h v", v=HD)
            step(tt_(c_qd, tts[:, 0:2, :].unsqueeze(2).to_broadcast([P, 2, NS, NS]), d88.unsqueeze(1).to_broadcast([P, 2, NS, NS]), ALU.mult))
            for hp in range(2):
                if hp:
                    dve.wait_ge(sem["c_vb"], 1)
                for two in range(2):
                    last = tt_(c_vdiag[:, two, :, :], vc[:, 2 * hp + two:2 * hp + two + 1, :].to_broadcast([NS, NS, HD]), d8.unsqueeze(2).to_broadcast([NS, NS, HD]), ALU.mult)
                last.then_inc(sem["c_vd"], 1)
                step(tt_(c_new[:, :, hp, :], c_S0[:, :, hp, :], cs_lf[:, hp, :].unsqueeze(2).to_broadcast([P, NS, HD]), ALU.mult))
                dve.wait_ge(sem["c_vb"], hp + 1)
                vb = bank[6 + hp][:, :].rearrange("p (b v) -> p b v", v=HD)
                step(tt_(cs_tmp, vb, cs_k[:, hp, :].unsqueeze(2).to_broadcast([P, NS, HD]), ALU.mult))
                tt_(c_new[:, :, hp, :], c_new[:, :, hp, :], cs_tmp, ALU.add).then_inc(sem["c_new"], 1)
                dve.wait_ge(sem["c_new"], hp + 1)
            for t in range(TILES):
                n = rows(t)
                dve.wait_ge(sem["c_raw"], t + 1)
                o3 = orow[0:n, t, 640:896].rearrange("p (h v) -> p h v", v=HD)
                step(tt_(c_sq[0:n], o3, o3, ALU.mult))
                last = dve.tensor_reduce(c_ss[0:n, t, :], c_sq[0:n], AX, ALU.add)
                if t < TILES - 1:
                    step(last)
            last.then_inc(sem["c_sum"], 1)
            dve.wait_ge(sem["c_sqrt"], 1)
            for t in range(TILES):
                n = rows(t)
                o3 = orow[0:n, t, 640:896].rearrange("p (h v) -> p h v", v=HD)
                step(dve.reciprocal(c_ss[0:n, t, :], c_ss[0:n, t, :]))
                step(tt_(o3, o3, c_ss[0:n, t, :].unsqueeze(2).to_broadcast([n, CH, HD]), ALU.mult))
                step(tt_(o3, o3, co_g[0:n].unsqueeze(1).to_broadcast([n, CH, HD]), ALU.mult))
                step(tt_(orow[0:n, t, 640:896], orow[0:n, t, 640:896], pv[0:n, t, 896:1152], ALU.mult))
            dve.wait_ge(sem["d_gelu"], 1)
            od = orow[0:NS, NT, 896:1152].rearrange("p (g v) -> p g v", v=HD)
            vd = pv[0:NS, NT, 1408:1664].rearrange("p (g v) -> p g v", v=HD)
            step(tt_(od, vd, w00[0:NS].unsqueeze(2).to_broadcast([NS, DG, HD]), ALU.mult))
            step(tt_(od, od, b00[0:NS].unsqueeze(2).to_broadcast([NS, DG, HD]), ALU.add))
            step(tt_(orow[0:NS, NT, 896:1152], orow[0:NS, NT, 896:1152], pv[0:NS, NT, 1152:1408], ALU.mult))
            dve.wait_ge(sem["d_mix"], 1)
            for g in range(DG):
                mixed = bank[6 + g // 2][:, 256 * (g % 2):256 * (g % 2) + 256].rearrange("p (t v) -> p t v", v=HD)
                last = stt(out=orow[:, 0:NT, 896 + g * HD:960 + g * HD], in0=mixed, scalar=sgu_bt[:, g:g + 1],
                           in1=pv[:, 0:NT, 1152 + g * HD:1216 + g * HD], op0=ALU.add, op1=ALU.mult)
            last.then_inc(sem["d_o"], 1)

            for j in range(32):
                half, br, m = j // 16, j // 4 % 4, j % 4
                dve.wait_ge(sem["m_sig"], j + 1)
                dve.wait_ge(sem["dense_out"], GATE_OUT + 2 * j + 2)
                out = mT[:, half * 4 + m, :] if br == 0 else tmp_m
                tt_(out[:, 0:SEQ], sg_m[j % 2][:, 0:SEQ], bank[2 + j % 2][:, :], ALU.mult)
                last = tt_(out[:, SEQ:TOK], sg_m[j % 2][:, SEQ:TOK], bank[6 + j % 2][:, 0:NS], ALU.mult)
                if br:
                    step(last)
                    last = tt_(mT[:, half * 4 + m, :], mT[:, half * 4 + m, :], tmp_m, ALU.add)
                last.then_inc(sem["m_acc"], 1)
                dve.wait_ge(sem["m_acc"], j + 1)
            dve.wait_ge(sem["x2_in"], 32)
            dve.wait_ge(sem["g_ps"], 1)
            for k in range(2 * TILES):
                c, t = k // TILES, k % TILES
                n, cc = rows(t), slice(c * 512, c * 512 + 512)
                dve.wait_ge(sem["mix_sb"], k + 1)
                g = bank[6 + c][:, :] if t < NT else mod_sb[0:NS, 2, cc]
                step(tt_(mixt[0:n], mixs[k % 2][0:n], g, ALU.mult))
                tt_(xr[0:n, t, cc], xr[0:n, t, cc], mixt[0:n], ALU.add).then_inc(sem["x1_ready"], 1)
                dve.wait_ge(sem["x1_ready"], k + 1)
            modulation(1)
            norm_rows(1)

            dve.wait_ge(sem["r_sc"], 1)
            step(dve.memset(r_M[:, NT, :], 0.0))
            for t in range(TILES):
                n = rows(t)
                c3 = r_c[0:n, t, :].rearrange("p (g e) -> p g e", e=NE // EG)
                step(tt_(r_c[0:n, t, :], r_s[0:n, t, :], brt[0:n], ALU.add))
                for g in range(EG):
                    last = dve.max(r_m8[0:n, g, :], c3[:, g, :])
                step(last)
                step(tt_(r_g[0:n], r_m8[0:n, :, 0], r_m8[0:n, :, 1], ALU.add))
                step(dve.max(r_g8[0:n], r_g[0:n]))
                step(dve.max_index(r_gi[0:n], r_g8[0:n], r_g[0:n]))
                step(dve.tensor_copy(r_gf[0:n], r_gi[0:n]))
                step(tt_(r_eq[0:n], iota_e[0:n, 0:EG].unsqueeze(2).to_broadcast([n, EG, TOPG]), r_gf[0:n, 0:TOPG].unsqueeze(1).to_broadcast([n, EG, TOPG]), ALU.is_equal))
                step(dve.tensor_reduce(r_gm[0:n], r_eq[0:n], AX, ALU.max))
                step(ts_(r_gm[0:n], r_gm[0:n], BIG, -BIG, ALU.mult, ALU.add))
                mc3 = r_mc[0:n].rearrange("p (g e) -> p g e", e=NE // EG)
                step(tt_(mc3, c3, r_gm[0:n].unsqueeze(2).to_broadcast([n, EG, NE // EG]), ALU.add))
                step(dve.max(r_t8[0:n], r_mc[0:n]))
                step(dve.max_index(r_ti[0:n], r_t8[0:n], r_mc[0:n]))
                step(dve.tensor_copy(r_tf[0:n], r_ti[0:n]))
                oh = onehot[0:n, t, :, :]
                step(tt_(oh, iota_e[0:n].unsqueeze(1).to_broadcast([n, TOPK, NE]), r_tf[0:n].unsqueeze(2).to_broadcast([n, TOPK, NE]), ALU.is_equal))
                step(tt_(r_prod[0:n], oh, r_s[0:n, t, :].unsqueeze(1).to_broadcast([n, TOPK, NE]), ALU.mult))
                step(dve.tensor_reduce(gates[0:n, t, :], r_prod[0:n], AX, ALU.add))
                step(dve.tensor_reduce(r_sum[0:n], gates[0:n, t, :], AX, ALU.add))
                step(dve.reciprocal(r_sum[0:n], r_sum[0:n]))
                step(ts_(gates[0:n, t, :], gates[0:n, t, :], r_sum[0:n], ROUTE_SCALE, ALU.mult, ALU.mult))
                dve.tensor_reduce(r_M[0:n, t, :], oh.rearrange("p k e -> p e k"), AX, ALU.add).then_inc(sem["r_mask"], 1)
            dve.wait_ge(sem["r_pos"], 1)
            step(ts_(r_cnt, bank[1][:, 320:384], float(P - 1), None, ALU.add))
            step(dve.tensor_copy(r_cnti, r_cnt))
            step(ts_(r_cnti, r_cnti, 7, None, ALU.logical_shift_right))
            step(dve.tensor_copy(r_nb, r_cnti))
            step(dve.tensor_tensor_scan(out=r_end, data0=ones[:, 0:NE], data1=r_nb, initial=0.0, op0=ALU.mult, op1=ALU.add))
            step(tt_(r_st, r_end, r_nb, ALU.subtract))
            step(ts_(r_st, r_st, float(P), None, ALU.mult))
            step(ts_(r_mc, r_end, pcol, None, ALU.is_le))
            step(dve.tensor_reduce(r_be, r_mc, AX, ALU.add))
            step(ts_(r_be, r_be, float(NE - 1), None, ALU.min))
            for t in range(TILES):
                n = rows(t)
                oh = onehot[0:n, t, :, :]
                step(tt_(r_mc[0:n], bank[1][0:n, t * NE:(t + 1) * NE], r_st[0:n], ALU.add))
                step(tt_(r_prod[0:n], oh, r_mc[0:n].unsqueeze(1).to_broadcast([n, TOPK, NE]), ALU.mult))
                step(dve.tensor_reduce(r_d[0:n], r_prod[0:n], AX, ALU.add))
                step(dve.tensor_copy(dest_i[0:n, t, :], r_d[0:n]))
                step(ts_(r_dv[0:n], dest_i[0:n, t, :], P - 1, None, ALU.bitwise_and))
                step(dve.tensor_copy(r_f8[0:n], r_dv[0:n]))
                if t:
                    dve.wait_ge(sem["r_tab"], t)
                step(tt_(r_hs[0:n], iota_s[0:n].unsqueeze(1).to_broadcast([n, TOPK, P]), r_f8[0:n].unsqueeze(2).to_broadcast([n, TOPK, P]), ALU.is_equal))
                step(ts_(r_dv[0:n], dest_i[0:n, t, :], 7, None, ALU.logical_shift_right))
                step(dve.tensor_copy(r_f8[0:n], r_dv[0:n]))
                step(tt_(r_hb[0:n], iota_b[0:n].unsqueeze(1).to_broadcast([n, TOPK, MAXB]), r_f8[0:n].unsqueeze(2).to_broadcast([n, TOPK, MAXB]), ALU.is_equal))
                tt_(r_hb[0:n], r_hb[0:n], row_code[0:n, t, :].unsqueeze(2).to_broadcast([n, TOPK, MAXB]), ALU.mult).then_inc(sem["r_tab_in"], 1)
                dve.wait_ge(sem["r_tab_in"], t + 1)
            dve.wait_ge(sem["r_tab"], TILES + 1)
            step(ts_(slot_row, bank[7][:, 0:MAXB], -1.0, float(TOK * TOPK), ALU.mult, ALU.add))
            step(ts_(slot_tok, slot_row, 3, None, ALU.logical_shift_right))
            step(dve.tensor_copy(be_row[:, 0:MAXB], bank[7][0:1, P:P + MAXB]))
            step(ts_(r_sum[0:1], r_end[0:1, NE - 1:NE], 2.0, 43.0, ALU.add, ALU.mult))
            step(dve.tensor_copy(be_row[:, MAXB:MAXB + 1], r_sum[0:1]))
            step(ts_(be_row[:, MAXB:MAXB + 1], be_row[:, MAXB:MAXB + 1], 7, None, ALU.logical_shift_right))
            ts_(be_row[:, MAXB:MAXB + 1], be_row[:, MAXB:MAXB + 1], -2.0, None, ALU.add).then_inc(sem["r_ready"], 1)

            def sh_mid(t):
                n = rows(t)
                dve.wait_ge(sem["sh_sg"], t + 1)
                if t >= 2:
                    dve.wait_ge(sem["sh_hT"], t - 1)
                tt_(hmid[t % 2][0:n], sgate[t % 2][0:n], bank[4 + t % 2][0:n, ED:2 * ED], ALU.mult).then_inc(sem["sh_h"], 1)

            sh_mid(0)
            for t in range(TILES):
                if t + 1 < TILES:
                    sh_mid(t + 1)
                dve.wait_ge(sem["sh_y"], t + 1)
                dve.tensor_copy(sh[0:rows(t), t, 512:1024], bank[3][0:rows(t), :]).then_inc(sem["sh_rv"], 1)

            dve.wait_ge(sem["r_ready"], 1)
            dve.wait_ge(sem["sh_row"], TILES)
            last = dve.value_load(be_row[0:1, MAXB:MAXB + 1], min_val=THREES_MIN - 2, max_val=MAXB // 3 - 2) + 1

            def middle(p, q):
                i = p * 3 + q
                dve.wait_ge(sem["m_sg"], i + 1)
                if later(p):
                    dve.wait_ge(sem["m_hT"], i - 2)
                tt_(hmid[q], sgate[q], bank[gu_bank[q]][:, ED:2 * ED], ALU.mult).then_inc(sem["m_h"], 1)

            def rows_half(p, q):
                i = p * 3 + q
                dve.wait_ge(sem["x_t"], i + 1)
                if later(p):
                    dve.wait_ge(sem["gu_done"], i - 2)
                dve.tensor_copy(xT[q][:, 4:8, :], bank[1][:, :].rearrange("p (c n) -> p c n", n=P)).then_inc(sem["x_cv"], 1)

            def result_half(p, q):
                i = p * 3 + q
                dve.wait_ge(sem["dn_done"], i + 1)
                if later(p):
                    dve.wait_ge(sem[f"yst{q}"], p * 16)
                dve.tensor_copy(ybuf[q][:, 512:1024], bank[6][:, :]).then_inc(sem["y_v"], 1)

            def block(p, q, front=True, back=True):
                middle(p, q)
                if front:
                    rows_half(*block_at(p, q, 1))
                if back:
                    result_half(*block_at(p, q, -1))

            rows_half(0, 0)
            block(0, 0, back=False)
            for i in range(1, 6):
                block(i // 3, i % 3)
            with dve.Fori(2, last) as p:
                for q in range(3):
                    block(p, q)
            for q in range(3):
                block(last, q, front=q < 2)
            result_half(last, 2)

            dve.wait_ge(sem["g_ps"], 2)
            for n in range(TILES * TOPK):
                t, k = n // TOPK, n % TOPK
                m = rows(t)
                dve.wait_ge(sem[f"kv{n % 4}"], 192 + 16 * (n // 4 + 1))
                stt(out=sh[0:m, t, :], in0=fbuf[n % 4][0:m, :], scalar=gates[0:m, t, k:k + 1], in1=sh[0:m, t, :], op0=ALU.mult, op1=ALU.add).then_inc(sem["f_used"], 1)
                dve.wait_ge(sem["f_used"], n + 1)
                if k == TOPK - 1:
                    for c in range(2):
                        cc = slice(c * 512, c * 512 + 512)
                        g = bank[c][:, :] if t < NT else mod_sb[0:NS, 2, cc]
                        step(tt_(sh[0:m, t, cc], sh[0:m, t, cc], g, ALU.mult))
                    tt_(xr[0:m, t, :], xr[0:m, t, :], sh[0:m, t, :], ALU.add).then_inc(sem["f_acc"], 1)

        @blk.tensor
        def _(pe):
            mm, tr = pe.matmul, pe.transpose

            def panel_wait(i, n=1):
                pe.wait_ge(sem[f"w_in{i % 2}"], 16 * (i // 2 + n))

            pe.wait_ge(sem["const_ready"], 1)
            pe.wait_ge(sem["silu_c"], 1)
            for c in range(KC):
                last = tr(bank[2][:, c * 9:(c + 1) * 9], cs[:, c * P:(c + 1) * P], ident[0:9, 0:9])
            last.then_inc(sem["cT_ps"], 1)
            pe.wait_ge(sem["params_in"], 16 * NPARAM)
            tr(bank[3][:, 0:32], bmg_r, ident[0:32, 0:32])
            tr(bank[3][:, 32:36], sgub_r, ident[0:4, 0:4])
            for g in range(DG):
                last = tr(bank[4][:, g * P:(g + 1) * P], sguw_r[:, g, :], ident)
            last.then_inc(sem["small_ps"], 1)
            pe.wait_ge(sem["cT_ready"], 1)

            def modulation(half):
                first = 0 if half == 0 else ADA2
                for g in range(6):
                    i = first + g
                    k = out_before[i]
                    panel_wait(i)
                    if half == 1 and g < 2:
                        pe.wait_ge(sem["mix_sb"], 2 * TILES)
                    if g >= 2:
                        pe.wait_ge(sem["dense_evac"], (0 if half == 0 else 6 + 7 * TILES) + g - 1)
                    for c in range(KC):
                        last = mm(bank[k % 2][0:9, :], cT[:, c, :], panel[i % 2][:, c, :], start=(c == 0), stop=(c == KC - 1))
                    last.then_inc(sem["dense_out"], 1)
                pe.wait_ge(sem["mod_gain"], half + 1)
                if half == 0:
                    pe.wait_ge(sem["small_ready"], 1)
                else:
                    pe.wait_ge(sem["x1_ready"], 2 * TILES)
                for s, b in ((1, 4), (0, 6)):
                    for c in range(2):
                        last = mm(bank[b + c][:, :], sel9[0:9, :], mod_sb[0:9, s, c * 512:c * 512 + 512], start=True, stop=True)
                last.then_inc(sem["bc_ps"], 1)

            def transposed_rows(half):
                for t in range(TILES):
                    n = rows(t)
                    pe.wait_ge(sem["h_row"], half * TILES + t + 1)
                    for j in range(2):
                        if t or half:
                            pe.wait_ge(sem["hT_evac"], 2 * (half * TILES + t - 1) + j + 1)
                        for c in range(4):
                            d = (4 * j + c) * P
                            last = tr(bank[2 + j][:, c * n:(c + 1) * n], hrow[t % 2][0:n, d:d + P], ident[0:n, 0:n])
                        last.then_inc(sem["h_ps"], 1)

            modulation(0)
            transposed_rows(0)

            pe.wait_ge(sem["hT_evac"], 2 * TILES)
            for g in range(7):
                w = min(PANEL, IN_W - g * PANEL)
                panel_wait(IN0 + g)
                for t in range(TILES):
                    k = IN0_OUT + g * TILES + t
                    if k - IN0_OUT >= 2:
                        pe.wait_ge(sem["dense_evac"], k - 1)
                    for c in range(KC):
                        last = mm(bank[k % 2][0:rows(t), 0:w], hT[:, c, cols(t)], panel[(IN0 + g) % 2][:, c, 0:w], start=(c == 0), stop=(c == KC - 1))
                    last.then_inc(sem["dense_out"], 1)
            for t in range(NT):
                pe.wait_ge(sem["qk_norm"], t + 1)
                if t == 0:
                    pe.wait_ge(sem["dense_evac"], 6 + 7 * TILES)
                for j in range(4):
                    if t:
                        pe.wait_ge(sem["t_evac"], 4 * (t - 1) + j + 1)
                    for c in range(4 if j < 3 else 2):
                        last = tr(bank[2 + j][:, c * P:(c + 1) * P], pqk[:, t, (4 * j + c) * P:(4 * j + c + 1) * P], ident)
                    last.then_inc(sem["t_ps"], 1)
            pe.wait_ge(sem["t_evac"], 13)
            for c in range(4):
                last = tr(bank[2][:, c * NS:(c + 1) * NS], pqk[0:NS, NT, 1280 + c * P:1280 + (c + 1) * P], ident[0:NS, 0:NS])
            last.then_inc(sem["t_ps"], 1)

            def head(h):
                return slice(h % 2 * HD, h % 2 * HD + HD)

            NI = AH * NT
            pe.wait_ge(sem["t_act"], 1)

            def a_scores(i):
                h, t = i // NT, i % NT
                if i >= 2:
                    pe.wait_ge(sem["a_nm"], i - 1)
                mm(bank[4 + i % 2][:, 0:(t + 1) * P], tt[head(h), h // 2, cols(t)], tt[head(h), 3 + h // 2, 0:(t + 1) * P],
                   start=True, stop=True).then_inc(sem["a_s"], 1)

            a_scores(0)
            for i in range(NI):
                h, t = i // NT, i % NT
                if i + 1 < NI:
                    a_scores(i + 1)
                pe.wait_ge(sem["a_p"], i + 1)
                if i:
                    pe.wait_ge(sem["a_ptc"], i)
                for j in range(t + 1):
                    last = tr(bank[6][:, j * P:(j + 1) * P], a_pr[i % 2][:, j * P:(j + 1) * P], ident)
                last.then_inc(sem["a_pt"], 1)
                pe.wait_ge(sem["a_ptc"], i + 1)
                if i >= 2:
                    pe.wait_ge(sem["a_o"], i - 1)
                for j in range(t + 1):
                    last = mm(bank[7 - 4 * (i % 2)][:, 0:HD], a_prT[i % 2][:, j, :], pv[:, j, h * HD:(h + 1) * HD], start=(j == 0), stop=(j == t))
                last.then_inc(sem["a_pv"], 1)

            def b_scores(h):
                s = 4 * (h % 2)
                if h == 1:
                    pe.wait_ge(sem["a_o"], NI)
                if h >= 2:
                    pe.wait_ge(sem["b_sum"], h - 1)
                for j in range(NT):
                    b, at = J_BANK[j]
                    last = mm(bank[s + b][:, at:at + JN[j]], tt[head(h), 8 + h // 2, cols(j)], tt[head(h), 6 + h // 2, j * P:SEQ], start=True, stop=True)
                last.then_inc(sem["b_z"], 1)

            b_scores(0)
            for h in range(BH):
                s = 4 * (h % 2)
                if h + 1 < BH:
                    b_scores(h + 1)
                pe.wait_ge(sem["b_lk"], h + 1)
                for j in range(NT):
                    b, at = J_BANK[j]
                    last = mm(bank[s + b][:, at:at + JN[j]], tri_gt, bz[h % 2][:, JO[j]:JO[j] + JN[j]], start=True, stop=(j == NT - 1))
                    for j2 in range(j + 1, NT):
                        o = at + (j2 - j) * P
                        last = mm(bank[s + b][:, o:o + JN[j2]], ones, bz[h % 2][:, JO[j2]:JO[j2] + JN[j2]], start=False, stop=(j2 == NT - 1))
                last.then_inc(sem["b_after"], 1)
                pe.wait_ge(sem["b_a"], h + 1)
                if h:
                    pe.wait_ge(sem["b_o"], h)
                for t in range(NT):
                    for j in range(t + 1):
                        o = JO[j] + (t - j) * P
                        last = mm(bank[3][:, t * HD:(t + 1) * HD], bl[h % 2][:, o:o + P], pv[:, j, AW + h * HD:AW + (h + 1) * HD], start=(j == 0), stop=(j == t))
                last.then_inc(sem["b_pv"], 1)

            pe.wait_ge(sem["qd_ready"], 1)
            for b in range(NS):
                if b >= 2:
                    pe.wait_ge(sem["kvk_used"], b - 1)
                mm(bank[b % 2][:, 0:AW], ones[0:NS, :], as_qd[:, b, :], start=True, stop=True).then_inc(sem["qb_ps"], 1)
            pe.wait_ge(sem["as_used"], 1)
            for g in range(3):
                tr(bank[2][0:48, g * P:(g + 1) * P], as_s[:, g, :], ident)
            tr(bank[2][0:48, 384:392], as_self.rearrange("p b h -> p (b h)"), ident[0:NS, 0:NS]).then_inc(sem["sT_ps"], 1)
            pe.wait_ge(sem["s_norm"], 1)
            for g in range(3):
                tr(bank[3][:, g * 48:(g + 1) * 48], as_p[:, g * P:(g + 1) * P], ident[0:48, 0:48])
            tr(bank[3][0:NS, 144:192], as_p[:, 384:392], ident[0:48, 0:48]).then_inc(sem["pT_ps"], 1)
            pe.wait_ge(sem["bs_qd"], 1)

            def bs_spread(b):
                if b >= 2:
                    pe.wait_ge(sem["kvk_used"], NS + 4 * (b - 1))
                mm(bank[4 + b % 2][:, 0:BW], ones[0:NS, :], bs_qd[:, b, :], start=True, stop=True).then_inc(sem["qb_ps"], 1)

            bs_spread(0)
            bs_spread(1)
            pe.wait_ge(sem["pT_ready"], 1)
            for b in range(NS):
                n = NS + b
                pe.wait_ge(sem[f"kv{n % 4}"], 48 * (n // 4 + 1))
                for c in range(3):
                    o = bank[7][:, b * AH + 2 * c:b * AH + 2 * c + 2]
                    for g in range(3):
                        mm(o, view(kvbuf[n % 4], [3, AW])[:, g, c * P:(c + 1) * P], as_pT[:, g, b * AH + 2 * c:b * AH + 2 * c + 2], start=(g == 0), stop=False)
                    last = mm(o, pv[0:NS, NT, c * P:(c + 1) * P], as_pT[0:NS, 3, b * AH + 2 * c:b * AH + 2 * c + 2], start=False, stop=True)
                last.then_inc(sem["kvv_used"], 1)
            pe.wait_ge(sem["kvv_used"], NS)
            pe.sem_inc(sem["as_pv"], 1)

            for b in range(2, NS):
                bs_spread(b)
            pe.wait_ge(sem["bs_tot"], 1)
            mm(bank[6][:, 0:32], tri_gt, bs_tot.rearrange("p b h -> p (b h)"), start=True, stop=True).then_inc(sem["bs_cross"], 1)
            pe.wait_ge(sem["bs_ex"], 1)
            for n in range(32):
                b, c = n // 4, n % 4
                pe.wait_ge(sem[f"gather{n % 4}"], 16 * (8 + n // 4 + 1))
                chunk = view(kvbuf[n % 4], [8, BW])
                for r in range(8):
                    for hp in range(2):
                        last = mm(bank[hp][:, 2 * b:2 * b + 2], chunk[:, r, hp * P:(hp + 1) * P], bs_l[:, b, 8 * c + r, 2 * hp:2 * hp + 2],
                                  start=(c == 0 and r == 0), stop=(c == 3 and r == 7))
                last.then_inc(sem["kvv_used"], 1)
            pe.wait_ge(sem["kvv_used"], NS + 32)
            pe.sem_inc(sem["bs_pv"], 1)

            pe.wait_ge(sem["bs_o"], 1)
            for L in range(8):
                if L < 7:
                    pe.wait_ge(sem["c_q"], L + 1)
                    pe.wait_ge(sem["c_k"], L + 1)
                if L >= 2:
                    pe.wait_ge(sem["c_cp"], 4 * (L - 1))
                ks, qs = (ck1[L % 2], cq1[L % 2]) if L < 7 else (ck, tt[:, 10:12, :])
                for h in range(CH):
                    for t in range(NT):
                        last = mm(bank[4 * (L % 2) + h][:, cols(t)], ks[head(h), h // 2, cols(t)], qs[head(h), h // 2, cols(t)], start=True, stop=True)
                last.then_inc(sem["c_lev"], 1)
            pe.wait_ge(sem["c_k"], 8)
            pe.wait_ge(sem["c_cp"], 32)
            for j in range(2):
                for c in range(4):
                    last = tr(bank[j][:, c * P:(c + 1) * P], ck1[0][:, j, cols(c)], ident)
                last.then_inc(sem["c_kt"], 1)
            pe.wait_ge(sem["c_ktc"], 2)
            pe.wait_ge(sem["c_q"], 8)
            for t in range(NT):
                if t:
                    pe.wait_ge(sem["c_s"], t)
                if t >= 2:
                    pe.wait_ge(sem["c_raw"], t - 1)
                for h in range(CH):
                    o = bank[2 + 4 * (h % 2) + t % 2][:, h * HD:(h + 1) * HD]
                    v = pv[:, t, 640 + h * HD:704 + h * HD]
                    last = mm(o, c_att[:, h, t, :], v, start=True, stop=(t == 0))
                    if t:
                        last = mm(o, cq1[1][head(h), h // 2, cols(t)], c_S[head(h), h // 2, :], start=False, stop=True)
                last.then_inc(sem["c_pv"], 1)
                for h in range(CH):
                    last = mm(bank[4 + t % 2][head(h), h // 2 * HD:(h // 2 + 1) * HD], c_krow[:, h // 2 * 4 + t, head(h)], pv[:, t, 640 + h * HD:704 + h * HD], start=True, stop=True)
                last.then_inc(sem["c_pv"], 1)
            for hp in range(2):
                pe.wait_ge(sem["c_vd"], hp + 1)
                pe.wait_ge(sem["c_raw"], NT)
                for two in range(2):
                    last = mm(bank[6 + hp][two * HD:two * HD + HD, :], ones[0:NS, 0:HD], c_vdiag[:, two, :, :].rearrange("p b v -> p (b v)"), start=True, stop=True)
                last.then_inc(sem["c_vb"], 1)
            pe.wait_ge(sem["c_new"], 2)
            for h in range(CH):
                for b in range(NS):
                    last = mm(bank[5 - h % 2][0:NS, h * HD:(h + 1) * HD], c_qd[head(h), h // 2, b, :], c_new[head(h), b, h // 2, :], start=(b == 0), stop=(b == NS - 1))
            last.then_inc(sem["c_so"], 1)
            pe.wait_ge(sem["d_gelu"], 1)
            for g in range(DG):
                last = mm(bank[6 + g // 2][:, 256 * (g % 2):256 * (g % 2) + 256], sgu_wt[:, g, :], pv[:, 0:NT, 1408 + g * HD:1472 + g * HD], start=True, stop=True)
            last.then_inc(sem["d_mix"], 1)
            pe.wait_ge(sem["d_o"], 1)
            pe.wait_ge(sem["b_o"], BH)
            for t in range(NT):
                for j in range(3):
                    if t:
                        pe.wait_ge(sem["oT_evac"], 3 * (t - 1) + j + 1)
                    for c in range(4 if j < 2 else 1):
                        last = tr(bank[j][:, c * P:(c + 1) * P], orow[:, t, (4 * j + c) * P:(4 * j + c + 1) * P], ident)
                    last.then_inc(sem["oT_ps"], 1)
            for c in range(4):
                last = tr(bank[3][:, c * NS:(c + 1) * NS], orow[0:NS, NT, (5 + c) * P:(6 + c) * P], ident[0:NS, 0:NS])
            last.then_inc(sem["oT_ps"], 1)

            pe.wait_ge(sem["oT_evac"], 13)
            for j in range(32):
                k8, m = j // 4, j % 4
                half, br = k8 // NB, k8 % NB
                ms = slice(m * P, (m + 1) * P)
                if m == 0:
                    panel_wait(GATE0 + k8)
                if j >= 2:
                    pe.wait_ge(sem["m_acc"], j - 1)
                w = panel[(GATE0 + k8) % 2]
                for part, o in ((slice(0, SEQ), bank[j % 2][:, :]), (slice(SEQ, TOK), bank[4 + j % 2][:, 0:NS])):
                    for c in range(KC):
                        last = mm(o, w[:, c, ms], hT[:, c, part], start=(c == 0), stop=(c == KC - 1))
                last.then_inc(sem["dense_out"], 1)
                if m == 0:
                    pe.wait_ge(sem[f"w_br{k8 % 2}"], 16 * (k8 // 2 + 1))
                w = branch_panel[k8 % 2]
                for part, o in ((slice(0, SEQ), bank[2 + j % 2][:, :]), (slice(SEQ, TOK), bank[6 + j % 2][:, 0:NS])):
                    for c in range(BR_K[br]):
                        last = mm(o, w[:, c, ms], oT[:, BR_AT[br] + c, part], start=(c == 0), stop=(c == BR_K[br] - 1))
                last.then_inc(sem["dense_out"], 1)
            pe.wait_ge(sem["m_acc"], 32)
            for c in range(2):
                last = mm(bank[6 + c][:, :], sel9[0:9, :], mod_sb[0:9, 2, c * 512:c * 512 + 512], start=True, stop=True)
            last.then_inc(sem["g_ps"], 1)
            for k in range(2 * TILES):
                g, t = k // TILES, k % TILES
                if t == 0:
                    panel_wait(OUT0 + g)
                if k >= 2:
                    pe.wait_ge(sem["mix_sb"], k - 1)
                for c in range(KC):
                    last = mm(bank[k % 2][0:rows(t), :], mT[:, c, cols(t)], panel[(OUT0 + g) % 2][:, c, :], start=(c == 0), stop=(c == KC - 1))
                last.then_inc(sem["dense_out"], 1)
            modulation(1)
            transposed_rows(1)

            pe.wait_ge(sem["hT_evac"], 4 * TILES)
            for t in range(TILES):
                for c in range(KC):
                    last = mm(bank[0][0:rows(t), t * NE:(t + 1) * NE], hT[:, c, cols(t)], w_router[:, c, :], start=(c == 0), stop=(c == KC - 1))
            last.then_inc(sem["r_log"], 1)

            def sh_gu(t):
                if t == 0:
                    panel_wait(SHGU, 2)
                if t >= 2:
                    pe.wait_ge(sem["sh_h"], t - 1)
                for c in range(KC):
                    last = mm(bank[4 + t % 2][0:rows(t), :], hT[:, c, cols(t)], panel[SHGU % 2][:, c, :], start=(c == 0), stop=(c == KC - 1))
                last.then_inc(sem["sh_gu"], 1)

            sh_gu(0)
            sh_gu(1)
            pe.wait_ge(sem["r_mask"], TILES)
            for t in range(TILES):
                o = bank[1][0:rows(t), t * NE:(t + 1) * NE]
                for t2 in range(t):
                    mm(o, ones[:, 0:rows(t)], r_M[:, t2, :], start=(t2 == 0), stop=False)
                mm(o, tri_lt[0:rows(t), 0:rows(t)], r_M[0:rows(t), t, :], start=(t == 0), stop=True)
            for t in range(TILES):
                last = mm(bank[1][:, 320:384], ones[0:rows(t), :], r_M[0:rows(t), t, :], start=(t == 0), stop=(t == NT))
            last.then_inc(sem["r_pos"], 1)
            for t in range(TILES):
                n = rows(t)
                pe.wait_ge(sem["r_tab_in"], t + 1)
                for k in range(TOPK):
                    last = mm(bank[7][:, 0:MAXB], r_hs[0:n, k, :], r_hb[0:n, k, :], start=(t == 0 and k == 0), stop=(t == NT and k == TOPK - 1))
                last.then_inc(sem["r_tab"], 1)
            mm(bank[7][0:1, P:2 * P], r_be, ident, start=True, stop=True).then_inc(sem["r_tab"], 1)
            for t in range(TILES):
                n = rows(t)
                if t + 1 < TILES and t >= 1:
                    sh_gu(t + 1)
                pe.wait_ge(sem["sh_h"], t + 1)
                if t:
                    pe.wait_ge(sem["sh_hTc"], t)
                for c in range(2):
                    last = tr(bank[6][:, c * n:(c + 1) * n], hmid[t % 2][0:n, c * P:(c + 1) * P], ident[0:n, 0:n])
                last.then_inc(sem["sh_hT"], 1)
                pe.wait_ge(sem["sh_hTc"], t + 1)
                if t == 0:
                    panel_wait(SHD, 1 if SHD % 2 != SHGU % 2 else 2)
                else:
                    pe.wait_ge(sem["sh_row"], t)
                    pe.wait_ge(sem["sh_rv"], t)
                for m in range(2):
                    for c in range(2):
                        last = mm(bank[2 + m][0:n, :], hmT[t % 2][:, c, 0:n], panel_wide[SHD % 2][:, c, m * 512:(m + 1) * 512], start=(c == 0), stop=(c == 1))
                last.then_inc(sem["sh_y"], 1)

            pe.wait_ge(sem["r_ready"], 1)
            pe.wait_ge(sem["sh_row"], TILES)
            pe.wait_ge(sem["sh_rv"], TILES)
            last = pe.value_load(be_row[0:1, MAXB:MAXB + 1], min_val=THREES_MIN - 2, max_val=MAXB // 3 - 2) + 1

            def rows_transposed(p, q):
                pe.wait_ge(sem[f"gather{q}"], p * 16 + 16 * 17)
                if later(p) or q:
                    pe.wait_ge(sem["x_ca"], p * 3 + q)
                    pe.wait_ge(sem["x_cv"], p * 3 + q)
                for c in range(KC):
                    ins = tr(bank[c // 4][:, (c % 4) * P:(c % 4 + 1) * P], xg[q].rearrange("p (n c) -> p c n", c=KC)[:, c, :], ident)
                ins.then_inc(sem["x_t"], 1)

            def gate_up(p, q):
                i = p * 3 + q
                pe.wait_ge(sem[f"wg{q}"], p * 32 + 32)
                pe.wait_ge(sem["x_ca"], i + 1)
                pe.wait_ge(sem["x_cv"], i + 1)
                if later(p):
                    pe.wait_ge(sem["m_h"], i - 2)
                for c in range(KC):
                    ins = mm(bank[gu_bank[q]][:, :].rearrange("p (g n) -> p g n", g=2), xT[q][:, c, :], wgu[q][:, :, c, :], start=(c == 0), stop=(c == KC - 1))
                ins.then_inc(sem["gu_done"], 1)

            def middle_transposed(p, q):
                i = p * 3 + q
                pe.wait_ge(sem["m_h"], i + 1)
                if later(p) or q:
                    pe.wait_ge(sem["m_hTc"], i)
                for c in range(2):
                    ins = tr(bank[4][:, c * P:(c + 1) * P], hmid[q].rearrange("p (n c) -> p c n", c=2)[:, c, :], ident)
                ins.then_inc(sem["m_hT"], 1)

            def down(p, q):
                i = p * 3 + q
                pe.wait_ge(sem["m_hTc"], i + 1)
                pe.wait_ge(sem[f"wd{q}"], p * 16 + 16)
                if later(p) or q:
                    pe.wait_ge(sem["y_a"], i)
                    pe.wait_ge(sem["y_v"], i)
                for m in range(2):
                    for c in range(2):
                        ins = mm(bank[5 + m][:, :], hmT[q][:, c, :], wdn[q][:, c, m * 512:(m + 1) * 512], start=(c == 0), stop=(c == 1))
                ins.then_inc(sem["dn_done"], 1)

            def block(p, q, front=True, back=True):
                gate_up(p, q)
                if front:
                    rows_transposed(*block_at(p, q, 1))
                if back:
                    down(*block_at(p, q, -1))
                middle_transposed(p, q)

            rows_transposed(0, 0)
            block(0, 0, back=False)
            for i in range(1, 6):
                block(i // 3, i % 3)
            with pe.Fori(2, last) as p:
                for q in range(3):
                    block(p, q)
            for q in range(3):
                block(last, q, front=q < 2)
            down(last, 2)
            pe.wait_ge(sem["gu_done"], last * 3 + 3)
            for c in range(2):
                last = mm(bank[c][:, :], sel9[0:9, :], mod_sb[0:9, 2, c * 512:c * 512 + 512], start=True, stop=True)
            last.then_inc(sem["g_ps"], 1)


_INS = """x_prompt x_sample c_prompt c_sample cache_swa_k cache_swa_v cache_sb_k cache_sb_v state_hgrn page_table
norm1_g norm2_g w_ada b_ada w_in a_q_norm_g a_k_norm_g sb_bias c_out_norm_g sgu_w sgu_b w_branch_a w_branch_b
w_branch_c w_branch_d w_merge_gate b_merge_gate w_out w_router b_router w_exp_gate w_exp_up w_exp_down w_sh_gate
w_sh_up w_sh_down""".split()
_OUTS = [("y_p", (SEQ, D), (1, SEQ, D)), ("y_s", (NS, D), (NS, 1, D)),
         ("swa_k_p", (SEQ, AW), (1, 1, SEQ, AH, HD)), ("swa_v_p", (SEQ, AW), (1, 1, SEQ, AH, HD)),
         ("sb_k_p", (SEQ, BW), (1, 1, SEQ, BH, HD)), ("sb_v_p", (SEQ, BW), (1, 1, SEQ, BH, HD)),
         ("hgrn_p", (CH, HD, HD), (1, 1, CH, HD, HD)),
         ("swa_k_s", (NS, AW), (1, NS, 1, AH, HD)), ("swa_v_s", (NS, AW), (1, NS, 1, AH, HD)),
         ("sb_k_s", (NS, BW), (1, NS, 1, BH, HD)), ("sb_v_s", (NS, BW), (1, NS, 1, BH, HD)),
         ("hgrn_s", (NS, CH, HD, HD), (1, NS, CH, HD, HD)), ("sgu_v_s", (NS, DG * HD), (1, NS, 1, DG, HD))]


def kernel(**inputs):
    import numpy as _np
    import concourse.bacc as _bacc
    from concourse import mybir as _mybir
    from concourse.bass_utils import run_bass_kernel_spmd as _run

    nc = _bacc.Bacc("TRN2", target_bir_lowering=False, num_devices=1)
    arrays, ins, outs = {}, {}, {}
    for name in _INS:
        a = _np.ascontiguousarray(inputs[name])
        arrays[f"in_{name}_dram"] = a
        ins[name] = nc.dram_tensor(f"in_{name}_dram", a.shape, _mybir.dt.from_np(a.dtype), kind="ExternalInput").ap()
    for i, (name, shape, _) in enumerate(_OUTS):
        outs[name] = nc.dram_tensor(f"out_{i}_dram", shape, F32, kind="ExternalOutput").ap()
    trunk(nc, ins, outs)
    r = _run(nc, [arrays], core_ids=[0])
    return tuple(r.results[0][f"out_{i}_dram"].reshape(shape) for i, (_, _, shape) in enumerate(_OUTS))
```

```python
from contextlib import ExitStack

import concourse.bass as bass
from concourse import mybir

ALU = mybir.AluOpType
ACT = mybir.ActivationFunctionType
F32 = mybir.dt.float32
I32 = mybir.dt.int32
U32 = mybir.dt.uint32
AX = mybir.AxisListType.X

P = 128
D = 1024
KC = D // P
SEQ = 512
NT = SEQ // P
NS = 8
TILES = NT + 1
TOK = SEQ + NS
AH, BH, CH, DG, HD = 6, 4, 4, 4, 64
AW, BW = AH * HD, BH * HD
GROUPS_A = 3
PAST = 4096
PAGE = 128
PAGES = PAST // PAGE
SWA = 2048
NE, TOPK, EG, TOPG = 64, 8, 8, 4
ED = 256
MAXB = 99
EPS = 1e-6
SCALE = HD ** -0.5
BIG = 1e30
NB = 4
ROUTE_SCALE = 2.5
NPARAM = 15
PANEL = 512
IN_W = 3 * AW + 3 * BW + 6 * 256
BR_K = [AW // P, BW // P, 2, 2]
BR_AT = [0, 3, 5, 7]
LEVELS = [64, 32, 16, 8, 4, 2, 1]

SEMS = """const_ready params_in x_in c_in bada_in silu_c cT_ps cT_ready small_ps small_ready dense_out dense_evac
mod_gain bc_ps rstd_sqrt h_row h_ps hT_evac hro0 hro1
w_in0 w_in1 w_br0 w_br1 qk_sum qk_sqrt qk_norm t_ps t_evac t_act rows_out
a_s a_nm a_exp a_p a_pt a_ptc a_pv a_o
b_z b_l b_lk b_after b_sum b_e b_a b_pv b_o
kv0 kv1 kv2 kv3 kvk_used kvv_used qd_ready qb_ps as_used sT_ps s_nm s_exp s_norm pT_ps pT_ready as_ov as_pv as_o
idx_ready bs_qd bs_z bs_l bs_tot bs_cross bs_e bs_ex bs_ov bs_pv
c_lf c_x c_ab c_e c_q c_k c_lev c_cp c_kk c_kt c_ktc c_pv c_s c_raw c_sum c_sqrt hg_out
s0_in c_vd c_vb c_new c_so
d_gelu d_mix d_o oT_ps oT_evac m_sig m_acc x2_in g_ps mix_sb x1_ready
sh_gu sh_rv sh_sg sh_h sh_hT sh_hTc sh_y sh_row
r_log r_sc r_mask r_pos r_tab_in r_tab r_ready
wg0 wg1 wg2 wd0 wd1 wd2 x_col x_t x_ca x_cv gu_done m_sg m_h m_hT m_hTc dn_done y_a y_v yst0 yst1 yst2
gather0 gather1 gather2 gather3 f_used f_diag f_pe f_acc out_done act_chain dve_chain pool_chain""".split()


class Chain:

    def __init__(self, eng, sem):
        self.eng, self.sem, self.n = eng, sem, 0

    def __call__(self, ins):
        self.n += 1
        ins.then_inc(self.sem, 1)
        self.eng.wait_ge(self.sem, self.n)


def later(p):
    return not isinstance(p, int) or p > 0


def block_at(p, q, off):
    return p + (q + off) // 3, (q + off) % 3


THREES_MIN = -(-TOK * TOPK // P) // 3


IN_ORDER = [2, 0, 1, 3, 4, 5, 6]
KEYS_GATHERED = [11, 11, 10, 0]
ALL_GATHERED = [n + 8 for n in KEYS_GATHERED]


def dense_plan():
    panels = [("ada", g, 1) for g in range(6)]
    panels += [("in", g, TILES) for g in IN_ORDER]
    panels += [("gate", (half, br), 8) for half in range(2) for br in range(NB)]
    panels += [("out", g, TILES) for g in range(2)]
    panels += [("ada", g, 1) for g in range(6, 12)]
    panels += [("shgu", 0, 0), ("shd", 0, 0)]
    used, n = [], 0
    for _, _, outs in panels:
        n += outs
        used.append(n)
    return panels, used


def trunk(nc, A, O):
    panels, panel_used = dense_plan()
    at_of = {(kind, g): i for i, (kind, g, _) in enumerate(panels)}
    out_before = [0] + panel_used
    IN0_OUT, GATE_OUT = out_before[at_of[("in", IN_ORDER[0])]], out_before[at_of[("gate", (0, 0))]]
    IN0, GATE0, OUT0, ADA2, SHGU, SHD = (at_of[k] for k in (("in", IN_ORDER[0]), ("gate", (0, 0)), ("out", 0), ("ada", 6), ("shgu", 0), ("shd", 0)))

    h2d = nc.dram_tensor("h2_rows", (TOK, D), F32, kind="Internal").ap()
    yd = nc.dram_tensor("expert_rows", (TOK * TOPK, D), F32, kind="Internal").ap()

    with ExitStack() as ctx:
        sem = {n: ctx.enter_context(nc.semaphore(n)) for n in SEMS}
        total = 53200
        arena = ctx.enter_context(nc.sbuf_tensor("arena", [P, total], F32))
        top = [0]

        def view(off, dims, parts=P, dt=F32):
            n = 1
            for d in dims:
                n *= d
            ap = arena[0:parts, off:off + n]
            if dt is not F32:
                ap = ap.bitcast(dt)
            names = "abcd"[:len(dims)]
            if len(dims) > 1:
                kw = {names[i]: dims[i] for i in range(1, len(dims))}
                ap = ap.rearrange(f"p ({' '.join(names)}) -> p {' '.join(names)}", **kw)
            return ap

        def region(n):
            at = top[0]
            top[0] += n
            assert top[0] <= total, (top[0], total)
            return at

        def new(dims, parts=P, dt=F32):
            n = 1
            for d in dims:
                n *= d
            return view(region(n), dims, parts, dt)

        bank = [ctx.enter_context(nc.psum_tensor(f"bank{i}", [P, 512], F32)) for i in range(8)]

        ident, ones, tri_gt, tri_lt = new([P]), new([P]), new([P]), new([P])
        amult, aneg = new([NT, P]), new([NT, P])
        lmask = new([8, P], dt=I32)
        iota_e, iota_s, iota_b, row_code, pcol = new([NE]), new([P]), new([MAXB]), new([TILES, TOPK]), new([1])
        d88, sel9, eps_t = new([8, 8]), new([P]), new([1])
        qk_g, co_g, sbb = new([2, HD]), new([HD]), new([BH])
        sgu_wt, sgu_bt, w00, b00 = new([DG, P]), new([DG]), new([DG]), new([DG])
        bmg_t, brt, w_router = new([32]), new([NE]), new([KC, NE])
        pt_sb, q4, idx_kv = new([NS], dt=I32), new([1], dt=I32), new([NS, 4], dt=I32)
        cT, gates = new([KC, 9]), new([TILES, TOPK])
        ssq, rstd, qk_ss = new([8]), new([8]), new([TILES, 12])
        nm, den = new([2]), new([2])
        HT = region(KC * TOK)
        hT = view(HT, [KC, TOK])
        mod_sb = new([3, D])
        ring = region(8192)
        X = region(5760)
        W = region(TILES * 1792)
        PV = region(TILES * 1664)
        T = region(14 * SEQ)
        tts = new([4, NS])
        os_T = new([5, NS])
        rows_s = new([1024])
        BS_Z = region(3 * AW)
        bs_z = view(BS_Z, [NS, 32, BH])

        xr = view(X, [TILES, D])
        orow = view(X, [TILES, 1152])
        pqk = view(W, [TILES, 1792])
        pv = view(PV, [TILES, 1664])
        tt = view(T, [14, SEQ])
        panel = [view(ring + 4096 * i, [KC, PANEL]) for i in range(2)]
        panel_wide = [view(ring + 4096 * i, [4, D]) for i in range(2)]
        branch_panel = [view(PV + 1536 * i, [3, PANEL]) for i in range(2)]
        kvbuf = [ring + 2048 * i for i in range(4)]

        bada = view(T, [3, D], 9)
        hrow = [view(T + 3072 + 1024 * i, [D]) for i in range(2)]
        junk = view(T + 5120, [D])
        g9 = view(T + 6144, [D], 9)
        cs = view(W, [D], 9)
        bmg_r = view(W + 2048, [P], 32)
        sgub_r = view(W + 2176, [P], 4)
        sguw_r = view(W + 2304, [DG, P])
        m_dist, m_bits = view(W + 3072, [NT, P], dt=I32), view(W + 3584, [NT, P], dt=I32)
        m_a, m_b, m_c = (view(W + 4096 + 512 * i, [NT, P]) for i in range(3))
        l_t, l_s, l_x, l_sh = (view(W + 5632 + 128 * i, [P], dt=I32) for i in range(4))
        l_gt, l_eq, tri_le = view(W + 6144, [P]), view(W + 6272, [P]), view(W + 6400, [P])
        qk_sq = view(T + 6144, [768])
        a_sm = [view(W + 512 * i, [512]) for i in range(2)]
        a_pr = [view(W + 1024 + 512 * i, [512]) for i in range(2)]
        a_prT = [view(W + 2048 + 512 * i, [4, P]) for i in range(2)]
        JN = [SEQ - j * P for j in range(NT)]
        JO = [sum(JN[:j]) for j in range(NT)]
        JW = sum(JN)
        bz = [view(W + 3840 * i, [JW]) for i in range(2)]
        bl = [view(W + 3840 * i + 1280, [JW]) for i in range(2)]
        blb = [view(W + 3840 * i + 2560, [JW]) for i in range(2)]
        JPIECE = [(0, 0, 512, 0), (1, 512, 384, 0), (2, 896, 384, 0)]
        J_BANK = [(0, 0), (1, 0), (2, 0), (2, 256)]
        as_qd = view(T, [NS, AW], NS)
        as_prod = view(T + 3072, [3, AW])
        as_s = view(T + 4224, [3, NS * AH])
        as_self = view(T + 4368, [NS, AH], NS)
        as_p = view(T + 4416, [392], 48)
        as_pT = view(T + 4808, [4, 48])
        as_tmp = view(T + 5000, [AH], NS)
        as_ov = [mod_sb[0:AH, 0:2, :].rearrange("p a n -> p (a n)")[:, b * AW:(b + 1) * AW] for b in range(5)]
        as_ov += [view(BS_Z + b * AW, [AW], AH) for b in range(3)]
        as_own = view(W + 3072, [AW], NS)
        key_slot = [view(T + 2048 * i, [8, BW]) for i in range(3)]
        bs_prod, bs_qd = view(X, [8, BW]), view(X + 2048, [NS, BW], NS)
        bs_l, bs_lb = (view(X + 1024 * i, [NS, 32, BH]) for i in range(2))
        bs_e = [view(X + 2048 + 1024 * i, [NS, 32, BH]) for i in range(2)]
        bs_tot = view(X + 4096, [NS, BH])
        bs_w = bs_z
        bs_ov = mod_sb[0:BH, 0:2, :].rearrange("p a (b n) -> p (a b) n", n=BW)
        BS_BANK = [0, 1, 2, 7]
        ck, cb = (view(W + 1024 * i, [2, SEQ]) for i in range(2))
        cx = [view(W + 2048, [2, SEQ]), view(W + 7168, [2, SEQ])]
        cq1 = [view(W + 3072, [2, SEQ]), view(T, [2, SEQ])]
        ck1 = [view(W + 4096, [2, SEQ]), view(T + 1024, [2, SEQ])]
        c_att = view(W + 5120, [CH, NT, P])
        c_krow = view(W + 7168, [8, P])
        c_S = view(W + 8192, [2, HD])
        c_tot = view(W + 8320, [2, NT])
        c_qd = view(W + 8328, [2, NS, NS])
        cs_lf, cs_k = view(W + 8456, [2, NS]), view(W + 8472, [2, NS])
        c_ss = view(W + 8488, [TILES, CH])
        c_vdiag = view(T + 2048, [2, NS, HD], NS)
        c_S0 = view(T + 3072, [NS, 2, HD])
        c_new = view(T + 4096, [NS, 2, HD])
        cs_tmp = view(W + 3072, [NS, HD])
        c_sq = view(W + 4096, [CH, HD])
        OT_BANK = [2, 3, 6]
        HALF = TOK // 2
        row_half = [slice(0, HALF), slice(HALF, TOK)]
        oT = view(T, [9, TOK])
        mT = view(W, [KC, TOK])
        sg_m = [view(W + 4160 + 520 * i, [TOK]) for i in range(2)]
        tmp_m = view(W + 5200, [TOK])
        mixs = [view(W + 5720 + 512 * i, [512]) for i in range(2)]
        mixt = view(W + 6744, [512])
        sh = view(PV, [TILES, D])
        xg = [view(PV + 5120, [D]), view(PV + 6144, [D]), view(T + 3072, [D])]
        sgate = [view(PV + 7168, [ED]), view(PV + 7424, [ED]), view(W + 7168, [ED])]
        hmid = [view(PV + 7680, [ED]), view(PV + 7936, [ED]), view(W + 7424, [ED])]
        xT = [view(T, [KC, P]), view(T + D, [KC, P]), view(T + 4096, [KC, P])]
        hmT = [view(T + 2048, [2, P]), view(T + 2304, [2, P]), view(W + 7680, [2, P])]
        slot_tok = view(T + 2560, [MAXB], dt=I32)
        be_row = view(T + 2660, [P], 1, dt=I32)
        gidx = [view(T + 2790 + i, [1], dt=I32) for i in range(3)]
        slot_row = view(T + 2840, [MAXB], dt=I32)
        sidx = [view(T + 2940 + i, [1], dt=I32) for i in range(3)]
        dest_i = view(T + 2800, [TILES, TOPK], dt=I32)
        ybuf = [view(T + 5120, [D]), view(T + 6144, [D]), view(W + 6144, [D])]
        onehot = view(W + 6144, [TILES, TOPK, NE])
        r_s = view(T + 5120, [TILES, NE])
        r_c = view(T + 5440, [TILES, NE])
        r_M = view(T + 5760, [TILES, NE])
        r_m8 = view(T + 6080, [EG, 8])
        r_g, r_g8, r_gi = view(T + 6144, [8]), view(T + 6152, [8]), view(T + 6160, [8], dt=U32)
        r_gf, r_gm = view(T + 6168, [8]), view(T + 6176, [8])
        r_eq = view(T + 6184, [8, 4])
        r_mc, r_t8, r_ti, r_tf = view(T + 6216, [NE]), view(T + 6280, [8]), view(T + 6288, [8], dt=U32), view(T + 6296, [8])
        r_prod = view(T + 6304, [TOPK, NE])
        r_sum = view(T + 6816, [1])
        r_cnt, r_cnti, r_nb, r_end = view(T + 6820, [NE]), view(T + 6884, [NE], dt=I32), view(T + 6948, [NE]), view(T + 7012, [NE])
        r_st, r_be = view(T + 7076, [NE]), view(T + 7140, [1])
        r_d, r_dv = view(T + 7142, [8]), view(T + 7150, [8], dt=I32)
        r_f8 = view(T + 7158, [8])
        r_hs = mod_sb[:, 0, :].rearrange("p (a b) -> p a b", b=P)
        r_hb = mod_sb[:, 1, 0:TOPK * MAXB].rearrange("p (a b) -> p a b", b=MAXB)
        wset = [W, ring, HT]
        wgu = [view(w, [2, KC, ED]) for w in wset]
        gu_bank = [2, 3, 7]
        wdn = [view(w + 4096, [2, D]) for w in wset]
        fbuf = [[view(at + 2 * D * i, [2, D]) for i in range(4)] for at in (W, ring)]
        w_in_loads = [len(range(i, len(panels), 2)) + (SHGU % 2 == i) for i in range(2)]
        f_sem = [[(f"kv{i}", 192) for i in range(4)],
                 [(f"w_in{i}", 16 * w_in_loads[i]) for i in range(2)] + [(f"w_br{i}", 64) for i in range(2)]]
        F_ORDER = [NT] + list(range(NT))
        F_BANK = [(2, 3), (4, 7)]
        f_dg = view(T, [TILES, TOPK // 2, P])

        def rows(t):
            return P if t < NT else NS

        def cols(t):
            return slice(t * P, t * P + rows(t))

        blk = ctx.enter_context(nc.Block())

        @blk.sync
        def _(sp):
            def load(dst, src, s):
                sp.dma_start(dst, src).then_inc(sem[s], 16)

            def w_panel(name, c0, w):
                return A[name][0, :, c0:c0 + w].rearrange("(c p) n -> p c n", p=P)

            def panel_load(i):
                kind, g, _ = panels[i]
                s = f"w_in{i % 2}"
                if i >= 2:
                    sp.wait_ge(sem["dense_out"], panel_used[i - 2])
                dst = panel[i % 2]
                if kind == "ada":
                    load(dst, w_panel("w_ada", g * PANEL, PANEL), s)
                elif kind == "in":
                    w = min(PANEL, IN_W - g * PANEL)
                    load(dst[:, :, 0:w], w_panel("w_in", g * PANEL, w), s)
                elif kind == "gate":
                    load(dst, w_panel("w_merge_gate", g[1] * D + g[0] * PANEL, PANEL), s)
                elif kind == "out":
                    load(dst, w_panel("w_out", g * PANEL, PANEL), s)
                elif kind == "shgu":
                    load(dst[:, :, 0:ED], w_panel("w_sh_gate", 0, ED), s)
                    load(dst[:, :, ED:2 * ED], w_panel("w_sh_up", 0, ED), s)
                else:
                    load(panel_wide[i % 2][:, 0:2, :], w_panel("w_sh_down", 0, D), s)

            def branch_load(k):
                half, br = k // NB, k % NB
                if k >= 2:
                    sp.wait_ge(sem["dense_out"], panel_used[GATE0 + k - 2])
                name = "w_branch_" + "abcd"[br]
                load(branch_panel[k % 2][:, 0:BR_K[br], :], w_panel(name, half * PANEL, PANEL), f"w_br{k % 2}")

            load(cs[0:NS, :], A["c_sample"], "c_in")
            load(cs[NS:NS + 1, :], A["c_prompt"], "c_in")
            panel_load(0)
            panel_load(1)
            load(bada.rearrange("p a b -> p (a b)"), A["b_ada"][0, 0:3 * D].partition_broadcast(9), "bada_in")
            load(g9, A["norm1_g"][0].partition_broadcast(9), "bada_in")
            load(xr[:, 0:NT, :], A["x_prompt"][0].rearrange("(t p) d -> p t d", p=P), "x_in")
            load(xr[0:NS, NT, :], A["x_sample"][:, 0, :], "x_in")
            load(qk_g[:, 0, :], A["a_q_norm_g"][0].partition_broadcast(P), "params_in")
            load(qk_g[:, 1, :], A["a_k_norm_g"][0].partition_broadcast(P), "params_in")
            load(co_g, A["c_out_norm_g"][0].partition_broadcast(P), "params_in")
            load(sbb, A["sb_bias"][0].partition_broadcast(P), "params_in")
            load(brt, A["b_router"][0].partition_broadcast(P), "params_in")
            load(sguw_r, A["sgu_w"][0].rearrange("g p q -> p g q"), "params_in")
            load(sgub_r, A["sgu_b"][0], "params_in")
            load(bmg_r, A["b_merge_gate"][0].rearrange("(c p) -> c p", p=P), "params_in")
            load(w_router, A["w_router"][0].rearrange("(c p) n -> p c n", p=P), "params_in")
            with nc.allow_non_contiguous_dma("a few words of parameters and the page table"):
                load(w00[0:NS, :], A["sgu_w"][0, :, 0, 0].partition_broadcast(NS), "params_in")
                load(b00[0:NS, :], A["sgu_b"][0, :, 0].partition_broadcast(NS), "params_in")
                for q in range(4):
                    load(pt_sb[q::4, :], A["page_table"].rearrange("b a -> a b"), "params_in")
            for i in range(2, GATE0):
                panel_load(i)
            sp.wait_ge(sem["qk_norm"], TILES)
            sp.wait_ge(sem["dense_evac"], 6 + 7 * TILES)
            for n, (name, buf, c) in enumerate((("swa_k", pqk, AW), ("swa_v", pv, 0), ("sb_k", pqk, 2 * AW + BW), ("sb_v", pv, AW))):
                w = AW if n < 2 else BW
                sp.dma_start(O[name + "_p"].rearrange("(t p) n -> p t n", p=P), buf[:, 0:NT, c:c + w]).then_inc(sem["rows_out"], 16)
                sp.dma_start(O[name + "_s"], buf[0:NS, NT, c:c + w]).then_inc(sem["rows_out"], 16)
            for n in range(16):
                cache = A["cache_swa_k"] if n < NS else A["cache_swa_v"]
                src = cache[0, n % NS].rearrange("r h d -> r (h d)")
                if n < 4:
                    sp.wait_ge(sem["kvv_used"], 29 + n)
                elif n < 12:
                    sp.wait_ge(sem["kvk_used"], 32 + n - 3)
                else:
                    sp.wait_ge(sem["kvv_used"], 32 + n - 11)
                dst = view(kvbuf[n % 4], [3, AW])
                for g, step in enumerate((1, 4, 16)):
                    load(dst[:, g, :], src[SWA - P * step:SWA:step, :], f"kv{n % 4}")
            sp.wait_ge(sem["kvv_used"], NS + 32)
            panel_load(GATE0)
            panel_load(GATE0 + 1)
            sp.wait_ge(sem["as_o"], 1)
            for two in range(2):
                load(c_S0[two * HD:two * HD + HD, :, :, :], A["state_hgrn"][0].rearrange("b (c two) k v -> two k b c v", two=2)[two], "s0_in")
            sp.wait_ge(sem["c_s"], NT)
            for two in range(2):
                load(O["hgrn_p"].rearrange("(c two) k v -> two k c v", two=2)[two], c_S[two * HD:two * HD + HD, :, :], "hg_out")
            sp.wait_ge(sem["c_new"], 2)
            for two in range(2):
                for c in range(2):
                    load(O["hgrn_s"].rearrange("b (c two) k v -> c two k b v", two=2)[c, two], c_new[two * HD:two * HD + HD, :, c, :], "hg_out")
            sp.wait_ge(sem["d_gelu"], 1)
            sp.dma_start(O["sgu_v_s"], pv[0:NS, NT, 1408:1664]).then_inc(sem["rows_out"], 16)
            sp.wait_ge(sem["d_o"], 1)
            sp.wait_ge(sem["rows_out"], 16 * 9)
            branch_load(0)
            branch_load(1)
            for k in range(2, 8):
                panel_load(GATE0 + k)
                branch_load(k)
            sp.wait_ge(sem["oT_ps"], 13)
            load(xr[:, 0:NT, :], A["x_prompt"][0].rearrange("(t p) d -> p t d", p=P), "x2_in")
            load(xr[0:NS, NT, :], A["x_sample"][:, 0, :], "x2_in")
            panel_load(OUT0)
            panel_load(OUT0 + 1)
            sp.wait_ge(sem["dense_out"], out_before[OUT0])
            load(bada.rearrange("p a b -> p (a b)"), A["b_ada"][0, 3 * D:6 * D].partition_broadcast(9), "bada_in")
            load(g9, A["norm2_g"][0].partition_broadcast(9), "bada_in")
            for i in range(ADA2, len(panels)):
                panel_load(i)
            for t in range(TILES):
                sp.wait_ge(sem["h_row"], TILES + t + 1)
                sp.dma_start(h2d[t * P:t * P + rows(t), :], hrow[t % 2][0:rows(t), :]).then_inc(sem[f"hro{t % 2}"], 16)

            sp.wait_ge(sem["r_ready"], 1)
            last = sp.value_load(be_row[0:1, MAXB:MAXB + 1], min_val=THREES_MIN - 2, max_val=MAXB // 3 - 2) + 1

            def block_loads(p, q, first):
                i = p * 3 + q
                e = sp.value_load(be_row[0:1, bass.ds(i, 1)], min_val=0, max_val=NE - 1)
                if not first:
                    sp.wait_ge(sem["gu_done"], i - 2)
                sp.dma_start(wgu[q][:, 0, :, :], A["w_exp_gate"][0, bass.ds(e, 1)].rearrange("e (p c) n -> p (e c) n", c=KC)).then_inc(sem[f"wg{q}"], 16)
                sp.dma_start(wgu[q][:, 1, :, :], A["w_exp_up"][0, bass.ds(e, 1)].rearrange("e (p c) n -> p (e c) n", c=KC)).then_inc(sem[f"wg{q}"], 16)
                if not first:
                    sp.wait_ge(sem["dn_done"], i - 2)
                sp.dma_start(wdn[q], A["w_exp_down"][0, bass.ds(e, 1)].rearrange("e (p c) n -> p (e c) n", c=2)).then_inc(sem[f"wd{q}"], 16)

            sp.wait_ge(sem["sh_y"], TILES)
            block_loads(0, 0, True)
            block_loads(0, 1, True)
            sp.wait_ge(sem["r_ready"], 2)
            sp.wait_ge(sem["x_col"], 3)
            block_loads(0, 2, True)
            with sp.Fori(1, last + 1) as p:
                for q in range(3):
                    block_loads(p, q, False)
            for q in range(3):
                sp.wait_ge(sem[f"yst{q}"], last * 16 + 16)
            for n in range(TILES * TOPK // 2):
                u, kk = n // 4, n % 4
                t = F_ORDER[u]
                if u >= 2:
                    if kk < 2:
                        sp.wait_ge(sem["f_used"], 4 * (u - 2) + 2 * kk + 2)
                    else:
                        sp.wait_ge(sem["f_pe"], 2 * (u - 2) + kk - 1)
                load(fbuf[u % 2][kk][0:rows(t), :, :], yd.rearrange("(n k) d -> n k d", k=TOPK)[t * P:t * P + rows(t), 2 * kk:2 * kk + 2, :], f_sem[u % 2][kk][0])
            sp.wait_ge(sem["rows_out"], 16 * 9)
            sp.wait_ge(sem["hg_out"], 16 * 6)
            sp.wait_ge(sem["hro0"], 16 * 3)
            sp.wait_ge(sem["hro1"], 16 * 2)
            sp.wait_ge(sem["out_done"], 16 * TILES)

        @blk.gpsimd
        def _(pool):
            step = Chain(pool, sem["pool_chain"])

            def select(out, in_, pattern, base, mult, op, fill):
                step(pool.affine_select(out=out, in_=in_, pattern=pattern, base=base, channel_multiplier=mult,
                                        compare_op=op, fill=fill))

            step(pool.memset(ones, 1.0))
            step(pool.memset(ident, 0.0))
            select(ident, ident, [[-1, P]], 0, 1, ALU.not_equal, 1.0)
            pool.memset(eps_t, EPS)
            select(tri_gt, ones, [[-1, P]], 0, 1, ALU.is_gt, 0.0)
            select(tri_lt, ones, [[1, P]], 0, -1, ALU.is_gt, 0.0)
            step(pool.memset(sel9, 0.0))
            select(sel9, sel9, [[0, P]], -NS, 1, ALU.not_equal, 1.0)
            step(pool.memset(d88, 0.0))
            select(d88, d88, [[1, NS], [-1, NS]], 0, 0, ALU.not_equal, 1.0)
            step(pool.iota(m_dist, pattern=[[-P, NT], [-1, P]], base=(NT - 1) * P, channel_multiplier=1))
            step(pool.iota(l_t, pattern=[[1, P]], base=0, channel_multiplier=0))
            step(pool.iota(l_s, pattern=[[0, P]], base=0, channel_multiplier=1))
            for out, pat in ((iota_e, [[1, NE]]), (iota_s, [[1, P]]), (iota_b, [[1, MAXB]])):
                step(pool.iota(out, pattern=pat, base=0, channel_multiplier=0, allow_small_or_imprecise_dtypes=True))
            step(pool.iota(row_code, pattern=[[-P * TOPK, TILES], [-1, TOPK]], base=TOK * TOPK, channel_multiplier=-TOPK, allow_small_or_imprecise_dtypes=True))
            pool.iota(pcol, pattern=[[0, 1]], base=0, channel_multiplier=1, allow_small_or_imprecise_dtypes=True)
            pool.iota(q4, pattern=[[0, 1]], base=0, channel_multiplier=1).then_inc(sem["const_ready"], 1)

            pool.wait_ge(sem["idx_ready"], 1)
            for n in range(64):
                cache = A["cache_sb_k"] if n < 32 else A["cache_sb_v"]
                src = cache[0].rearrange("n (q r) h d -> (n q) (r h d)", q=16)
                b, c = (n % 32) // 4, n % 4
                if n < 3:
                    pool.wait_ge(sem["h_ps"], 2 * TILES)
                elif n < 32:
                    pool.wait_ge(sem["kvk_used"], n - 2)
                elif n < 36:
                    pool.wait_ge(sem["dense_out"], panel_used[GATE0 - 1])
                else:
                    pool.wait_ge(sem["kvv_used"], n - 35)
                dst = key_slot[n % 3].rearrange("p r n -> p (r n)") if n < 32 else view(kvbuf[n % 4], [2048])
                slot = n % 3 if n < 32 else n % 4
                pool.indirect_dma_start(out=dst, out_offset=None, in_=src,
                                        in_offset=bass.IndirectOffsetOnAxis(ap=idx_kv[:, b, c:c + 1], axis=0)).then_inc(sem[f"gather{slot}"], 16)

            for L in range(9):
                pool.wait_ge(sem["c_e"], L + 1)
                if L == 0:
                    pool.wait_ge(sem["c_kk"], 1)
                if L >= 2:
                    pool.wait_ge(sem["c_lev"], L - 1)
                if L != 7:
                    pool.tensor_tensor(ck1[L % 2], ck, cx[L % 2], ALU.mult).then_inc(sem["c_k"], 1)

            pool.wait_ge(sem["r_ready"], 2)
            pool.wait_ge(sem["hro0"], 16 * 3)
            pool.wait_ge(sem["hro1"], 16 * 2)
            last = pool.value_load(be_row[0:1, MAXB:MAXB + 1], min_val=THREES_MIN - 2, max_val=MAXB // 3 - 2) + 1

            def column(dst, table, i, count):
                pool.tensor_copy(dst, table[:, bass.ds(i, 1)]).then_inc(sem["pool_chain"], 1)
                pool.wait_ge(sem["pool_chain"], count)
                pool.sem_inc(sem["x_col"], 1)

            def block_gather(p, q, count):
                i = p * 3 + q
                if not isinstance(p, int) or p > 0:
                    pool.wait_ge(sem["x_t"], i - 2)
                column(gidx[q], slot_tok, i, count)
                pool.indirect_dma_start(out=xg[q], out_offset=None, in_=h2d, bounds_check=TOK - 1, oob_is_err=False,
                                        in_offset=bass.IndirectOffsetOnAxis(ap=gidx[q], axis=0)).then_inc(sem[f"gather{q}"], 16)

            def block_scatter(p, q, count):
                i = p * 3 + q
                if not isinstance(p, int) or p > 0:
                    pool.wait_ge(sem[f"yst{q}"], p * 16)
                column(sidx[q], slot_row, i, count)
                pool.wait_ge(sem["y_a"], i + 1)
                pool.wait_ge(sem["y_v"], i + 1)
                pool.sem_inc(sem["x_col"], 1)
                pool.indirect_dma_start(out=yd, out_offset=bass.IndirectOffsetOnAxis(ap=sidx[q], axis=0), in_=ybuf[q],
                                        in_offset=None, bounds_check=TOK * TOPK - 1, oob_is_err=False).then_inc(sem[f"yst{q}"], 16)

            for q in range(3):
                step(pool.memset(xg[q], 0.0))
            n0 = step.n
            for q in range(3):
                block_gather(0, q, n0 + q + 1)

            def gather_and_scatter(p):
                for q in range(3):
                    block_gather(p, q, p * 6 + (n0 + 2 * q - 2))
                    block_scatter(p - 1, q, p * 6 + (n0 + 2 * q - 1))

            gather_and_scatter(1)
            with pool.Fori(2, last + 1) as p:
                gather_and_scatter(p)
            for q in range(3):
                block_scatter(last, q, last * 6 + (n0 + 4 + q))

        @blk.scalar
        def _(act):
            step = Chain(act, sem["act_chain"])
            fn = nc.scalar.activation

            def norm_stats(half):
                if half == 0:
                    act.wait_ge(sem["x_in"], 32)
                for t in range(TILES):
                    n = rows(t)
                    if half == 1:
                        act.wait_ge(sem["x1_ready"], TILES + t + 1)
                    step(fn(junk[0:n], xr[0:n, t, :], ACT.Square, accum_out=ssq[0:n, t:t + 1]))
                    fn(rstd[0:n, t:t + 1], ssq[0:n, t:t + 1], ACT.Sqrt, bias=eps_t[0:n], scale=1.0 / D).then_inc(sem["rstd_sqrt"], 1)

            def hT_copies(half):
                for t in range(TILES):
                    for j in range(2):
                        act.wait_ge(sem["h_ps"], 2 * (TILES * half + t) + j + 1)
                        n = rows(t)
                        src = bank[2 + j][:, 0:4 * n].rearrange("p (c n) -> p c n", n=n)
                        act.copy(hT[:, 4 * j:4 * j + 4, cols(t)], src).then_inc(sem["hT_evac"], 1)

            act.wait_ge(sem["c_in"], 32)
            fn(cs, cs, ACT.Silu).then_inc(sem["silu_c"], 1)
            act.wait_ge(sem["const_ready"], 1)
            norm_stats(0)
            hT_copies(0)

            places = [(0, 768, pqk, 0), (768, 1152, pv, 0), (1152, 1664, pqk, 768), (1664, 1920, pv, 384),
                      (1920, 2432, pqk, 1280), (2432, 3456, pv, 640)]
            for i, g in enumerate(IN_ORDER):
                for t in range(TILES):
                    k = IN0_OUT + i * TILES + t
                    act.wait_ge(sem["dense_out"], k + 1)
                    for lo, hi, buf, at in places:
                        a, b = max(lo, g * PANEL), min(hi, (g + 1) * PANEL)
                        if a < b:
                            last = act.copy(buf[0:rows(t), t, at + a - lo:at + b - lo],
                                            bank[k % 2][0:rows(t), a - g * PANEL:b - g * PANEL])
                    last.then_inc(sem["dense_evac"], 1)
                if i == 5:
                    act.wait_ge(sem["bs_z"], 1)
                    step(fn(bs_l, bs_z, ACT.Abs))
                    step(fn(bs_l, bs_l, ACT.Exp, scale=-1.0))
                    fn(bs_l, bs_l, ACT.Ln, bias=ones[:, 0:1]).then_inc(sem["bs_l"], 1)
            for t in range(TILES):
                act.wait_ge(sem["qk_sum"], t + 1)
                n = rows(t)
                fn(qk_ss[0:n, t, :], qk_ss[0:n, t, :], ACT.Sqrt, bias=eps_t[0:n], scale=1.0 / HD).then_inc(sem["qk_sqrt"], 1)
            for t in range(NT):
                for j in range(4):
                    act.wait_ge(sem["t_ps"], 4 * t + j + 1)
                    w = 4 if j < 3 else 2
                    src = bank[2 + j][:, 0:P * w].rearrange("p (c n) -> p c n", n=P)
                    act.copy(tt[:, 4 * j:4 * j + w, cols(t)], src).then_inc(sem["t_evac"], 1)
            act.wait_ge(sem["t_ps"], 17)
            act.copy(tts, bank[2][:, 0:32].rearrange("p (c n) -> p c n", n=NS)).then_inc(sem["t_evac"], 1)
            act.wait_ge(sem["t_evac"], 17)
            fn(tt[:, 10:12, :], tt[:, 10:12, :], ACT.Silu)
            fn(tts[:, 0:2, :], tts[:, 0:2, :], ACT.Silu)
            step(fn(pv[:, 0:NT, 896:1152], pv[:, 0:NT, 896:1152], ACT.Silu))
            fn(pv[0:NS, NT, 896:1152], pv[0:NS, NT, 896:1152], ACT.Silu).then_inc(sem["t_act"], 1)
            act.wait_ge(sem["bs_e"], 1)
            fn(bs_w, bs_e[1], ACT.Exp).then_inc(sem["bs_ex"], 1)
            step(fn(pv[:, 0:NT, 1152:1664], pv[:, 0:NT, 1152:1664], ACT.Gelu))
            fn(pv[0:NS, NT, 1152:1664], pv[0:NS, NT, 1152:1664], ACT.Gelu).then_inc(sem["d_gelu"], 1)

            NI = AH * NT
            act.wait_ge(sem["rows_out"], 16 * 8)

            def a_exp(i):
                t = i % NT
                w = (t + 1) * P
                act.wait_ge(sem["a_nm"], i + 1)
                if i >= 2:
                    act.wait_ge(sem["a_pt"], i - 1)
                fn(a_pr[i % 2][:, 0:w], a_sm[i % 2][:, 0:w], ACT.Exp, bias=nm[:, i % 2:i % 2 + 1], scale=SCALE).then_inc(sem["a_exp"], 1)

            a_exp(0)
            for i in range(NI):
                if i + 1 < NI:
                    a_exp(i + 1)
                act.wait_ge(sem["a_pt"], i + 1)
                if i >= 2:
                    act.wait_ge(sem["a_pv"], i - 1)
                w = i % NT + 1
                act.copy(a_prT[i % 2][:, 0:w, :], bank[6][:, 0:w * P].rearrange("p (c n) -> p c n", n=P)).then_inc(sem["a_ptc"], 1)

            act.wait_ge(sem["a_o"], NI)

            def b_logits(h):
                if h >= 2:
                    act.wait_ge(sem["b_pv"], h - 1)
                act.wait_ge(sem["b_z"], h + 1)
                for j, at, w, _ in JPIECE:
                    step(fn(bz[h % 2][:, at:at + w], bank[4 * (h % 2) + j][:, 0:w], ACT.Identity, bias=sbb[:, h:h + 1], scale=SCALE))
                step(fn(bl[h % 2], bz[h % 2], ACT.Abs))
                step(fn(bl[h % 2], bl[h % 2], ACT.Exp, scale=-1.0))
                fn(bl[h % 2], bl[h % 2], ACT.Ln, bias=ones[:, 0:1]).then_inc(sem["b_l"], 1)

            b_logits(0)
            for h in range(BH):
                if h + 1 < BH:
                    b_logits(h + 1)
                act.wait_ge(sem["b_sum"], h + 1)
                fn(bl[h % 2], blb[h % 2], ACT.Exp).then_inc(sem["b_e"], 1)
                act.wait_ge(sem["b_pv"], h + 1)
                c0 = AW + h * HD
                act.copy(orow[:, 0:NT, c0:c0 + HD], bank[3][:, 0:NT * HD].rearrange("p (t n) -> p t n", n=HD)).then_inc(sem["b_o"], 1)

            fz = tt[:, 12:14, :]
            fn(ck, fz, ACT.Sigmoid, scale=-1.0)
            fn(cs_k, tts[:, 2:4, :], ACT.Sigmoid, scale=-1.0)
            step(fn(cs_lf, tts[:, 2:4, :], ACT.Sigmoid))
            act.sem_inc(sem["c_kk"], 1)
            step(fn(cx[0], fz, ACT.Abs))
            step(fn(cx[0], cx[0], ACT.Exp, scale=-1.0))
            fn(cx[0], cx[0], ACT.Ln, bias=ones[:, 0:1]).then_inc(sem["c_lf"], 1)

            act.wait_ge(sem["s_nm"], 1)
            fn(as_p, bank[2][0:48, 0:392], ACT.Exp, bias=nm[0:48, 0:1], scale=SCALE).then_inc(sem["s_exp"], 1)
            act.wait_ge(sem["pT_ps"], 1)
            act.copy(as_pT[:, 0:3, :], bank[3][:, 0:144].rearrange("p (g n) -> p g n", n=48))
            act.copy(as_pT[0:NS, 3, :], bank[3][0:NS, 144:192]).then_inc(sem["pT_ready"], 1)

            for L in range(9):
                act.wait_ge(sem["c_x"], L + 1)
                x = cx[L % 2]
                step(fn(x, cb if L == 7 else x, ACT.Abs))
                fn(x, x, ACT.Exp, scale=-1.0).then_inc(sem["c_e"], 1)
            fn(c_tot, cb.rearrange("p c (t n) -> p c t n", n=P)[:, :, :, P - 1], ACT.Exp).then_inc(sem["c_ab"], 1)
            for j in range(2):
                act.wait_ge(sem["c_kt"], j + 1)
                act.copy(c_krow[:, 4 * j:4 * j + 4, :], bank[j][:, :].rearrange("p (c n) -> p c n", n=P)).then_inc(sem["c_ktc"], 1)
            for t in range(NT):
                act.wait_ge(sem["c_pv"], 2 * t + 1)
                for two in range(2):
                    o4 = orow[:, t, 640:896].rearrange("p (c two v) -> p c two v", two=2, v=HD)[:, :, two, :]
                    last = act.copy(o4, bank[2 + 4 * two + t % 2][:, 0:256].rearrange("p (c two v) -> p c two v", two=2, v=HD)[:, :, two, :])
                last.then_inc(sem["c_raw"], 1)
            act.wait_ge(sem["c_so"], 1)
            for two in range(2):
                o4 = orow[0:NS, NT, 640:896].rearrange("p (c two v) -> p c two v", two=2, v=HD)[:, :, two, :]
                last = act.copy(o4, bank[5 - two][0:NS, 0:256].rearrange("p (c two v) -> p c two v", two=2, v=HD)[:, :, two, :])
            last.then_inc(sem["c_raw"], 1)
            act.wait_ge(sem["c_sum"], 1)
            fn(c_ss[:, 0:NT, :], c_ss[:, 0:NT, :], ACT.Sqrt, bias=eps_t, scale=1.0 / HD)
            fn(c_ss[0:NS, NT, :], c_ss[0:NS, NT, :], ACT.Sqrt, bias=eps_t[0:NS], scale=1.0 / HD).then_inc(sem["c_sqrt"], 1)

            act.wait_ge(sem["hg_out"], 16 * 6)
            for t in range(NT):
                for j in range(3):
                    act.wait_ge(sem["oT_ps"], 3 * t + j + 1)
                    w = 4 if j < 2 else 1
                    act.copy(oT[:, 4 * j:4 * j + w, cols(t)], bank[OT_BANK[j]][:, 0:P * w].rearrange("p (c n) -> p c n", n=P)).then_inc(sem["oT_evac"], 1)
            act.wait_ge(sem["oT_ps"], 13)
            act.copy(oT[:, 5:9, SEQ:TOK], bank[7][:, 0:32].rearrange("p (c n) -> p c n", n=NS))
            act.copy(oT[:, 0:5, SEQ:TOK], os_T).then_inc(sem["oT_evac"], 1)

            for j in range(32):
                half, br, m = j // 16, j // 4 % 4, j % 4
                b = bmg_t[:, br * KC + half * 4 + m:br * KC + half * 4 + m + 1]
                act.wait_ge(sem["dense_out"], GATE_OUT + 2 * j + 1)
                if j >= 2:
                    act.wait_ge(sem["m_acc"], j - 1)
                fn(sg_m[j % 2][:, row_half[0]], bank[j % 2][:, 0:HALF], ACT.Sigmoid, bias=b)
                fn(sg_m[j % 2][:, row_half[1]], bank[4 + j % 2][:, 0:HALF], ACT.Sigmoid, bias=b).then_inc(sem["m_sig"], 1)
            for k in range(2 * TILES):
                n = rows(k % TILES)
                act.wait_ge(sem["dense_out"], out_before[OUT0] + k + 1)
                if k >= 2:
                    act.wait_ge(sem["x1_ready"], k - 1)
                act.copy(mixs[k % 2][0:n, :], bank[k % 2][0:n, :]).then_inc(sem["mix_sb"], 1)
            act.wait_ge(sem["mod_gain"], 2)
            norm_stats(1)
            hT_copies(1)
            act.wait_ge(sem["r_log"], 1)
            fn(r_s[:, 0:NT, :], bank[0][:, 0:NT * NE].rearrange("p (t n) -> p t n", n=NE), ACT.Sigmoid)
            fn(r_s[0:NS, NT, :], bank[0][0:NS, NT * NE:TILES * NE], ACT.Sigmoid).then_inc(sem["r_sc"], 1)

            def sh_gate(t):
                act.wait_ge(sem["sh_gu"], t + 1)
                if t >= 2:
                    act.wait_ge(sem["sh_h"], t - 1)
                fn(sgate[t % 2][0:rows(t), :], bank[4 + t % 2][0:rows(t), 0:ED], ACT.Silu).then_inc(sem["sh_sg"], 1)

            sh_gate(0)
            for t in range(TILES):
                if t + 1 < TILES:
                    sh_gate(t + 1)
                n = rows(t)
                act.wait_ge(sem["sh_hT"], t + 1)
                act.copy(hmT[t % 2][:, :, 0:n], bank[6][:, 0:2 * n].rearrange("p (c n) -> p c n", n=n)).then_inc(sem["sh_hTc"], 1)
                act.wait_ge(sem["sh_y"], t + 1)
                act.copy(sh[0:n, t, 0:512], bank[2][0:n, :]).then_inc(sem["sh_row"], 1)

            act.wait_ge(sem["r_ready"], 2)
            act.wait_ge(sem["sh_rv"], TILES)
            last = act.value_load(be_row[0:1, MAXB:MAXB + 1], min_val=THREES_MIN - 2, max_val=MAXB // 3 - 2) + 1

            def gate(p, q):
                i = p * 3 + q
                act.wait_ge(sem["gu_done"], i + 1)
                if later(p):
                    act.wait_ge(sem["m_h"], i - 2)
                fn(sgate[q], bank[gu_bank[q]][:, 0:ED], ACT.Silu).then_inc(sem["m_sg"], 1)

            def rows_half(p, q):
                i = p * 3 + q
                act.wait_ge(sem["x_t"], i + 1)
                if later(p):
                    act.wait_ge(sem["gu_done"], i - 2)
                act.copy(xT[q][:, 0:4, :], bank[0][:, :].rearrange("p (c n) -> p c n", n=P)).then_inc(sem["x_ca"], 1)

            def result_half(p, q):
                i = p * 3 + q
                act.wait_ge(sem["dn_done"], i + 1)
                if later(p):
                    act.wait_ge(sem[f"yst{q}"], p * 16)
                act.copy(ybuf[q][:, 0:512], bank[5][:, :]).then_inc(sem["y_a"], 1)

            def middle(p, q):
                i = p * 3 + q
                act.wait_ge(sem["m_hT"], i + 1)
                if later(p):
                    act.wait_ge(sem["dn_done"], i - 2)
                act.copy(hmT[q], bank[4][:, 0:2 * P].rearrange("p (c n) -> p c n", n=P)).then_inc(sem["m_hTc"], 1)

            def block(p, q, front=True, back=True):
                gate(p, q)
                if front:
                    rows_half(*block_at(p, q, 1))
                if back:
                    result_half(*block_at(p, q, -1))
                middle(p, q)

            rows_half(0, 0)
            block(0, 0, back=False)
            for i in range(1, 6):
                block(i // 3, i % 3)
            with act.Fori(2, last) as p:
                for q in range(3):
                    block(p, q)
            for q in range(3):
                block(last, q, front=q < 2)
            result_half(last, 2)

            for t in F_ORDER:
                n = rows(t)
                for k in range(TOPK // 2):
                    ins = fn(f_dg[0:n, t, k, 0:n], ident[0:n, 0:n], ACT.Copy, scale=gates[0:n, t, TOPK // 2 + k:TOPK // 2 + k + 1])
                ins.then_inc(sem["f_diag"], 1)
            for u, t in enumerate(F_ORDER):
                act.wait_ge(sem["f_acc"], u + 1)
                dst = O["y_p"][t * P:t * P + P, :] if t < NT else O["y_s"]
                act.dma_start(dst, xr[0:rows(t), t, :]).then_inc(sem["out_done"], 16)


        @blk.vector
        def _(dve):
            step = Chain(dve, sem["dve_chain"])
            tt_, ts_, stt = dve.tensor_tensor, dve.tensor_scalar, dve.scalar_tensor_tensor

            dve.wait_ge(sem["cT_ps"], 1)
            dve.tensor_copy(cT, bank[2][:, 0:72].rearrange("p (c n) -> p c n", n=9)).then_inc(sem["cT_ready"], 1)
            dve.wait_ge(sem["const_ready"], 1)
            dve.wait_ge(sem["c_in"], 32)
            step(ts_(m_c, m_dist, 0.0, None, ALU.is_ge))
            step(ts_(m_a, m_dist, float(P), None, ALU.is_le))
            for dil in (4, 16):
                step(ts_(m_bits, m_dist, dil - 1, None, ALU.bitwise_and))
                step(ts_(m_b, m_bits, 0.0, None, ALU.is_equal))
                step(tt_(m_a, m_a, m_b, ALU.add))
            step(tt_(amult, m_a, m_c, ALU.mult))
            step(ts_(aneg, amult, 0.0, -BIG, ALU.is_equal, ALU.mult))
            step(tt_(l_x, l_t, l_s, ALU.bitwise_xor))
            step(tt_(l_gt, l_t, l_s, ALU.is_gt))
            for L, H in enumerate(LEVELS):
                step(ts_(l_sh, l_x, H.bit_length() - 1, None, ALU.logical_shift_right))
                step(ts_(l_eq, l_sh, 1.0, None, ALU.is_equal))
                step(tt_(lmask[:, L, :], l_eq, l_gt, ALU.mult))
            step(ts_(lmask[:, 7, :], l_x, 0.0, None, ALU.is_equal))
            step(tt_(tri_le, tri_lt, ident, ALU.add))

            def modulation(half):
                base = out_before[0 if half == 0 else ADA2]
                for g in range(6):
                    dve.wait_ge(sem["dense_out"], base + g + 1)
                    if g == 0:
                        dve.wait_ge(sem["bada_in"], 32 * (half + 1))
                    s, c = g // 2, g % 2 * PANEL
                    tt_(mod_sb[0:9, s, c:c + PANEL], bank[(base + g) % 2][0:9, :], bada[:, s, c:c + PANEL], ALU.add).then_inc(sem["dense_evac"], 1)
                dve.wait_ge(sem["dense_evac"], 6 if half == 0 else 6 + 7 * TILES + 6)
                stt(out=mod_sb[0:9, 1, :], in0=mod_sb[0:9, 1, :], scalar=1.0, in1=g9, op0=ALU.add, op1=ALU.mult).then_inc(sem["mod_gain"], 1)

            def norm_rows(half):
                base = half * TILES
                for t in range(TILES):
                    n = rows(t)
                    dve.wait_ge(sem["rstd_sqrt"], base + t + 1)
                    step(dve.reciprocal(rstd[0:n, t:t + 1], rstd[0:n, t:t + 1]))
                    if t == 0:
                        dve.wait_ge(sem["bc_ps"], half + 1)
                        dve.wait_ge(sem["mod_gain"], half + 1)
                    if t >= 2:
                        dve.wait_ge(sem["h_ps"], 2 * (base + t - 1))
                        if half == 1:
                            dve.wait_ge(sem[f"hro{t % 2}"], 16 * (t // 2))
                    h = hrow[t % 2]
                    for c in range(2):
                        cc = slice(c * 512, c * 512 + 512)
                        gain = bank[4 + c][:, :] if t < NT else mod_sb[0:NS, 1, cc]
                        shift = bank[6 + c][:, :] if t < NT else mod_sb[0:NS, 0, cc]
                        step(stt(out=h[0:n, cc], in0=xr[0:n, t, cc], scalar=rstd[0:n, t:t + 1], in1=gain, op0=ALU.mult, op1=ALU.mult))
                        last = tt_(h[0:n, cc], h[0:n, cc], shift, ALU.add)
                        if c == 0:
                            step(last)
                    last.then_inc(sem["h_row"], 1)

            modulation(0)
            dve.wait_ge(sem["small_ps"], 1)
            dve.tensor_copy(bmg_t, bank[3][:, 0:32])
            dve.tensor_copy(sgu_bt, bank[3][:, 32:36])
            for g in range(DG):
                last = tt_(sgu_wt[:, g, :], bank[4][:, g * P:(g + 1) * P], tri_le, ALU.mult)
            last.then_inc(sem["small_ready"], 1)
            norm_rows(0)
            dve.wait_ge(sem["params_in"], 16 * NPARAM)
            step(ts_(q4, q4, 3, None, ALU.bitwise_and))
            step(ts_(q4, q4, 2, None, ALU.logical_shift_left))
            step(ts_(pt_sb, pt_sb, 4, None, ALU.logical_shift_left))
            step(tt_(pt_sb, pt_sb, q4.to_broadcast([P, NS]), ALU.add))
            for c in range(4):
                step(ts_(idx_kv[:, :, c], pt_sb, float(c), None, ALU.add))
            dve.sem_inc(sem["idx_ready"], 1)

            d8 = ident[0:NS, 0:NS]
            dve.wait_ge(sem["h_ps"], 2 * TILES)
            dve.wait_ge(sem["dense_evac"], 6 + TILES)
            tt_(bs_qd, pqk[0:NS, NT, 768:1024].unsqueeze(1).to_broadcast([NS, NS, BW]), d8.unsqueeze(2).to_broadcast([NS, NS, BW]), ALU.mult).then_inc(sem["bs_qd"], 1)
            for n in range(32):
                b, c = n // 4, n % 4
                if c == 0:
                    dve.wait_ge(sem["qb_ps"], b + 1)
                dve.wait_ge(sem[f"gather{n % 3}"], 16 * (n // 3 + 1))
                q = bank[4 + b % 2][:, 0:BW].unsqueeze(1).to_broadcast([P, 8, BW])
                tt_(bs_prod, key_slot[n % 3], q, ALU.mult).then_inc(sem["kvk_used"], 1)
                dve.wait_ge(sem["kvk_used"], n + 1)
                step(dve.tensor_reduce(bs_z[:, b, 8 * c:8 * c + 8, :], bs_prod.rearrange("p r (h d) -> p r h d", d=HD), AX, ALU.add))
            flat = lambda v: v.rearrange("p b r h -> p (b r) h")
            stt(out=flat(bs_z), in0=flat(bs_z), scalar=SCALE, in1=sbb.unsqueeze(1).to_broadcast([P, NS * 32, BH]), op0=ALU.mult, op1=ALU.add).then_inc(sem["bs_z"], 1)

            dve.wait_ge(sem["h_ps"], 2 * TILES)
            for t in range(TILES):
                n = rows(t)
                qk = pqk[0:n, t, 0:768]
                qk3 = qk.rearrange("p (h d) -> p h d", d=HD)
                dve.wait_ge(sem["dense_evac"], 6 + 2 * TILES + t + 1)
                if t:
                    dve.wait_ge(sem["qk_sum"], t)
                step(tt_(qk_sq[0:n], qk, qk, ALU.mult))
                dve.tensor_reduce(qk_ss[0:n, t, :], qk_sq[0:n].rearrange("p (h d) -> p h d", d=HD), AX, ALU.add).then_inc(sem["qk_sum"], 1)
            one = lambda v: v.rearrange("p b r h -> p (b r h)")
            dve.wait_ge(sem["bs_l"], 1)
            step(stt(out=one(bs_lb), in0=one(bs_z), scalar=0.0, in1=one(bs_l), op0=ALU.min, op1=ALU.subtract))
            step(tt_(one(bs_z), one(bs_lb), one(bs_z), ALU.subtract))
            dve.memset(bs_e[0][:, :, 31:32, :], 0.0)
            step(dve.tensor_copy(bs_e[0][:, :, 0:31, :], bs_z[:, :, 1:32, :]))
            for k, s in enumerate((1, 2, 4, 8, 16)):
                a, b = bs_e[k % 2], bs_e[(k + 1) % 2]
                dve.tensor_copy(b[:, :, 32 - s:32, :], a[:, :, 32 - s:32, :])
                step(tt_(b[:, :, 0:32 - s, :], a[:, :, 0:32 - s, :], a[:, :, s:32, :], ALU.add))
            tt_(bs_tot, bs_e[1][:, :, 0, :], bs_z[:, :, 0, :], ALU.add).then_inc(sem["bs_tot"], 1)
            dve.wait_ge(sem["bs_tot"], 1)
            step(tt_(one(bs_e[1]), one(bs_e[1]), one(bs_lb), ALU.add))
            for t in range(TILES):
                n = rows(t)
                qk3 = pqk[0:n, t, 0:768].rearrange("p (h d) -> p h d", d=HD)
                dve.wait_ge(sem["qk_sqrt"], t + 1)
                step(dve.reciprocal(qk_ss[0:n, t, :], qk_ss[0:n, t, :]))
                step(tt_(qk3, qk3, qk_ss[0:n, t, :].unsqueeze(2).to_broadcast([n, 12, HD]), ALU.mult))
                for k in range(2):
                    part = qk3[:, AH * k:AH * k + AH, :]
                    last = tt_(part, part, qk_g[0:n, k:k + 1, :].to_broadcast([n, AH, HD]), ALU.mult)
                last.then_inc(sem["qk_norm"], 1)
            dve.wait_ge(sem["qk_norm"], TILES)
            step(dve.tensor_copy(rows_s[0:NS, :], pqk[0:NS, NT, 0:1024]))

            dve.wait_ge(sem["bs_cross"], 1)
            cross = bank[6][:, 0:32].rearrange("p (b h) -> p b h", h=BH).unsqueeze(2).to_broadcast([P, NS, 32, BH])
            tt_(bs_e[1], bs_e[1], cross, ALU.add).then_inc(sem["bs_e"], 1)

            dve.wait_ge(sem["rows_out"], 16 * 8)
            dve.wait_ge(sem["t_ps"], 17)
            NI = AH * NT

            def a_front(i):
                t = i % NT
                w = (t + 1) * P
                b = i % 2
                dve.wait_ge(sem["a_s"], i + 1)
                if i >= 2:
                    dve.wait_ge(sem["a_exp"], i - 1)
                neg = aneg.rearrange("p a j -> p (a j)")[:, SEQ - w:SEQ]
                step(tt_(a_sm[b][:, 0:w], bank[4 + b][:, 0:w], neg, ALU.add))
                step(dve.tensor_reduce(nm[:, b:b + 1], a_sm[b][:, 0:w], AX, ALU.max))
                ts_(nm[:, b:b + 1], nm[:, b:b + 1], -SCALE, None, ALU.mult).then_inc(sem["a_nm"], 1)

            def a_out(i):
                b = i % 2
                c0 = i // NT * HD
                dve.wait_ge(sem["a_pv"], i + 1)
                ts_(orow[:, i % NT, c0:c0 + HD], bank[7 - 4 * b][:, 0:HD], den[:, b:b + 1], None, ALU.mult).then_inc(sem["a_o"], 1)

            def bs_values(m):
                dve.wait_ge(sem["kvv_used"], 8 * (m + 1))
                dve.tensor_copy(bs_ov[:, 2 * m:2 * m + 2, :], bank[BS_BANK[m]][0:BH, :].rearrange("p (b n) -> p b n", n=BW)).then_inc(sem["bs_ov"], 1)

            a_front(0)
            for i in range(NI):
                if i + 1 < NI:
                    a_front(i + 1)
                if i >= 2:
                    dve.wait_ge(sem["a_o"], i - 1)
                b, w = i % 2, (i % NT + 1) * P
                mult = amult.rearrange("p a j -> p (a j)")[:, SEQ - w:SEQ]
                dve.wait_ge(sem["a_exp"], i + 1)
                step(stt(out=a_pr[b][:, 0:w], in0=a_pr[b][:, 0:w], scalar=1.0, in1=mult, op0=ALU.mult, op1=ALU.mult, accum_out=den[:, b:b + 1]))
                dve.reciprocal(den[:, b:b + 1], den[:, b:b + 1]).then_inc(sem["a_p"], 1)
                if i >= 1:
                    a_out(i - 1)
                if i in (10, 18):
                    bs_values(i // 8 - 1)
            a_out(NI - 1)
            bs_values(2)

            def b_front(h):
                s = h % 2
                dve.wait_ge(sem["b_l"], h + 1)
                step(stt(out=blb[s], in0=bz[s], scalar=0.0, in1=bl[s], op0=ALU.min, op1=ALU.subtract))
                step(tt_(bz[s], blb[s], bz[s], ALU.subtract))
                for j in range(NT):
                    last = tt_(bz[s][:, JO[j]:JO[j] + P], bz[s][:, JO[j]:JO[j] + P], tri_lt, ALU.mult)
                last.then_inc(sem["b_lk"], 1)

            def b_back(h):
                s = h % 2
                dve.wait_ge(sem["b_after"], h + 1)
                for j, at, w, _ in JPIECE:
                    last = tt_(blb[s][:, at:at + w], blb[s][:, at:at + w], bank[4 * s + j][:, 0:w], ALU.add)
                last.then_inc(sem["b_sum"], 1)
                dve.wait_ge(sem["b_e"], h + 1)
                for j in range(NT):
                    last = tt_(bl[s][:, JO[j]:JO[j] + P], bl[s][:, JO[j]:JO[j] + P], tri_lt, ALU.mult)
                last.then_inc(sem["b_a"], 1)

            b_front(0)
            for h in range(BH):
                if h + 1 < BH:
                    b_front(h + 1)
                b_back(h)
            bs_values(3)
            dve.wait_ge(sem["bs_pv"], 1)
            for hp in range(2):
                for j in range(2):
                    last = dve.tensor_copy(os_T[j * HD:j * HD + HD, 3 + hp, :],
                                           bank[6][j * HD:j * HD + HD, 0:64].rearrange("p (b hp h) -> p b hp h", hp=2, h=BH)[:, :, hp, 2 * hp + j])
            step(last)

            dve.wait_ge(sem["b_o"], BH)
            tt_(as_qd, rows_s[0:NS, 0:AW].unsqueeze(1).to_broadcast([NS, NS, AW]), d8.unsqueeze(2).to_broadcast([NS, NS, AW]), ALU.mult).then_inc(sem["qd_ready"], 1)
            step(tt_(as_own, rows_s[0:NS, 0:AW], rows_s[0:NS, AW:2 * AW], ALU.mult))
            step(dve.tensor_reduce(as_tmp, as_own.rearrange("p (h d) -> p h d", d=HD), AX, ALU.add))
            step(ts_(as_self, d8.unsqueeze(2).to_broadcast([NS, NS, AH]), BIG, -BIG, ALU.mult, ALU.add))
            step(tt_(as_self, as_self, as_tmp.unsqueeze(1).to_broadcast([NS, NS, AH]), ALU.add))
            for b in range(NS):
                dve.wait_ge(sem["qb_ps"], NS + b + 1)
                dve.wait_ge(sem[f"kv{b % 4}"], 48 * (b // 4 + 1))
                tt_(as_prod, view(kvbuf[b % 4], [3, AW]), bank[b % 2][:, 0:AW].unsqueeze(1).to_broadcast([P, 3, AW]), ALU.mult).then_inc(sem["kvk_used"], 1)
                dve.wait_ge(sem["kvk_used"], 32 + b + 1)
                step(dve.tensor_reduce(as_s[:, :, b * AH:(b + 1) * AH], as_prod.rearrange("p g (h d) -> p g h d", d=HD), AX, ALU.add))
            dve.sem_inc(sem["as_used"], 1)
            dve.wait_ge(sem["sT_ps"], 1)
            step(dve.tensor_reduce(nm[0:48, 0:1], bank[2][0:48, 0:392], AX, ALU.max))
            ts_(nm[0:48, 0:1], nm[0:48, 0:1], -SCALE, None, ALU.mult).then_inc(sem["s_nm"], 1)
            dve.wait_ge(sem["s_exp"], 1)
            step(ts_(as_p[:, 384:392], as_p[:, 384:392], float(GROUPS_A), None, ALU.mult))
            step(dve.tensor_reduce(den[0:48, 0:1], as_p, AX, ALU.add))
            step(dve.reciprocal(den[0:48, 0:1], den[0:48, 0:1]))
            ts_(as_p, as_p, den[0:48, 0:1], None, ALU.mult).then_inc(sem["s_norm"], 1)

            fz = tt[:, 12:14, :]
            dve.wait_ge(sem["c_lf"], 1)
            step(stt(out=fz, in0=fz, scalar=0.0, in1=cx[0], op0=ALU.min, op1=ALU.subtract))
            for c in range(2):
                for t in range(NT):
                    step(dve.tensor_tensor_scan(out=cb[:, c, cols(t)], data0=ones, data1=fz[:, c, cols(t)], initial=0.0, op0=ALU.mult, op1=ALU.add))
            flatc = lambda v: v.rearrange("p c n -> p (c n)")
            qz = tt[:, 10:12, :]
            step(dve.memset(c_att, 0.0))

            def c_decay(L):
                if L == 7:
                    dve.sem_inc(sem["c_x"], 1)
                    return
                H = LEVELS[L] if L < 7 else P
                b2 = 2 * H if L < 7 else P
                blocks = flatc(cb).rearrange("p (m w) -> p m w", w=b2)
                ref = blocks[:, :, H - 1:H].to_broadcast([P, 2 * SEQ // b2, b2])
                tt_(flatc(cx[L % 2]).rearrange("p (m w) -> p m w", w=b2), blocks, ref, ALU.subtract).then_inc(sem["c_x"], 1)

            def c_copies(L):
                dve.wait_ge(sem["c_lev"], L + 1)
                if L:
                    dve.wait_ge(sem["c_cp"], 4 * L)
                for h in range(CH):
                    dve.copy_predicated(c_att[:, h, :, :], lmask[:, L:L + 1, :].to_broadcast([P, NT, P]),
                                        bank[4 * (L % 2) + h][:, :].rearrange("p (t n) -> p t n", n=P)).then_inc(sem["c_cp"], 1)

            c_decay(0)
            for L in range(9):
                if L < 8:
                    if L >= 1:
                        dve.wait_ge(sem["c_q"], L)
                        dve.wait_ge(sem["c_k"], L)
                    c_decay(L + 1)
                    dve.wait_ge(sem["c_e"], L + 1)
                    if L >= 2:
                        dve.wait_ge(sem["c_lev"], L - 1)
                    tt_(cq1[L % 2], qz, cx[L % 2], ALU.mult).then_inc(sem["c_q"], 1)
                if L == 1:
                    for b in range(NS):
                        dve.wait_ge(sem["kvv_used"], 32 + b + 1)
                        dve.tensor_copy(as_ov[b], bank[b][0:AH, 0:AW]).then_inc(sem["as_ov"], 1)
                    dve.wait_ge(sem["as_pv"], 1)
                    for j in range(2):
                        last = dve.tensor_copy(os_T[j * HD:j * HD + HD, 0:3, :].rearrange("p c b -> p b c"),
                                               bank[0][j * HD:j * HD + HD, 0:3 * 48].rearrange("p (b x) -> p b x", x=3 * AH)[:, :, j:j + 2 * AH + 5:AH + 2])
                    last.then_inc(sem["as_o"], 1)
                if L >= 1:
                    c_copies(L - 1)
            dve.wait_ge(sem["c_ab"], 1)
            for t in range(NT):
                dve.wait_ge(sem["c_pv"], 2 * t + 2)
                for hp in range(2):
                    u = bank[4 + t % 2][:, hp * HD:(hp + 1) * HD]
                    if t == 0:
                        last = dve.tensor_copy(c_S[:, hp, :], u)
                    else:
                        last = stt(out=c_S[:, hp, :], in0=c_S[:, hp, :], scalar=c_tot[:, hp, t:t + 1], in1=u, op0=ALU.mult, op1=ALU.add)
                last.then_inc(sem["c_s"], 1)
                dve.wait_ge(sem["c_s"], t + 1)
            dve.wait_ge(sem["s0_in"], 32)
            vc = pv[0:NS, NT, 640:896].rearrange("p (h v) -> p h v", v=HD)
            step(tt_(c_qd, tts[:, 0:2, :].unsqueeze(2).to_broadcast([P, 2, NS, NS]), d88.unsqueeze(1).to_broadcast([P, 2, NS, NS]), ALU.mult))
            for hp in range(2):
                if hp:
                    dve.wait_ge(sem["c_vb"], 1)
                for two in range(2):
                    last = tt_(c_vdiag[:, two, :, :], vc[:, 2 * hp + two:2 * hp + two + 1, :].to_broadcast([NS, NS, HD]), d8.unsqueeze(2).to_broadcast([NS, NS, HD]), ALU.mult)
                last.then_inc(sem["c_vd"], 1)
                step(tt_(c_new[:, :, hp, :], c_S0[:, :, hp, :], cs_lf[:, hp, :].unsqueeze(2).to_broadcast([P, NS, HD]), ALU.mult))
                dve.wait_ge(sem["c_vb"], hp + 1)
                vb = bank[6 + hp][:, :].rearrange("p (b v) -> p b v", v=HD)
                step(tt_(cs_tmp, vb, cs_k[:, hp, :].unsqueeze(2).to_broadcast([P, NS, HD]), ALU.mult))
                tt_(c_new[:, :, hp, :], c_new[:, :, hp, :], cs_tmp, ALU.add).then_inc(sem["c_new"], 1)
                dve.wait_ge(sem["c_new"], hp + 1)
            for t in range(TILES):
                n = rows(t)
                dve.wait_ge(sem["c_raw"], t + 1)
                o3 = orow[0:n, t, 640:896].rearrange("p (h v) -> p h v", v=HD)
                step(tt_(c_sq[0:n], o3, o3, ALU.mult))
                last = dve.tensor_reduce(c_ss[0:n, t, :], c_sq[0:n], AX, ALU.add)
                if t < TILES - 1:
                    step(last)
            last.then_inc(sem["c_sum"], 1)
            dve.wait_ge(sem["c_sqrt"], 1)
            for t in range(TILES):
                n = rows(t)
                o3 = orow[0:n, t, 640:896].rearrange("p (h v) -> p h v", v=HD)
                step(dve.reciprocal(c_ss[0:n, t, :], c_ss[0:n, t, :]))
                step(tt_(o3, o3, c_ss[0:n, t, :].unsqueeze(2).to_broadcast([n, CH, HD]), ALU.mult))
                step(tt_(o3, o3, co_g[0:n].unsqueeze(1).to_broadcast([n, CH, HD]), ALU.mult))
                step(tt_(orow[0:n, t, 640:896], orow[0:n, t, 640:896], pv[0:n, t, 896:1152], ALU.mult))
            dve.wait_ge(sem["d_gelu"], 1)
            od = orow[0:NS, NT, 896:1152].rearrange("p (g v) -> p g v", v=HD)
            vd = pv[0:NS, NT, 1408:1664].rearrange("p (g v) -> p g v", v=HD)
            step(tt_(od, vd, w00[0:NS].unsqueeze(2).to_broadcast([NS, DG, HD]), ALU.mult))
            step(tt_(od, od, b00[0:NS].unsqueeze(2).to_broadcast([NS, DG, HD]), ALU.add))
            step(tt_(orow[0:NS, NT, 896:1152], orow[0:NS, NT, 896:1152], pv[0:NS, NT, 1152:1408], ALU.mult))
            dve.wait_ge(sem["d_mix"], 1)
            for g in range(DG):
                mixed = bank[6 + g // 2][:, 256 * (g % 2):256 * (g % 2) + 256].rearrange("p (t v) -> p t v", v=HD)
                last = stt(out=orow[:, 0:NT, 896 + g * HD:960 + g * HD], in0=mixed, scalar=sgu_bt[:, g:g + 1],
                           in1=pv[:, 0:NT, 1152 + g * HD:1216 + g * HD], op0=ALU.add, op1=ALU.mult)
            last.then_inc(sem["d_o"], 1)

            for j in range(32):
                half, br, m = j // 16, j // 4 % 4, j % 4
                dve.wait_ge(sem["m_sig"], j + 1)
                dve.wait_ge(sem["dense_out"], GATE_OUT + 2 * j + 2)
                out = mT[:, half * 4 + m, :] if br == 0 else tmp_m
                for i, part in enumerate(row_half):
                    last = tt_(out[:, part], sg_m[j % 2][:, part], bank[2 + 4 * i + j % 2][:, 0:HALF], ALU.mult)
                    if br and i == 0:
                        step(last)
                if br:
                    step(last)
                    last = tt_(mT[:, half * 4 + m, :], mT[:, half * 4 + m, :], tmp_m, ALU.add)
                last.then_inc(sem["m_acc"], 1)
                dve.wait_ge(sem["m_acc"], j + 1)
            dve.wait_ge(sem["x2_in"], 32)
            dve.wait_ge(sem["g_ps"], 1)
            for k in range(2 * TILES):
                c, t = k // TILES, k % TILES
                n, cc = rows(t), slice(c * 512, c * 512 + 512)
                dve.wait_ge(sem["mix_sb"], k + 1)
                g = bank[6 + c][:, :] if t < NT else mod_sb[0:NS, 2, cc]
                step(tt_(mixt[0:n], mixs[k % 2][0:n], g, ALU.mult))
                tt_(xr[0:n, t, cc], xr[0:n, t, cc], mixt[0:n], ALU.add).then_inc(sem["x1_ready"], 1)
                dve.wait_ge(sem["x1_ready"], k + 1)
            modulation(1)
            norm_rows(1)

            dve.wait_ge(sem["r_sc"], 1)
            step(dve.memset(r_M[:, NT, :], 0.0))
            def sh_mid(t):
                n = rows(t)
                dve.wait_ge(sem["sh_sg"], t + 1)
                if t >= 2:
                    dve.wait_ge(sem["sh_hT"], t - 1)
                tt_(hmid[t % 2][0:n], sgate[t % 2][0:n], bank[4 + t % 2][0:n, ED:2 * ED], ALU.mult).then_inc(sem["sh_h"], 1)

            def sh_result(t):
                dve.wait_ge(sem["sh_y"], t + 1)
                dve.tensor_copy(sh[0:rows(t), t, 512:1024], bank[3][0:rows(t), :]).then_inc(sem["sh_rv"], 1)

            for t in range(TILES):
                n = rows(t)
                c3 = r_c[0:n, t, :].rearrange("p (g e) -> p g e", e=NE // EG)
                step(tt_(r_c[0:n, t, :], r_s[0:n, t, :], brt[0:n], ALU.add))
                for g in range(EG):
                    last = dve.max(r_m8[0:n, g, :], c3[:, g, :])
                step(last)
                step(tt_(r_g[0:n], r_m8[0:n, :, 0], r_m8[0:n, :, 1], ALU.add))
                step(dve.max(r_g8[0:n], r_g[0:n]))
                step(dve.max_index(r_gi[0:n], r_g8[0:n], r_g[0:n]))
                step(dve.tensor_copy(r_gf[0:n], r_gi[0:n]))
                step(tt_(r_eq[0:n], iota_e[0:n, 0:EG].unsqueeze(2).to_broadcast([n, EG, TOPG]), r_gf[0:n, 0:TOPG].unsqueeze(1).to_broadcast([n, EG, TOPG]), ALU.is_equal))
                step(dve.tensor_reduce(r_gm[0:n], r_eq[0:n], AX, ALU.max))
                step(ts_(r_gm[0:n], r_gm[0:n], BIG, -BIG, ALU.mult, ALU.add))
                mc3 = r_mc[0:n].rearrange("p (g e) -> p g e", e=NE // EG)
                step(tt_(mc3, c3, r_gm[0:n].unsqueeze(2).to_broadcast([n, EG, NE // EG]), ALU.add))
                step(dve.max(r_t8[0:n], r_mc[0:n]))
                step(dve.max_index(r_ti[0:n], r_t8[0:n], r_mc[0:n]))
                step(dve.tensor_copy(r_tf[0:n], r_ti[0:n]))
                oh = onehot[0:n, t, :, :]
                step(tt_(oh, iota_e[0:n].unsqueeze(1).to_broadcast([n, TOPK, NE]), r_tf[0:n].unsqueeze(2).to_broadcast([n, TOPK, NE]), ALU.is_equal))
                step(tt_(r_prod[0:n], oh, r_s[0:n, t, :].unsqueeze(1).to_broadcast([n, TOPK, NE]), ALU.mult))
                step(dve.tensor_reduce(gates[0:n, t, :], r_prod[0:n], AX, ALU.add))
                step(dve.tensor_reduce(r_sum[0:n], gates[0:n, t, :], AX, ALU.add))
                step(dve.reciprocal(r_sum[0:n], r_sum[0:n]))
                step(ts_(gates[0:n, t, :], gates[0:n, t, :], r_sum[0:n], ROUTE_SCALE, ALU.mult, ALU.mult))
                dve.tensor_reduce(r_M[0:n, t, :], oh.rearrange("p k e -> p e k"), AX, ALU.add).then_inc(sem["r_mask"], 1)
                sh_mid(t)
                if t:
                    sh_result(t - 1)
            sh_result(TILES - 1)
            dve.wait_ge(sem["r_pos"], 1)
            step(ts_(r_cnt, bank[1][:, 320:384], float(P - 1), None, ALU.add))
            step(dve.tensor_copy(r_cnti, r_cnt))
            step(ts_(r_cnti, r_cnti, 7, None, ALU.logical_shift_right))
            step(dve.tensor_copy(r_nb, r_cnti))
            step(dve.tensor_tensor_scan(out=r_end, data0=ones[:, 0:NE], data1=r_nb, initial=0.0, op0=ALU.mult, op1=ALU.add))
            step(tt_(r_st, r_end, r_nb, ALU.subtract))
            step(ts_(r_st, r_st, float(P), None, ALU.mult))
            step(ts_(r_mc, r_end, pcol, None, ALU.is_le))
            step(dve.tensor_reduce(r_be, r_mc, AX, ALU.add))
            ts_(r_be, r_be, float(NE - 1), None, ALU.min).then_inc(sem["r_tab_in"], 1)
            for t in range(TILES):
                n = rows(t)
                oh = onehot[0:n, t, :, :]
                step(tt_(r_mc[0:n], bank[1][0:n, t * NE:(t + 1) * NE], r_st[0:n], ALU.add))
                step(tt_(r_prod[0:n], oh, r_mc[0:n].unsqueeze(1).to_broadcast([n, TOPK, NE]), ALU.mult))
                step(dve.tensor_reduce(r_d[0:n], r_prod[0:n], AX, ALU.add))
                step(dve.tensor_copy(dest_i[0:n, t, :], r_d[0:n]))
                step(ts_(r_dv[0:n], dest_i[0:n, t, :], P - 1, None, ALU.bitwise_and))
                step(dve.tensor_copy(r_f8[0:n], r_dv[0:n]))
                if t:
                    dve.wait_ge(sem["r_tab"], t + 1)
                step(tt_(r_hs[0:n], iota_s[0:n].unsqueeze(1).to_broadcast([n, TOPK, P]), r_f8[0:n].unsqueeze(2).to_broadcast([n, TOPK, P]), ALU.is_equal))
                step(ts_(r_dv[0:n], dest_i[0:n, t, :], 7, None, ALU.logical_shift_right))
                step(dve.tensor_copy(r_f8[0:n], r_dv[0:n]))
                step(tt_(r_hb[0:n], iota_b[0:n].unsqueeze(1).to_broadcast([n, TOPK, MAXB]), r_f8[0:n].unsqueeze(2).to_broadcast([n, TOPK, MAXB]), ALU.is_equal))
                tt_(r_hb[0:n], r_hb[0:n], row_code[0:n, t, :].unsqueeze(2).to_broadcast([n, TOPK, MAXB]), ALU.mult).then_inc(sem["r_tab_in"], 1)
                dve.wait_ge(sem["r_tab_in"], t + 2)
                if t == 0:
                    dve.wait_ge(sem["r_tab"], 1)
                    step(dve.tensor_copy(be_row[:, 0:MAXB], bank[0][0:1, 0:MAXB]))
                    step(ts_(r_sum[0:1], r_end[0:1, NE - 1:NE], 2.0, 43.0, ALU.add, ALU.mult))
                    step(dve.tensor_copy(be_row[:, MAXB:MAXB + 1], r_sum[0:1]))
                    step(ts_(be_row[:, MAXB:MAXB + 1], be_row[:, MAXB:MAXB + 1], 7, None, ALU.logical_shift_right))
                    ts_(be_row[:, MAXB:MAXB + 1], be_row[:, MAXB:MAXB + 1], -2.0, None, ALU.add).then_inc(sem["r_ready"], 1)
            dve.wait_ge(sem["r_tab"], TILES + 1)
            step(ts_(slot_row, bank[7][:, 0:MAXB], -1.0, float(TOK * TOPK), ALU.mult, ALU.add))
            ts_(slot_tok, slot_row, 3, None, ALU.logical_shift_right).then_inc(sem["r_ready"], 1)

            dve.wait_ge(sem["r_ready"], 2)
            dve.wait_ge(sem["sh_row"], TILES)
            last = dve.value_load(be_row[0:1, MAXB:MAXB + 1], min_val=THREES_MIN - 2, max_val=MAXB // 3 - 2) + 1

            def middle(p, q):
                i = p * 3 + q
                dve.wait_ge(sem["m_sg"], i + 1)
                if later(p):
                    dve.wait_ge(sem["m_hT"], i - 2)
                tt_(hmid[q], sgate[q], bank[gu_bank[q]][:, ED:2 * ED], ALU.mult).then_inc(sem["m_h"], 1)

            def rows_half(p, q):
                i = p * 3 + q
                dve.wait_ge(sem["x_t"], i + 1)
                if later(p):
                    dve.wait_ge(sem["gu_done"], i - 2)
                dve.tensor_copy(xT[q][:, 4:8, :], bank[1][:, :].rearrange("p (c n) -> p c n", n=P)).then_inc(sem["x_cv"], 1)

            def result_half(p, q):
                i = p * 3 + q
                dve.wait_ge(sem["dn_done"], i + 1)
                if later(p):
                    dve.wait_ge(sem[f"yst{q}"], p * 16)
                dve.tensor_copy(ybuf[q][:, 512:1024], bank[6][:, :]).then_inc(sem["y_v"], 1)

            def block(p, q, front=True, back=True):
                middle(p, q)
                if front:
                    rows_half(*block_at(p, q, 1))
                if back:
                    result_half(*block_at(p, q, -1))

            rows_half(0, 0)
            block(0, 0, back=False)
            for i in range(1, 6):
                block(i // 3, i % 3)
            with dve.Fori(2, last) as p:
                for q in range(3):
                    block(p, q)
            for q in range(3):
                block(last, q, front=q < 2)
            result_half(last, 2)

            dve.wait_ge(sem["g_ps"], 2)
            for u, t in enumerate(F_ORDER):
                m = rows(t)
                for k in range(TOPK // 2):
                    if k % 2 == 0:
                        name, before = f_sem[u % 2][k // 2]
                        dve.wait_ge(sem[name], before + 16 * (u // 2 + 1))
                    stt(out=sh[0:m, t, :], in0=fbuf[u % 2][k // 2][0:m, k % 2, :], scalar=gates[0:m, t, k:k + 1], in1=sh[0:m, t, :], op0=ALU.mult, op1=ALU.add).then_inc(sem["f_used"], 1)
                    dve.wait_ge(sem["f_used"], TOPK // 2 * u + k + 1)
                dve.wait_ge(sem["f_pe"], 2 * (u + 1))
                for c in range(2):
                    cc = slice(c * 512, c * 512 + 512)
                    g = bank[c][:, :] if t < NT else mod_sb[0:NS, 2, cc]
                    step(tt_(sh[0:m, t, cc], sh[0:m, t, cc], bank[F_BANK[u % 2][c]][0:m, :], ALU.add))
                    step(tt_(sh[0:m, t, cc], sh[0:m, t, cc], g, ALU.mult))
                tt_(xr[0:m, t, :], xr[0:m, t, :], sh[0:m, t, :], ALU.add).then_inc(sem["f_acc"], 1)


        @blk.tensor
        def _(pe):
            mm, tr = pe.matmul, pe.transpose

            def panel_wait(i, n=1):
                pe.wait_ge(sem[f"w_in{i % 2}"], 16 * (i // 2 + n))

            pe.wait_ge(sem["const_ready"], 1)
            pe.wait_ge(sem["silu_c"], 1)
            for c in range(KC):
                last = tr(bank[2][:, c * 9:(c + 1) * 9], cs[:, c * P:(c + 1) * P], ident[0:9, 0:9])
            last.then_inc(sem["cT_ps"], 1)
            pe.wait_ge(sem["cT_ready"], 1)

            def modulation(half):
                first = 0 if half == 0 else ADA2
                for g in range(6):
                    i = first + g
                    k = out_before[i]
                    panel_wait(i)
                    if half == 1 and g < 2:
                        pe.wait_ge(sem["mix_sb"], 2 * TILES)
                    if g >= 2:
                        pe.wait_ge(sem["dense_evac"], (0 if half == 0 else 6 + 7 * TILES) + g - 1)
                    for c in range(KC):
                        last = mm(bank[k % 2][0:9, :], cT[:, c, :], panel[i % 2][:, c, :], start=(c == 0), stop=(c == KC - 1))
                    last.then_inc(sem["dense_out"], 1)
                if half == 0:
                    pe.wait_ge(sem["params_in"], 16 * NPARAM)
                    tr(bank[3][:, 0:32], bmg_r, ident[0:32, 0:32])
                    tr(bank[3][:, 32:36], sgub_r, ident[0:4, 0:4])
                    for g in range(DG):
                        last = tr(bank[4][:, g * P:(g + 1) * P], sguw_r[:, g, :], ident)
                    last.then_inc(sem["small_ps"], 1)
                pe.wait_ge(sem["mod_gain"], half + 1)
                if half == 0:
                    pe.wait_ge(sem["small_ready"], 1)
                else:
                    pe.wait_ge(sem["x1_ready"], 2 * TILES)
                for s, b in ((1, 4), (0, 6)):
                    for c in range(2):
                        last = mm(bank[b + c][:, :], sel9[0:9, :], mod_sb[0:9, s, c * 512:c * 512 + 512], start=True, stop=True)
                last.then_inc(sem["bc_ps"], 1)

            def transposed_rows(half, product):
                for t in range(TILES):
                    n = rows(t)
                    pe.wait_ge(sem["h_row"], half * TILES + t + 1)
                    for j in range(2):
                        if t or half:
                            pe.wait_ge(sem["hT_evac"], 2 * (half * TILES + t - 1) + j + 1)
                        for c in range(4):
                            d = (4 * j + c) * P
                            last = tr(bank[2 + j][:, c * n:(c + 1) * n], hrow[t % 2][0:n, d:d + P], ident[0:n, 0:n])
                        last.then_inc(sem["h_ps"], 1)
                    if t:
                        product(t - 1)
                product(TILES - 1)

            def projection(i, t):
                w = min(PANEL, IN_W - IN_ORDER[i] * PANEL)
                k = IN0_OUT + i * TILES + t
                if t == 0:
                    panel_wait(IN0 + i)
                if i == 0:
                    pe.wait_ge(sem["hT_evac"], 2 * (t + 1))
                if k - IN0_OUT >= 2:
                    pe.wait_ge(sem["dense_evac"], k - 1)
                for c in range(KC):
                    last = mm(bank[k % 2][0:rows(t), 0:w], hT[:, c, cols(t)], panel[(IN0 + i) % 2][:, c, 0:w], start=(c == 0), stop=(c == KC - 1))
                last.then_inc(sem["dense_out"], 1)

            modulation(0)
            transposed_rows(0, lambda t: projection(0, t) if t < 2 else None)

            def bs_spread(b):
                if b == 0:
                    pe.wait_ge(sem["bs_qd"], 1)
                if b >= 2:
                    pe.wait_ge(sem["kvk_used"], 4 * (b - 1))
                mm(bank[4 + b % 2][:, 0:BW], ones[0:NS, :], bs_qd[:, b, :], start=True, stop=True).then_inc(sem["qb_ps"], 1)

            spread_at = {6: (0, 1)}
            for b in range(2, NS):
                spread_at[9 + (8 * (b - 2) + 2) // 3] = (b,)
            for k in range(2, 7 * TILES):
                for b in spread_at.get(k, ()):
                    bs_spread(b)
                projection(k // TILES, k % TILES)
            pe.wait_ge(sem["bs_tot"], 1)
            mm(bank[6][:, 0:32], tri_gt, bs_tot.rearrange("p b h -> p (b h)"), start=True, stop=True).then_inc(sem["bs_cross"], 1)
            for t in range(NT):
                pe.wait_ge(sem["qk_norm"], t + 1)
                if t == 0:
                    pe.wait_ge(sem["dense_evac"], 6 + 7 * TILES)
                for j in range(4):
                    if t:
                        pe.wait_ge(sem["t_evac"], 4 * (t - 1) + j + 1)
                    for c in range(4 if j < 3 else 2):
                        last = tr(bank[2 + j][:, c * P:(c + 1) * P], pqk[:, t, (4 * j + c) * P:(4 * j + c + 1) * P], ident)
                    last.then_inc(sem["t_ps"], 1)
            pe.wait_ge(sem["t_evac"], 13)
            for c in range(4):
                last = tr(bank[2][:, c * NS:(c + 1) * NS], pqk[0:NS, NT, 1280 + c * P:1280 + (c + 1) * P], ident[0:NS, 0:NS])
            last.then_inc(sem["t_ps"], 1)

            def head(h):
                return slice(h % 2 * HD, h % 2 * HD + HD)

            NI = AH * NT
            pe.wait_ge(sem["t_act"], 1)

            def a_scores(i):
                h, t = i // NT, i % NT
                if i >= 2:
                    pe.wait_ge(sem["a_nm"], i - 1)
                mm(bank[4 + i % 2][:, 0:(t + 1) * P], tt[head(h), h // 2, cols(t)], tt[head(h), 3 + h // 2, 0:(t + 1) * P],
                   start=True, stop=True).then_inc(sem["a_s"], 1)

            def bs_values(n):
                b, c = n // 4, n % 4
                if n == 0:
                    pe.wait_ge(sem["bs_ex"], 1)
                pe.wait_ge(sem[f"gather{n % 4}"], 16 * (KEYS_GATHERED[n % 4] + n // 4 + 1))
                chunk = view(kvbuf[n % 4], [8, BW])
                for r in range(8):
                    last = mm(bank[BS_BANK[b // 2]][0:BH, b % 2 * BW:b % 2 * BW + BW], bs_w[:, b, 8 * c + r, :], chunk[:, r, :],
                              start=(c == 0 and r == 0), stop=(c == 3 and r == 7))
                last.then_inc(sem["kvv_used"], 1)

            a_scores(0)
            for i in range(NI):
                h, t = i // NT, i % NT
                if i + 1 < NI:
                    a_scores(i + 1)
                bs_values(i)
                pe.wait_ge(sem["a_p"], i + 1)
                if i:
                    pe.wait_ge(sem["a_ptc"], i)
                for j in range(t + 1):
                    last = tr(bank[6][:, j * P:(j + 1) * P], a_pr[i % 2][:, j * P:(j + 1) * P], ident)
                last.then_inc(sem["a_pt"], 1)
                pe.wait_ge(sem["a_ptc"], i + 1)
                if i >= 2:
                    pe.wait_ge(sem["a_o"], i - 1)
                for j in range(t + 1):
                    last = mm(bank[7 - 4 * (i % 2)][:, 0:HD], a_prT[i % 2][:, j, :], pv[:, j, h * HD:(h + 1) * HD], start=(j == 0), stop=(j == t))
                last.then_inc(sem["a_pv"], 1)

            def b_scores(h):
                s = 4 * (h % 2)
                if h == 0:
                    pe.wait_ge(sem["bs_ov"], 3)
                if h == 1:
                    pe.wait_ge(sem["a_o"], NI)
                if h >= 2:
                    pe.wait_ge(sem["b_sum"], h - 1)
                for j in range(NT):
                    b, at = J_BANK[j]
                    last = mm(bank[s + b][:, at:at + JN[j]], tt[head(h), 8 + h // 2, cols(j)], tt[head(h), 6 + h // 2, j * P:SEQ], start=True, stop=True)
                last.then_inc(sem["b_z"], 1)

            b_scores(0)
            for h in range(BH):
                s = 4 * (h % 2)
                if h + 1 < BH:
                    b_scores(h + 1)
                bs_values(NI + 2 * h)
                pe.wait_ge(sem["b_lk"], h + 1)
                for j in range(NT):
                    b, at = J_BANK[j]
                    last = mm(bank[s + b][:, at:at + JN[j]], tri_gt, bz[h % 2][:, JO[j]:JO[j] + JN[j]], start=True, stop=(j == NT - 1))
                    for j2 in range(j + 1, NT):
                        o = at + (j2 - j) * P
                        last = mm(bank[s + b][:, o:o + JN[j2]], ones, bz[h % 2][:, JO[j2]:JO[j2] + JN[j2]], start=False, stop=(j2 == NT - 1))
                last.then_inc(sem["b_after"], 1)
                bs_values(NI + 2 * h + 1)
                pe.wait_ge(sem["b_a"], h + 1)
                if h:
                    pe.wait_ge(sem["b_o"], h)
                for t in range(NT):
                    for j in range(t + 1):
                        o = JO[j] + (t - j) * P
                        last = mm(bank[3][:, t * HD:(t + 1) * HD], bl[h % 2][:, o:o + P], pv[:, j, AW + h * HD:AW + (h + 1) * HD], start=(j == 0), stop=(j == t))
                last.then_inc(sem["b_pv"], 1)

            pe.wait_ge(sem["bs_ov"], NS // 2)
            for b in range(NS):
                for hp in range(2):
                    last = tr(bank[6][:, (2 * b + hp) * BH:(2 * b + hp + 1) * BH], bs_ov[:, b, hp * P:(hp + 1) * P], ident[0:BH, 0:BH])
            last.then_inc(sem["bs_pv"], 1)

            pe.wait_ge(sem["qd_ready"], 1)
            for b in range(NS):
                if b >= 2:
                    pe.wait_ge(sem["kvk_used"], 32 + b - 1)
                mm(bank[b % 2][:, 0:AW], ones[0:NS, :], as_qd[:, b, :], start=True, stop=True).then_inc(sem["qb_ps"], 1)
            pe.wait_ge(sem["as_used"], 1)
            for g in range(3):
                tr(bank[2][0:48, g * P:(g + 1) * P], as_s[:, g, :], ident)
            tr(bank[2][0:48, 384:392], as_self.rearrange("p b h -> p (b h)"), ident[0:NS, 0:NS]).then_inc(sem["sT_ps"], 1)
            pe.wait_ge(sem["s_norm"], 1)
            for g in range(3):
                tr(bank[3][:, g * 48:(g + 1) * 48], as_p[:, g * P:(g + 1) * P], ident[0:48, 0:48])
            tr(bank[3][0:NS, 144:192], as_p[:, 384:392], ident[0:48, 0:48]).then_inc(sem["pT_ps"], 1)
            pe.wait_ge(sem["pT_ready"], 1)
            def as_transposed(b):
                pe.wait_ge(sem["as_ov"], b + 1)
                for c in range(3):
                    ins = tr(bank[0][:, (3 * b + c) * AH:(3 * b + c + 1) * AH], as_ov[b][:, c * P:(c + 1) * P], ident[0:AH, 0:AH])
                return ins

            for b in range(NS):
                n = NS + b
                pe.wait_ge(sem[f"kv{n % 4}"], 48 * (n // 4 + 1))
                o = bank[b][0:AH, 0:AW]
                for g in range(3):
                    mm(o, as_pT[:, g, b * AH:(b + 1) * AH], view(kvbuf[n % 4], [3, AW])[:, g, :], start=(g == 0), stop=False)
                mm(o, as_pT[0:NS, 3, b * AH:(b + 1) * AH], pv[0:NS, NT, 0:AW], start=False, stop=True).then_inc(sem["kvv_used"], 1)
                if b:
                    as_transposed(b - 1)
            as_transposed(NS - 1).then_inc(sem["as_pv"], 1)

            pe.wait_ge(sem["as_o"], 1)
            for L in range(8):
                if L < 7:
                    pe.wait_ge(sem["c_q"], L + 1)
                    pe.wait_ge(sem["c_k"], L + 1)
                if L >= 2:
                    pe.wait_ge(sem["c_cp"], 4 * (L - 1))
                ks, qs = (ck1[L % 2], cq1[L % 2]) if L < 7 else (ck, tt[:, 10:12, :])
                for h in range(CH):
                    for t in range(NT):
                        last = mm(bank[4 * (L % 2) + h][:, cols(t)], ks[head(h), h // 2, cols(t)], qs[head(h), h // 2, cols(t)], start=True, stop=True)
                last.then_inc(sem["c_lev"], 1)
            pe.wait_ge(sem["c_k"], 8)
            pe.wait_ge(sem["c_cp"], 32)
            for j in range(2):
                for c in range(4):
                    last = tr(bank[j][:, c * P:(c + 1) * P], ck1[0][:, j, cols(c)], ident)
                last.then_inc(sem["c_kt"], 1)
            pe.wait_ge(sem["c_ktc"], 2)
            pe.wait_ge(sem["c_q"], 8)
            for t in range(NT):
                if t:
                    pe.wait_ge(sem["c_s"], t)
                if t >= 2:
                    pe.wait_ge(sem["c_raw"], t - 1)
                for h in range(CH):
                    o = bank[2 + 4 * (h % 2) + t % 2][:, h * HD:(h + 1) * HD]
                    v = pv[:, t, 640 + h * HD:704 + h * HD]
                    last = mm(o, c_att[:, h, t, :], v, start=True, stop=(t == 0))
                    if t:
                        last = mm(o, cq1[1][head(h), h // 2, cols(t)], c_S[head(h), h // 2, :], start=False, stop=True)
                last.then_inc(sem["c_pv"], 1)
                for h in range(CH):
                    last = mm(bank[4 + t % 2][head(h), h // 2 * HD:(h // 2 + 1) * HD], c_krow[:, h // 2 * 4 + t, head(h)], pv[:, t, 640 + h * HD:704 + h * HD], start=True, stop=True)
                last.then_inc(sem["c_pv"], 1)
            for hp in range(2):
                pe.wait_ge(sem["c_vd"], hp + 1)
                pe.wait_ge(sem["c_raw"], NT)
                for two in range(2):
                    last = mm(bank[6 + hp][two * HD:two * HD + HD, :], ones[0:NS, 0:HD], c_vdiag[:, two, :, :].rearrange("p b v -> p (b v)"), start=True, stop=True)
                last.then_inc(sem["c_vb"], 1)
            pe.wait_ge(sem["c_new"], 2)
            for h in range(CH):
                for b in range(NS):
                    last = mm(bank[5 - h % 2][0:NS, h * HD:(h + 1) * HD], c_qd[head(h), h // 2, b, :], c_new[head(h), b, h // 2, :], start=(b == 0), stop=(b == NS - 1))
            last.then_inc(sem["c_so"], 1)
            pe.wait_ge(sem["d_gelu"], 1)
            for g in range(DG):
                last = mm(bank[6 + g // 2][:, 256 * (g % 2):256 * (g % 2) + 256], sgu_wt[:, g, :], pv[:, 0:NT, 1408 + g * HD:1472 + g * HD], start=True, stop=True)
            last.then_inc(sem["d_mix"], 1)
            def merge_gate(j):
                k8 = j // 4
                ms = slice(j % 4 * P, j % 4 * P + P)
                if j % 4 == 0:
                    panel_wait(GATE0 + k8)
                if j >= 2:
                    pe.wait_ge(sem["m_acc"], j - 1)
                w = panel[(GATE0 + k8) % 2]
                for part, o in zip(row_half, (bank[j % 2][:, 0:HALF], bank[4 + j % 2][:, 0:HALF])):
                    for c in range(KC):
                        last = mm(o, w[:, c, ms], hT[:, c, part], start=(c == 0), stop=(c == KC - 1))
                last.then_inc(sem["dense_out"], 1)

            pe.wait_ge(sem["c_raw"], TILES)
            pe.wait_ge(sem["c_s"], NT)
            merge_gate(0)
            pe.wait_ge(sem["d_o"], 1)
            pe.wait_ge(sem["b_o"], BH)
            for t in range(NT):
                for j in range(3):
                    if t:
                        pe.wait_ge(sem["oT_evac"], 3 * (t - 1) + j + 1)
                    for c in range(4 if j < 2 else 1):
                        last = tr(bank[OT_BANK[j]][:, c * P:(c + 1) * P], orow[:, t, (4 * j + c) * P:(4 * j + c + 1) * P], ident)
                    last.then_inc(sem["oT_ps"], 1)
            for c in range(4):
                last = tr(bank[7][:, c * NS:(c + 1) * NS], orow[0:NS, NT, (5 + c) * P:(6 + c) * P], ident[0:NS, 0:NS])
            last.then_inc(sem["oT_ps"], 1)

            pe.wait_ge(sem["oT_evac"], 13)
            for j in range(32):
                if j:
                    merge_gate(j)
                k8 = j // 4
                br = k8 % NB
                ms = slice(j % 4 * P, j % 4 * P + P)
                if j % 4 == 0:
                    pe.wait_ge(sem[f"w_br{k8 % 2}"], 16 * (k8 // 2 + 1))
                w = branch_panel[k8 % 2]
                for part, o in zip(row_half, (bank[2 + j % 2][:, 0:HALF], bank[6 + j % 2][:, 0:HALF])):
                    for c in range(BR_K[br]):
                        last = mm(o, w[:, c, ms], oT[:, BR_AT[br] + c, part], start=(c == 0), stop=(c == BR_K[br] - 1))
                last.then_inc(sem["dense_out"], 1)
            pe.wait_ge(sem["m_acc"], 32)
            for c in range(2):
                last = mm(bank[6 + c][:, :], sel9[0:9, :], mod_sb[0:9, 2, c * 512:c * 512 + 512], start=True, stop=True)
            last.then_inc(sem["g_ps"], 1)
            for k in range(2 * TILES):
                g, t = k // TILES, k % TILES
                if t == 0:
                    panel_wait(OUT0 + g)
                if k >= 2:
                    pe.wait_ge(sem["mix_sb"], k - 1)
                for c in range(KC):
                    last = mm(bank[k % 2][0:rows(t), :], mT[:, c, cols(t)], panel[(OUT0 + g) % 2][:, c, :], start=(c == 0), stop=(c == KC - 1))
                last.then_inc(sem["dense_out"], 1)
            modulation(1)

            def router(t):
                pe.wait_ge(sem["hT_evac"], 2 * (TILES + t + 1))
                for c in range(KC):
                    last = mm(bank[0][0:rows(t), t * NE:(t + 1) * NE], hT[:, c, cols(t)], w_router[:, c, :], start=(c == 0), stop=(c == KC - 1))
                if t == TILES - 1:
                    last.then_inc(sem["r_log"], 1)

            transposed_rows(1, router)

            def sh_gu(t):
                if t == 0:
                    panel_wait(SHGU, 2)
                if t >= 2:
                    pe.wait_ge(sem["sh_h"], t - 1)
                for c in range(KC):
                    last = mm(bank[4 + t % 2][0:rows(t), :], hT[:, c, cols(t)], panel[SHGU % 2][:, c, :], start=(c == 0), stop=(c == KC - 1))
                last.then_inc(sem["sh_gu"], 1)

            sh_gu(0)
            sh_gu(1)
            for t in range(TILES):
                n = rows(t)
                if t + 1 < TILES and t >= 1:
                    sh_gu(t + 1)
                pe.wait_ge(sem["sh_h"], t + 1)
                if t:
                    pe.wait_ge(sem["sh_hTc"], t)
                for c in range(2):
                    last = tr(bank[6][:, c * n:(c + 1) * n], hmid[t % 2][0:n, c * P:(c + 1) * P], ident[0:n, 0:n])
                last.then_inc(sem["sh_hT"], 1)
                pe.wait_ge(sem["sh_hTc"], t + 1)
                if t == 0:
                    panel_wait(SHD, 1 if SHD % 2 != SHGU % 2 else 2)
                else:
                    pe.wait_ge(sem["sh_row"], t)
                    pe.wait_ge(sem["sh_rv"], t)
                for m in range(2):
                    for c in range(2):
                        last = mm(bank[2 + m][0:n, :], hmT[t % 2][:, c, 0:n], panel_wide[SHD % 2][:, c, m * 512:(m + 1) * 512], start=(c == 0), stop=(c == 1))
                last.then_inc(sem["sh_y"], 1)
            pe.wait_ge(sem["r_mask"], TILES)
            for t in range(TILES):
                o = bank[1][0:rows(t), t * NE:(t + 1) * NE]
                for t2 in range(t):
                    mm(o, ones[:, 0:rows(t)], r_M[:, t2, :], start=(t2 == 0), stop=False)
                mm(o, tri_lt[0:rows(t), 0:rows(t)], r_M[0:rows(t), t, :], start=(t == 0), stop=True)
            for t in range(TILES):
                last = mm(bank[1][:, 320:384], ones[0:rows(t), :], r_M[0:rows(t), t, :], start=(t == 0), stop=(t == NT))
            last.then_inc(sem["r_pos"], 1)
            pe.wait_ge(sem["r_tab_in"], 1)
            mm(bank[0][0:1, 0:P], r_be, ident, start=True, stop=True).then_inc(sem["r_tab"], 1)
            for t in range(TILES):
                n = rows(t)
                pe.wait_ge(sem["r_tab_in"], t + 2)
                for k in range(TOPK):
                    last = mm(bank[7][:, 0:MAXB], r_hs[0:n, k, :], r_hb[0:n, k, :], start=(t == 0 and k == 0), stop=(t == NT and k == TOPK - 1))
                last.then_inc(sem["r_tab"], 1)

            pe.wait_ge(sem["r_ready"], 2)
            pe.wait_ge(sem["sh_row"], TILES)
            pe.wait_ge(sem["sh_rv"], TILES)
            last = pe.value_load(be_row[0:1, MAXB:MAXB + 1], min_val=THREES_MIN - 2, max_val=MAXB // 3 - 2) + 1

            def rows_transposed(p, q):
                pe.wait_ge(sem[f"gather{q}"], p * 16 + 16 * (ALL_GATHERED[q] + 1))
                if later(p) or q:
                    pe.wait_ge(sem["x_ca"], p * 3 + q)
                    pe.wait_ge(sem["x_cv"], p * 3 + q)
                for c in range(KC):
                    ins = tr(bank[c // 4][:, (c % 4) * P:(c % 4 + 1) * P], xg[q].rearrange("p (n c) -> p c n", c=KC)[:, c, :], ident)
                ins.then_inc(sem["x_t"], 1)

            def gate_up(p, q):
                i = p * 3 + q
                pe.wait_ge(sem[f"wg{q}"], p * 32 + 32)
                pe.wait_ge(sem["x_ca"], i + 1)
                pe.wait_ge(sem["x_cv"], i + 1)
                if later(p):
                    pe.wait_ge(sem["m_h"], i - 2)
                for c in range(KC):
                    ins = mm(bank[gu_bank[q]][:, :].rearrange("p (g n) -> p g n", g=2), xT[q][:, c, :], wgu[q][:, :, c, :], start=(c == 0), stop=(c == KC - 1))
                ins.then_inc(sem["gu_done"], 1)

            def middle_transposed(p, q):
                i = p * 3 + q
                pe.wait_ge(sem["m_h"], i + 1)
                if later(p) or q:
                    pe.wait_ge(sem["m_hTc"], i)
                for c in range(2):
                    ins = tr(bank[4][:, c * P:(c + 1) * P], hmid[q].rearrange("p (n c) -> p c n", c=2)[:, c, :], ident)
                ins.then_inc(sem["m_hT"], 1)

            def down(p, q):
                i = p * 3 + q
                pe.wait_ge(sem["m_hTc"], i + 1)
                pe.wait_ge(sem[f"wd{q}"], p * 16 + 16)
                if later(p) or q:
                    pe.wait_ge(sem["y_a"], i)
                    pe.wait_ge(sem["y_v"], i)
                for m in range(2):
                    for c in range(2):
                        ins = mm(bank[5 + m][:, :], hmT[q][:, c, :], wdn[q][:, c, m * 512:(m + 1) * 512], start=(c == 0), stop=(c == 1))
                ins.then_inc(sem["dn_done"], 1)

            def block(p, q, front=True, back=True):
                gate_up(p, q)
                if front:
                    rows_transposed(*block_at(p, q, 1))
                if back:
                    down(*block_at(p, q, -1))
                middle_transposed(p, q)

            rows_transposed(0, 0)
            block(0, 0, back=False)
            for i in range(1, 6):
                block(i // 3, i % 3)
            with pe.Fori(2, last) as p:
                for q in range(3):
                    block(p, q)
            for q in range(3):
                block(last, q, front=q < 2)
            down(last, 2)
            pe.wait_ge(sem["gu_done"], last * 3 + 3)
            for c in range(2):
                last = mm(bank[c][:, :], sel9[0:9, :], mod_sb[0:9, 2, c * 512:c * 512 + 512], start=True, stop=True)
            last.then_inc(sem["g_ps"], 1)
            for u, t in enumerate(F_ORDER):
                m = rows(t)
                pe.wait_ge(sem["f_diag"], u + 1)
                if u >= 2:
                    pe.wait_ge(sem["f_acc"], u - 1)
                for k in range(TOPK // 2, TOPK):
                    if k % 2 == 0:
                        name, before = f_sem[u % 2][k // 2]
                        pe.wait_ge(sem[name], before + 16 * (u // 2 + 1))
                    for c in range(2):
                        ins = mm(bank[F_BANK[u % 2][c]][0:m, :], f_dg[0:m, t, k - TOPK // 2, 0:m], fbuf[u % 2][k // 2][0:m, k % 2, c * 512:c * 512 + 512],
                                 start=(k == TOPK // 2), stop=(k == TOPK - 1))
                    if k % 2:
                        ins.then_inc(sem["f_pe"], 1)


_INS = """x_prompt x_sample c_prompt c_sample cache_swa_k cache_swa_v cache_sb_k cache_sb_v state_hgrn page_table
norm1_g norm2_g w_ada b_ada w_in a_q_norm_g a_k_norm_g sb_bias c_out_norm_g sgu_w sgu_b w_branch_a w_branch_b
w_branch_c w_branch_d w_merge_gate b_merge_gate w_out w_router b_router w_exp_gate w_exp_up w_exp_down w_sh_gate
w_sh_up w_sh_down""".split()
_OUTS = [("y_p", (SEQ, D), (1, SEQ, D)), ("y_s", (NS, D), (NS, 1, D)),
         ("swa_k_p", (SEQ, AW), (1, 1, SEQ, AH, HD)), ("swa_v_p", (SEQ, AW), (1, 1, SEQ, AH, HD)),
         ("sb_k_p", (SEQ, BW), (1, 1, SEQ, BH, HD)), ("sb_v_p", (SEQ, BW), (1, 1, SEQ, BH, HD)),
         ("hgrn_p", (CH, HD, HD), (1, 1, CH, HD, HD)),
         ("swa_k_s", (NS, AW), (1, NS, 1, AH, HD)), ("swa_v_s", (NS, AW), (1, NS, 1, AH, HD)),
         ("sb_k_s", (NS, BW), (1, NS, 1, BH, HD)), ("sb_v_s", (NS, BW), (1, NS, 1, BH, HD)),
         ("hgrn_s", (NS, CH, HD, HD), (1, NS, CH, HD, HD)), ("sgu_v_s", (NS, DG * HD), (1, NS, 1, DG, HD))]


def kernel(**inputs):
    import numpy as _np
    import concourse.bacc as _bacc
    from concourse import mybir as _mybir
    from concourse.bass_utils import run_bass_kernel_spmd as _run

    nc = _bacc.Bacc("TRN2", target_bir_lowering=False, num_devices=1)
    arrays, ins, outs = {}, {}, {}
    for name in _INS:
        a = _np.ascontiguousarray(inputs[name])
        arrays[f"in_{name}_dram"] = a
        ins[name] = nc.dram_tensor(f"in_{name}_dram", a.shape, _mybir.dt.from_np(a.dtype), kind="ExternalInput").ap()
    for i, (name, shape, _) in enumerate(_OUTS):
        outs[name] = nc.dram_tensor(f"out_{i}_dram", shape, F32, kind="ExternalOutput").ap()
    trunk(nc, ins, outs)
    r = _run(nc, [arrays], core_ids=[0])
    return tuple(r.results[0][f"out_{i}_dram"].reshape(shape) for i, (_, _, shape) in enumerate(_OUTS))
```
